# Optimizing a Trainium2 kernel written in Bass

```python
import math
import jax, jax.numpy as jnp
from jax import lax
import numpy as np

D_MODEL = 1024
BATCH = 1
SEQ = 1024
DEPTH = 1
DEC_BATCH = 8
DEC_SEQ = 16
PAST_LEN = 256

CHUNK = 64
QBLOCK = 128
HEAD_DIM = 64
DIFF_HEADS = 8
DIFF_COMP = HEAD_DIM // 2
SB_HEADS = 8
DIFF_WIDTH = DIFF_HEADS * HEAD_DIM
SB_WIDTH = SB_HEADS * HEAD_DIM
MIX_WIDTH = DIFF_WIDTH + SB_WIDTH
IN_COLS = 3 * MIX_WIDTH
ROPE_THETA = 10000.0
NORM_EPS = 1e-6
SUBLN_EPS = 1e-5
PEER_HEADS = 8
PEER_KEYS = 128
N_EXPERTS = PEER_KEYS * PEER_KEYS
PEER_TOPK = 16
PEER_QDIM = 256
PEER_HALF = PEER_QDIM // 2
PEER_BLOCK = 128
PLE_DIM = 256

kernel_name = 'stream_diff_stickbreak_peer'

def _rmsnorm(x, g, eps=NORM_EPS):
    x32 = x.astype(jnp.float32)
    y = x32 * lax.rsqrt(jnp.mean(x32 * x32, axis=-1, keepdims=True) + eps)
    return (y * g.astype(jnp.float32)).astype(x.dtype)

def _rope(x, pos):
    d = x.shape[-1]
    inv = ROPE_THETA ** (-jnp.arange(0, d, 2, dtype=jnp.float32) / d)
    ang = pos.astype(jnp.float32)[:, None] * inv[None, :]
    cos = jnp.cos(ang)[None, :, None, :]
    sin = jnp.sin(ang)[None, :, None, :]
    x32 = x.astype(jnp.float32)
    x1, x2 = jnp.split(x32, 2, axis=-1)
    return jnp.concatenate([x1 * cos - x2 * sin, x1 * sin + x2 * cos], axis=-1).astype(x.dtype)

def _rope_diff(x, pos):
    b, s, h, _ = x.shape
    return _rope(x.reshape(b, s, h * 2, DIFF_COMP), pos).reshape(b, s, h, 2 * DIFF_COMP)

def _diff_attend(q, q_pos, k, v, k_pos, lam):
    b, nq, h, _ = q.shape
    nk = k.shape[1]
    qc = q.reshape(b, nq, h, 2, DIFF_COMP)
    kc = k.reshape(b, nk, h, 2, DIFF_COMP)
    s = jnp.einsum('bqhcd,bkhcd->bhcqk', qc, kc).astype(jnp.float32) * (DIFF_COMP ** -0.5)
    visible = (k_pos[None, :] // CHUNK) <= (q_pos[:, None] // CHUNK)
    s = jnp.where(visible, s, -jnp.inf)
    prob = jax.nn.softmax(s, axis=-1)
    w = prob[:, :, 0] - lam * prob[:, :, 1]
    return jnp.einsum('bhqk,bkhd->bqhd', w, v.astype(jnp.float32))

def _sb_attend(q, q_pos, k, v, k_pos):
    z = jnp.einsum('bqhd,bkhd->bhqk', q, k).astype(jnp.float32) * (HEAD_DIM ** -0.5)
    earlier = k_pos[None, :] < q_pos[:, None]
    log_keep = jnp.where(earlier, jax.nn.log_sigmoid(-z), 0.0)
    log_keep_after = lax.cumsum(log_keep, axis=3, reverse=True) - log_keep
    wts = jnp.where(earlier, jnp.exp(jax.nn.log_sigmoid(z) + log_keep_after), 0.0)
    return jnp.einsum('bhqk,bkhd->bqhd', wts, v.astype(jnp.float32))

def _sweep(fn, q, q_pos):
    b, nq = q.shape[:2]
    if nq <= QBLOCK:
        return fn(q, q_pos)
    nb = nq // QBLOCK
    qb = q.reshape((b, nb, QBLOCK) + q.shape[2:]).swapaxes(0, 1)
    pb = q_pos.reshape(nb, QBLOCK)
    ob = lax.map(lambda args: fn(args[0], args[1]), (qb, pb))
    return ob.swapaxes(0, 1).reshape((b, nq) + ob.shape[3:])

def _peer(c, w_query, sub_keys, expert_u, expert_v):
    t = c.shape[0]
    q = (c @ w_query).reshape(t, PEER_HEADS, 2, PEER_HALF)
    s = jnp.einsum('thpd,pnd->thpn', q, sub_keys).astype(jnp.float32)
    s1, i1 = lax.top_k(s[:, :, 0], PEER_TOPK)
    s2, i2 = lax.top_k(s[:, :, 1], PEER_TOPK)
    cand = (s1[..., :, None] + s2[..., None, :]).reshape(t, PEER_HEADS, PEER_TOPK * PEER_TOPK)
    cidx = (i1[..., :, None] * PEER_KEYS + i2[..., None, :]).reshape(t, PEER_HEADS, PEER_TOPK * PEER_TOPK)
    top, sel = lax.top_k(cand, PEER_TOPK)
    idx = jnp.take_along_axis(cidx, sel, axis=-1)
    g = jax.nn.softmax(top, axis=-1)
    u = expert_u[idx]
    act = jax.nn.gelu(jnp.einsum('td,thkd->thk', c, u).astype(jnp.float32), approximate=False)
    coef = (g * act).astype(c.dtype)
    return jnp.einsum('thk,thkd->td', coef, expert_v[idx])

def _channel(c, w_query, sub_keys, expert_u, expert_v):
    b, s, d = c.shape
    t = b * s
    flat = c.reshape(t, d)
    if t > PEER_BLOCK and t % PEER_BLOCK == 0:
        blocks = flat.reshape(t // PEER_BLOCK, PEER_BLOCK, d)
        out = lax.map(lambda blk: _peer(blk, w_query, sub_keys, expert_u, expert_v), blocks).reshape(t, d)
    else:
        out = _peer(flat, w_query, sub_keys, expert_u, expert_v)
    return out.reshape(b, s, d)

def _mixers(a, pos, w_in, w_out, g_subln, lam, lam_init, cache):
    b, s, _ = a.shape
    proj = (a @ w_in).reshape(b, s, 6, DIFF_HEADS, HEAD_DIM)
    qd = _rope_diff(proj[:, :, 0], pos)
    kd = _rope_diff(proj[:, :, 1], pos)
    vd = proj[:, :, 2]
    qs = proj[:, :, 3]
    ks = proj[:, :, 4]
    vs = proj[:, :, 5]
    if cache is None:
        kd_all, vd_all, ks_all, vs_all = kd, vd, ks, vs
        k_pos = pos
    else:
        ck_d, cv_d, ck_s, cv_s = cache
        past = ck_d.shape[1]
        kd_all = jnp.concatenate([ck_d.astype(kd.dtype), kd], axis=1)
        vd_all = jnp.concatenate([cv_d.astype(vd.dtype), vd], axis=1)
        ks_all = jnp.concatenate([ck_s.astype(ks.dtype), ks], axis=1)
        vs_all = jnp.concatenate([cv_s.astype(vs.dtype), vs], axis=1)
        k_pos = jnp.concatenate([jnp.arange(past, dtype=jnp.int32), pos])
    diff = _sweep(lambda qb, pb: _diff_attend(qb, pb, kd_all, vd_all, k_pos, lam), qd, pos)
    diff = _rmsnorm(diff, g_subln, SUBLN_EPS) * (1.0 - lam_init)
    sb = _sweep(lambda qb, pb: _sb_attend(qb, pb, ks_all, vs_all, k_pos), qs, pos)
    heads = jnp.concatenate([diff.reshape(b, s, DIFF_WIDTH), sb.reshape(b, s, SB_WIDTH)], axis=-1).astype(a.dtype)
    return heads @ w_out, (kd, vd, ks, vs)

def setup_inputs(seed: int = 0) -> dict:
    key = jax.random.key(seed)
    ks = jax.random.split(key, 26)
    f32 = jnp.float32

    def nrm(k, shape, scale=1.0):
        return jax.random.normal(k, shape, f32) * scale

    def gain(k, shape):
        return 1.0 + 0.05 * jax.random.normal(k, shape, f32)

    kv_d = (DEPTH, DEC_BATCH, PAST_LEN, DIFF_HEADS, HEAD_DIM)
    kv_s = (DEPTH, DEC_BATCH, PAST_LEN, SB_HEADS, HEAD_DIM)
    return {
        'x_prompt': nrm(ks[0], (BATCH, SEQ, D_MODEL)),
        'x_sample': nrm(ks[1], (DEC_BATCH, DEC_SEQ, D_MODEL)),
        'cache_diff_k': nrm(ks[2], kv_d),
        'cache_diff_v': nrm(ks[3], kv_d),
        'cache_sb_k': nrm(ks[4], kv_s),
        'cache_sb_v': nrm(ks[5], kv_s),
        'p_prompt': nrm(ks[6], (DEPTH, BATCH, SEQ, PLE_DIM)),
        'p_sample': nrm(ks[7], (DEPTH, DEC_BATCH, DEC_SEQ, PLE_DIM)),
        'g_mix': gain(ks[8], (DEPTH, D_MODEL)),
        'w_in': nrm(ks[9], (DEPTH, D_MODEL, IN_COLS), D_MODEL ** -0.5),
        'lambda_q1': nrm(ks[10], (DEPTH, DIFF_COMP), 0.1),
        'lambda_k1': nrm(ks[11], (DEPTH, DIFF_COMP), 0.1),
        'lambda_q2': nrm(ks[12], (DEPTH, DIFF_COMP), 0.1),
        'lambda_k2': nrm(ks[13], (DEPTH, DIFF_COMP), 0.1),
        'g_subln': gain(ks[14], (DEPTH, HEAD_DIM)),
        'w_out': nrm(ks[15], (DEPTH, MIX_WIDTH, D_MODEL), MIX_WIDTH ** -0.5),
        'g_ffn': gain(ks[16], (DEPTH, D_MODEL)),
        'w_query': nrm(ks[17], (DEPTH, D_MODEL, PEER_HEADS * PEER_QDIM), D_MODEL ** -0.5),
        'sub_keys': nrm(ks[18], (DEPTH, 2, PEER_KEYS, PEER_HALF), PEER_HALF ** -0.5),
        'expert_u': nrm(ks[19], (DEPTH, N_EXPERTS, D_MODEL), D_MODEL ** -0.5),
        'expert_v': nrm(ks[20], (DEPTH, N_EXPERTS, D_MODEL), PEER_HEADS ** -0.5),
        'g_ple': gain(ks[21], (DEPTH, D_MODEL)),
        'w_pgate': nrm(ks[22], (DEPTH, D_MODEL, D_MODEL), D_MODEL ** -0.5),
        'w_ple': nrm(ks[23], (DEPTH, PLE_DIM, D_MODEL), PLE_DIM ** -0.5),
        'g_final': gain(ks[24], (D_MODEL,)),
    }

def reference(x_prompt, x_sample, cache_diff_k, cache_diff_v, cache_sb_k, cache_sb_v, p_prompt, p_sample,
              g_mix, w_in, lambda_q1, lambda_k1, lambda_q2, lambda_k2, g_subln, w_out, g_ffn, w_query,
              sub_keys, expert_u, expert_v, g_ple, w_pgate, w_ple, g_final):
    def run(x, p, pos, caches):
        h = x
        rows = []
        for i in range(DEPTH):
            lam_init = 0.8 - 0.6 * math.exp(-0.3 * i)
            lam = (jnp.exp(jnp.sum(lambda_q1[i].astype(jnp.float32) * lambda_k1[i].astype(jnp.float32)))
                   - jnp.exp(jnp.sum(lambda_q2[i].astype(jnp.float32) * lambda_k2[i].astype(jnp.float32)))
                   + lam_init)
            cache_i = None if caches is None else tuple(c[i] for c in caches)
            a = _rmsnorm(h, g_mix[i])
            mixed, new_rows = _mixers(a, pos, w_in[i], w_out[i], g_subln[i], lam, lam_init, cache_i)
            h = h + mixed
            h = h + _channel(_rmsnorm(h, g_ffn[i]), w_query[i], sub_keys[i], expert_u[i], expert_v[i])
            gate = jax.nn.sigmoid((_rmsnorm(h, g_ple[i]) @ w_pgate[i]).astype(jnp.float32)).astype(h.dtype)
            h = h + (p[i] @ w_ple[i]) * gate
            rows.append(new_rows)
        y = _rmsnorm(h, g_final)
        stacked = tuple(jnp.stack([r[j] for r in rows]) for j in range(4))
        return y, stacked

    pos_prompt = jnp.arange(x_prompt.shape[1], dtype=jnp.int32)
    past = cache_diff_k.shape[2]
    pos_sample = past + jnp.arange(x_sample.shape[1], dtype=jnp.int32)
    y_prompt, (dk_p, dv_p, sk_p, sv_p) = run(x_prompt, p_prompt, pos_prompt, None)
    y_sample, (dk_s, dv_s, sk_s, sv_s) = run(x_sample, p_sample, pos_sample,
                                             (cache_diff_k, cache_diff_v, cache_sb_k, cache_sb_v))
    return (y_prompt, y_sample, dk_p, dv_p, sk_p, sv_p, dk_s, dv_s, sk_s, sv_s)


_drawn_inputs = setup_inputs


def setup_inputs(seed=0):
    import zlib

    import numpy as np

    out = dict(_drawn_inputs(seed))
    spreads = {}
    factors = {'lambda_q2': 200.0, 'g_ple': 7.068}
    for name, (base, spread) in spreads.items():
        noise = np.random.default_rng([zlib.crc32(name.encode()), seed]).standard_normal(out[name].shape)
        drawn = base * np.exp(spread * noise) if base else spread * noise
        out[name] = __import__('jax').numpy.asarray(drawn.astype(out[name].dtype))
    for name, factor in factors.items():
        out[name] = (out[name] * factor).astype(out[name].dtype)
    return out
```

```python
from contextlib import ExitStack

import concourse.bass as bass
from concourse import mybir

F32 = mybir.dt.float32
U32 = mybir.dt.uint32
ALU = mybir.AluOpType
ACT = mybir.ActivationFunctionType
AX = mybir.AxisListType

P = 128
D = 1024
KC = D // P
W = 512
TP = 8
T = TP + 1
EPS = 1e-6
QD, KD, VD, QS, KS, VS = range(6)
TURNED = {QD: 0, KD: 1, QS: 2, KS: 3}


def stage_semaphores(nc, ctx):
    taken = []

    def clear():
        nc.clear_and_free_semaphores(taken)
        nc.all_engine_barrier()

    def sem(name):
        taken.append(nc.alloc_semaphore(name))
        return taken[-1]

    ctx.callback(clear)
    return sem


def prime(eng, *sems, by=1):
    for s in sems:
        eng.sem_inc(s, by)


def wait_apart(eng, const, sem, value):
    eng.wait_ge(sem, value)
    eng.sem_inc(const.passed[eng.engine], 1)


def project_inputs(nc, const, x_all, g_mix, w_in, rope, new_rows, qk_turned):
    with ExitStack() as ctx:
        def sb(name, shape, dt=F32):
            return ctx.enter_context(nc.sbuf_tensor(name, shape, dt))

        sem = stage_semaphores(nc, ctx)

        weights = sb("weights", [P, KC, 6 * W])
        x = sb("x", [P, D])
        squares = sb("squares", [P, D])
        a = sb("a", [P, D])
        aT = sb("aT", [P, KC, P])
        gain = sb("gain", [P, D])
        rope_tab = sb("rope_tab", [P, T, 64])
        rows = sb("rows", [P, 6, W])
        turned = sb("turned", [P, 4, W])
        rot = sb("rot", [P, 2, W])
        stat = sb("stat", [P, 4])
        turn_ps = ctx.enter_context(nc.psum_tensor("turn_ps", [P, D], F32))
        proj_ps = ctx.enter_context(nc.psum_tensor("proj_ps", [P, 3, W], F32))
        kind_ps = ctx.enter_context(nc.psum_tensor("kind_ps", [P, 2, W], F32))

        consts_in = sem("consts_in")
        w_in_sem = [sem(f"w_landed{g}") for g in range(6)]
        x_in = sem("x_in")
        sum_done = sem("sum_done")
        mean_done = sem("mean_done")
        rstd_done = sem("rstd_done")
        a_done = sem("a_done")
        turn_done = sem("turn_done")
        aT_done = sem("aT_done")
        proj_done = sem("proj_done")
        rot_done = sem("rot_done")
        rows_done = [sem(f"rows_done{k}") for k in range(6)]
        rows_turned = [sem(f"rows_turned{k}") for k in range(4)]
        turned_done = [sem(f"turned_done{k}") for k in range(4)]
        rows_out = [sem(f"rows_out{k}") for k in range(6)]
        turned_out = [sem(f"turned_out{k}") for k in range(4)]
        tile_stored = sem("tile_stored")
        block = ctx.enter_context(nc.Block())

        @block.sync
        def _(sp):
            sp.dma_start(gain[:, :], bass.AP(g_mix.tensor, 0, [[0, P], [1, D]])).then_inc(consts_in, 16)
            sp.dma_start(rope_tab[:, :, :], rope.rearrange("(t p) c -> p t c", p=P)).then_inc(consts_in, 16)
            for g in range(6):
                sp.dma_start(weights[:, :, g * W:(g + 1) * W],
                             w_in[:, g * W:(g + 1) * W].rearrange("(k p) n -> p k n", p=P)).then_inc(w_in_sem[g], 16)
            prime(sp, tile_stored)
            with sp.Fori(0, T) as t:
                for k in (KD, VD, KS, VS):
                    sp.wait_ge(rows_done[k], t + 2)
                    sp.dma_start(new_rows[k][bass.ds(t * P, P), :], rows[:, k, :]).then_inc(rows_out[k], 16)
                for k in (QD, KD, QS, KS):
                    n = TURNED[k]
                    sp.wait_ge(turned_done[n], t + 2)
                    sp.dma_start(qk_turned[n, bass.ds(t, 1), :, :].rearrange("a p n -> p (a n)"),
                                 turned[:, n, :]).then_inc(turned_out[n], 16)
                for k in (KD, VD, KS, VS):
                    sp.wait_ge(rows_out[k], t * 16 + 16)
                for n in range(4):
                    sp.wait_ge(turned_out[n], t * 16 + 16)
                sp.sem_inc(tile_stored, 1)

        @block.gpsimd
        def _(pool):
            with pool.Fori(0, T) as t:
                pool.wait_ge(a_done, t + 1)
                pool.dma_start(x[:, :], x_all[bass.ds(t * P, P), :]).then_inc(x_in, 16)
                pool.wait_ge(mean_done, t + 1)
                nc.gpsimd.tensor_tensor(stat[:, 2:3], stat[:, 1:2], const.minus_half, ALU.pow).then_inc(rstd_done, 1)

        @block.tensor
        def _(pe):
            prime(pe, turn_done, *rows_turned)
            with pe.Fori(0, T) as t:
                pe.wait_ge(a_done, t + 2)
                for k in range(KC):
                    last = nc.tensor.transpose(turn_ps[:, k * P:(k + 1) * P], a[:, k * P:(k + 1) * P], const.ident)
                last.then_inc(turn_done, 1)
                pe.wait_ge(aT_done, t + 1)

                def project(g):
                    pe.wait_ge(w_in_sem[g], 16)
                    pe.wait_ge(rows_done[(g + 3) % 6], t + 1 + g // 3)
                    for k in range(KC):
                        mm = nc.tensor.matmul(proj_ps[:, g % 3, :], aT[:, k, :], weights[:, k, g * W:(g + 1) * W],
                                              start=(k == 0), stop=(k == KC - 1))
                    mm.then_inc(proj_done, 1)

                def turn(kind):
                    n = TURNED[kind]
                    pe.wait_ge(rows_done[kind], t + 2)
                    pe.wait_ge(turned_done[(n + 2) % 4], t + 1 + n // 2)
                    for c in range(4):
                        mm = nc.tensor.transpose(kind_ps[:, n % 2, c * P:(c + 1) * P],
                                                 rows[:, kind, c * P:(c + 1) * P], const.ident)
                    mm.then_inc(rows_turned[n], 1)

                project(QD)
                project(KD)
                project(VD)
                turn(QD)
                project(QS)
                turn(KD)
                project(KS)
                project(VS)
                turn(QS)
                turn(KS)

        @block.scalar
        def _(act):
            prime(act, *(rows_done[g] for g in (VD, QS, KS, VS)), turned_done[2], turned_done[3])
            with act.Fori(0, T) as t:
                act.wait_ge(turn_done, t + 2)
                nc.scalar.copy(aT[:, :, :].rearrange("p k n -> p (k n)"), turn_ps[:, :]).then_inc(aT_done, 1)
                for g in (VD, QS, KS, VS):
                    act.wait_ge(proj_done, t * 6 + (g + 1))
                    if g != QS:
                        act.wait_ge(tile_stored, t + 1)
                    if g in TURNED:
                        act.wait_ge(rows_turned[TURNED[g]], t + 1)
                    nc.scalar.mul(rows[:, g, :], proj_ps[:, g % 3, :],
                                  0.125 if g == QS else 1.0).then_inc(rows_done[g], 1)
                for n in (2, 3):
                    act.wait_ge(rows_turned[n], t + 2)
                    act.wait_ge(tile_stored, t + 1)
                    nc.scalar.copy(turned[:, n, :], kind_ps[:, n % 2, :]).then_inc(turned_done[n], 1)

        @block.vector
        def _(dve):
            prime(dve, a_done, rows_done[QD], rows_done[KD], turned_done[0], turned_done[1])
            with dve.Fori(0, T) as t:
                dve.wait_ge(x_in, t * 16 + 16)
                nc.vector.tensor_tensor_reduce(squares[:, :], x[:, :], x[:, :], 1.0, 0.0, ALU.mult, ALU.add,
                                               stat[:, 0:1]).then_inc(sum_done, 1)
                dve.wait_ge(sum_done, t + 1)
                nc.vector.tensor_scalar(stat[:, 1:2], stat[:, 0:1], 1.0 / D, EPS, ALU.mult, ALU.add).then_inc(mean_done, 1)
                dve.wait_ge(rstd_done, t + 1)
                dve.wait_ge(consts_in, 32)
                dve.wait_ge(turn_done, t + 1)
                nc.vector.scalar_tensor_tensor(a[:, :], x[:, :], stat[:, 2:3], gain[:, :],
                                               ALU.mult, ALU.mult).then_inc(a_done, 1)
                for g in (QD, KD):
                    dve.wait_ge(proj_done, t * 6 + (g + 1))
                    src = proj_ps[:, g % 3, :].rearrange("p (h c d) -> p h c d", c=2, d=16)
                    out = rot[:, 1, :].rearrange("p (h c d) -> p h c d", c=2, d=16)
                    both = rot[:, 0, :].rearrange("p (h d) -> p h d", d=32)
                    cos = rope_tab[:, bass.ds(t, 1), 0:32].broadcast_to((P, 16, 32))
                    nc.vector.tensor_tensor(both, proj_ps[:, g % 3, :].rearrange("p (h d) -> p h d", d=32), cos,
                                            ALU.mult)
                    for c in range(2):
                        sin = rope_tab[:, bass.ds(t, 1), 32 + 16 * c:48 + 16 * c].broadcast_to((P, 16, 16))
                        mm = nc.vector.tensor_tensor(out[:, :, c, :], src[:, :, 1 - c, :], sin, ALU.mult)
                    mm.then_inc(rot_done, 1)
                    dve.wait_ge(rot_done, t * 2 + (g + 1))
                    if g == KD:
                        dve.wait_ge(tile_stored, t + 1)
                    dve.wait_ge(rows_turned[g], t + 1)
                    nc.vector.tensor_tensor(rows[:, g, :], rot[:, 0, :], rot[:, 1, :], ALU.add).then_inc(rows_done[g], 1)
                    dve.wait_ge(rows_done[g], t + 2)
                for n in (0, 1):
                    dve.wait_ge(rows_turned[n], t + 2)
                    dve.wait_ge(tile_stored, t + 1)
                    nc.vector.tensor_scalar(turned[:, n, :], kind_ps[:, n % 2, :], 32 ** -0.5 if n == 0 else 1.0,
                                            None, ALU.mult).then_inc(turned_done[n], 1)


def attend_prompt(nc, const, qk_turned, new_rows, heads):
    with ExitStack() as ctx:
        def sb(name, shape, dt=F32):
            return ctx.enter_context(nc.sbuf_tensor(name, shape, dt))

        sem = stage_semaphores(nc, ctx)

        kd = sb("kd", [P, 2, TP, P])
        ks = sb("ks", [P, 2, TP, P])
        vd = sb("vd", [P, 2, TP, P])
        vs = sb("vs", [P, 2, TP, P])
        qd = sb("qd", [P, 2, 4, P])
        qs = sb("qs", [P, 2, 2, P])
        prob = sb("prob", [P, 4, TP * P])
        soft = sb("soft", [P, 2, TP * P])
        stick = sb("stick", [P, 2, TP * P])
        zeros = sb("zeros", [P, TP * P])
        wT = sb("wT", [P, 2, TP * P])
        neg_max = sb("neg_max", [P, 4])
        total = sb("total", [P, 4])
        share = sb("share", [P, 4])
        head_rows = sb("head_rows", [P, 2, D])
        score_ps = ctx.enter_context(nc.psum_tensor("score_ps", [P, 2, TP * P], F32))
        turn_ps = ctx.enter_context(nc.psum_tensor("wturn_ps", [P, TP * P], F32))
        out_ps = ctx.enter_context(nc.psum_tensor("out_ps", [P, 2, W], F32))

        in_place = [sem(f"pair_landed{b}") for b in range(2)]
        cleared = sem("cleared")
        zeros_done = sem("zeros_done")
        scores_done = sem("scores_done")
        max_done = sem("max_done")
        prob_done = sem("prob_done")
        share_done = sem("share_done")
        part_done = sem("part_done")
        weights_done = sem("weights_done")
        abs_done = sem("abs_done")
        exp_done = sem("exp_done")
        log_done = sem("log_done")
        soft_done = sem("soft_done")
        scan_done = sem("scan_done")
        expo_done = sem("expo_done")
        stick_done = sem("stick_done")
        turned = sem("w_turned")
        wT_done = sem("wT_done")
        out_done = sem("out_done")
        rows_taken = sem("rows_taken")
        stored = [sem(f"heads_stored{b}") for b in range(2)]
        block = ctx.enter_context(nc.Block())

        def steps(eng, i, body):
            with eng.Fori(0, 2) as r:
                for b in range(2):
                    body(r, b, 4 * i + 2 * r + b)

        @block.sync
        def _(sp):
            sp.wait_ge(cleared, 2)
            for i in range(TP):
                def load(r, b, n):
                    done = in_place[b]
                    c = 2 * r + b
                    sp.wait_ge(out_done, 4 * n + 4)
                    for kt, kind in ((kd, 1), (ks, 3)):
                        sp.dma_start(kt[:, b, 0:i + 1, :], qk_turned[kind, 0:i + 1, :, bass.ds(c * P, P)]
                                     .rearrange("j p k -> p j k")).then_inc(done, 16)
                    for v, kind in ((vd, VD), (vs, VS)):
                        sp.dma_start(v[:, b, 0:i + 1, :], new_rows[kind][0:(i + 1) * P, bass.ds(c * P, P)]
                                     .rearrange("(j p) d -> p j d", p=P)).then_inc(done, 16)
                    for q, kind, parts in ((qd, 0, 4), (qs, 2, 2)):
                        w = P // parts
                        for m in range(parts):
                            sp.dma_start(q[m * w:(m + 1) * w, b, m, :],
                                         qk_turned[kind, i, m * w:(m + 1) * w, bass.ds(c * P, P)]).then_inc(done, 16)
                steps(sp, i, load)

        @block.gpsimd
        def _(pool):
            nc.gpsimd.memset(qd[:, :, :, :], 0.0).then_inc(cleared, 1)
            nc.gpsimd.memset(qs[:, :, :, :], 0.0).then_inc(cleared, 1)
            for i in range(TP):
                pool.wait_ge(rows_taken, 8 * (i + 1) + 2)
                pool.dma_start(heads[i], head_rows[:, i % 2, :]).then_inc(stored[i % 2], 16)
            for b in range(2):
                pool.wait_ge(stored[b], 16 * (TP // 2))

        @block.tensor
        def _(pe):
            prime(pe, turned, by=4)
            prime(pe, out_done, by=8)
            for i in range(TP):
                width = (i + 1) * P

                def scores(j, b, n):
                    if j < 2:
                        pe.wait_ge(expo_done, 2 * n + j + 1)
                    else:
                        pe.wait_ge(prob_done, 4 * n + j - 1)
                    q, kt, mask = (qd[:, b, j, :], kd, const.chunk_mask) if j < 4 else (
                        qs[:, b, j - 4, :], ks, const.strict_mask)
                    for c in range(0, width, W):
                        w = min(W, width - c)
                        keys = kt[:, b, :, :].rearrange("p j k -> p (j k)")[:, c:c + w]
                        nc.tensor.matmul(score_ps[:, j % 2, c:c + w], q, keys, start=True, stop=c + w < width)
                    nc.tensor.matmul(score_ps[:, j % 2, i * P:width], const.ident, mask,
                                     start=False, stop=True).then_inc(scores_done, 1)

                def turn(h, n):
                    if h < 2:
                        pe.wait_ge(weights_done, 2 * n + h + 1)
                    else:
                        pe.wait_ge(stick_done, 2 * n + h - 1)
                    pe.wait_ge(wT_done, 4 * n + h + 1)
                    for k in range(i + 1):
                        src = prob[:, 2 * h, :] if h < 2 else stick[:, h - 2, :]
                        mm = nc.tensor.transpose(turn_ps[:, k * P:(k + 1) * P], src[:, k * P:(k + 1) * P], const.ident)
                    mm.then_inc(turned, 1)

                def mix(h, b, n):
                    if h % 2 == 0:
                        pe.wait_ge(rows_taken, 2 * n + h // 2 + 1)
                    pe.wait_ge(wT_done, 4 * n + h + 2)
                    v = vd if h < 2 else vs
                    for k in range(i + 1):
                        mm = nc.tensor.matmul(out_ps[:, h // 2, 64 * (h % 2):64 * (h % 2) + 64],
                                              wT[:, h % 2, k * P:(k + 1) * P],
                                              v[:, b, k, 64 * (h % 2):64 * (h % 2) + 64],
                                              start=(k == 0), stop=(k == i))
                    mm.then_inc(out_done, 1)
                    return mm

                def step(r, b, n):
                    pe.wait_ge(in_place[b], 160 * (2 * i + r + 1))
                    for j in range(5):
                        scores(j, b, n)
                    turn(0, n)
                    scores(5, b, n)
                    mix(0, b, n)
                    for h in (1, 2, 3):
                        turn(h, n)
                        mix(h, b, n)
                steps(pe, i, step)

        @block.scalar
        def _(act):
            prime(act, wT_done)
            prime(act, rows_taken, by=2)
            for i in range(TP):
                width = (i + 1) * P

                def softmax_top(c, n):
                    act.wait_ge(max_done, 4 * n + c + 1)
                    act.wait_ge(turned, 4 * n + c // 2 + 1)
                    nc.scalar.activation(prob[:, c, 0:width], score_ps[:, c % 2, 0:width], ACT.Exp,
                                         bias=neg_max[:, c:c + 1], accum_out=total[:, c:c + 1]).then_inc(prob_done, 1)

                def log_term(s, n):
                    act.wait_ge(scores_done, 6 * n + 5 + s)
                    act.wait_ge(scan_done, 2 * n + s + 1)
                    u = soft[:, s, 0:width]
                    nc.scalar.activation(u, score_ps[:, s, 0:width], ACT.Abs).then_inc(abs_done, 1)
                    act.wait_ge(abs_done, 2 * n + s + 1)
                    nc.scalar.activation(u, u, ACT.Exp, scale=-1.0).then_inc(exp_done, 1)
                    act.wait_ge(exp_done, 2 * n + s + 1)
                    nc.scalar.activation(u, u, ACT.Ln, bias=const.one).then_inc(log_done, 1)

                def take_turned(h, n):
                    act.wait_ge(turned, 4 * n + h + 5)
                    act.wait_ge(out_done, 4 * n + h + 7)
                    nc.scalar.copy(wT[:, h % 2, 0:width], turn_ps[:, 0:width]).then_inc(wT_done, 1)

                def take_out(kind, r, b, n):
                    act.wait_ge(out_done, 4 * n + 2 * kind + 10)
                    nc.scalar.copy(head_rows[:, i % 2, bass.ds(kind * W + (2 * r + b) * P, P)],
                                   out_ps[:, kind, 0:P]).then_inc(rows_taken, 1)

                def step(r, b, n):
                    for c in range(4):
                        softmax_top(c, n)
                    log_term(0, n)
                    take_turned(0, n)
                    log_term(1, n)
                    take_turned(1, n)
                    take_out(0, r, b, n)
                    for s in range(2):
                        act.wait_ge(expo_done, 2 * n + s + 3)
                        nc.scalar.activation(stick[:, s, 0:width], stick[:, s, 0:width], ACT.Exp).then_inc(stick_done, 1)
                    take_turned(2, n)
                    take_turned(3, n)
                    take_out(1, r, b, n)

                if i >= 2:
                    act.wait_ge(stored[i % 2], 16 * (i // 2))
                steps(act, i, step)

        @block.vector
        def _(dve):
            prime(dve, expo_done, scan_done, by=2)
            nc.vector.memset(zeros[:, :], 0.0).then_inc(zeros_done, 1)
            dve.wait_ge(zeros_done, 1)
            for i in range(TP):
                width = (i + 1) * P

                def step(r, b, n):
                    for c in range(4):
                        dve.wait_ge(scores_done, 6 * n + c + 1)
                        nc.vector.tensor_reduce(neg_max[:, c:c + 1], score_ps[:, c % 2, 0:width], AX.X, ALU.max,
                                                negate=True).then_inc(max_done, 1)
                    for h in range(2):
                        dve.wait_ge(prob_done, 4 * n + 2 * h + 2)
                        nc.vector.reciprocal(share[:, 2 * h:2 * h + 2], total[:, 2 * h:2 * h + 2]).then_inc(share_done, 1)
                        dve.wait_ge(share_done, 2 * n + h + 1)
                        b2 = prob[:, 2 * h + 1, 0:width]
                        nc.vector.tensor_scalar(b2, b2, share[:, 2 * h + 1:2 * h + 2], const.lam,
                                                ALU.mult, ALU.mult).then_inc(part_done, 1)
                        dve.wait_ge(part_done, 2 * n + h + 1)
                        b1 = prob[:, 2 * h, 0:width]
                        nc.vector.scalar_tensor_tensor(b1, b1, share[:, 2 * h:2 * h + 1], b2,
                                                       ALU.mult, ALU.subtract).then_inc(weights_done, 1)
                    for s in range(2):
                        z = score_ps[:, s, 0:width]
                        u = soft[:, s, 0:width]
                        e = stick[:, s, 0:width]
                        dve.wait_ge(log_done, 2 * n + s + 1)
                        nc.vector.scalar_tensor_tensor(u, z, 0.0, u, ALU.max, ALU.add).then_inc(soft_done, 1)
                        dve.wait_ge(soft_done, 2 * n + s + 1)
                        dve.wait_ge(turned, 4 * n + s + 3)
                        nc.vector.tensor_tensor_scan(e[:, ::-1], u[:, ::-1], zeros[:, 0:width], 0.0,
                                                     ALU.add, ALU.add).then_inc(scan_done, 1)
                        dve.wait_ge(scan_done, 2 * n + s + 3)
                        nc.vector.tensor_tensor(e, z, e, ALU.subtract).then_inc(expo_done, 1)
                steps(dve, i, step)


def attend_samples(nc, const, ins, qk_turned, new_rows, heads):
    B, S, PAST = 8, 16, 256
    KEYS = PAST + S
    with ExitStack() as ctx:
        def sb(name, shape, dt=F32):
            return ctx.enter_context(nc.sbuf_tensor(name, shape, dt))

        sem = stage_semaphores(nc, ctx)

        cached = sb("cached", [P, 2, 2, 2, W])
        values = sb("values", [P, 2, 2, 3, W])
        qT = sb("qT", [P, 2, 4, P])
        newT = sb("newT", [P, 2, 4, P])
        kT = sb("kT", [P, 2, 4, KEYS])
        queries = sb("queries", [P, 3, 4, P])
        half_mask = sb("half_mask", [P, 3, 4, 8])
        head_mask = sb("head_mask", [P, W])
        fold = sb("fold", [P, S])
        late_mask = sb("late_mask", [P, S])
        prob = sb("sprob", [P, 2, KEYS])
        soft = sb("ssoft", [P, KEYS])
        stick = sb("sstick", [P, KEYS])
        zeros = sb("szeros", [P, KEYS])
        wT = sb("swT", [P, 2, 3 * P])
        own = sb("own", [P, 2, W])
        neg_max = sb("sneg_max", [P, 2])
        total = sb("stotal", [P, 2])
        share = sb("sshare", [P, 2])
        out_rows = sb("out_rows", [S, 2, D])
        k_ps = ctx.enter_context(nc.psum_tensor("k_ps", [P, 2, W], F32))
        score_ps = ctx.enter_context(nc.psum_tensor("sscore_ps", [P, 3, W], F32))
        turn_ps = ctx.enter_context(nc.psum_tensor("sturn_ps", [P, W], F32))
        mix_ps = ctx.enter_context(nc.psum_tensor("mix_ps", [P, W], F32))
        fold_ps = ctx.enter_context(nc.psum_tensor("fold_ps", [P, W], F32))

        tables_in = sem("tables_in")
        batch_in = [sem(f"batch_in{u}") for u in range(2)]
        zeroed = sem("zeroed")
        k_turned = sem("k_turned")
        k_taken = sem("k_taken")
        new_taken = sem("new_taken")
        queries_done = sem("queries_done")
        scores_done = sem("sscores_done")
        max_done = sem("smax_done")
        prob_done = sem("sprob_done")
        share_done = sem("sshare_done")
        part_done = sem("spart_done")
        weights_done = sem("sweights_done")
        abs_done = sem("sabs_done")
        exp_done = sem("sexp_done")
        log_done = sem("slog_done")
        soft_done = sem("ssoft_done")
        scan_done = sem("sscan_done")
        expo_done = sem("sexpo_done")
        stick_done = sem("sstick_done")
        w_turned = sem("sw_turned")
        wT_done = sem("swT_done")
        mixed = sem("mixed")
        own_done = sem("own_done")
        folded = sem("folded")
        taken = sem("taken")
        stored = [sem(f"sstored{u}") for u in range(2)]
        stored_free = sem("stored_free")
        block = ctx.enter_context(nc.Block())

        def batches(eng, body):
            with eng.Fori(0, B // 2) as r:
                for u in range(2):
                    body(r, u, 2 * r + u)

        @block.sync
        def _(sp):
            for a, name in ((half_mask[:, :, :, :].rearrange("p a c h -> p (a c h)"), "half_mask"),
                            (head_mask[:, :], "head_mask"), (fold[:, :], "fold"), (late_mask[:, :], "late_mask")):
                sp.dma_start(a, ins[name]).then_inc(tables_in, 16)
            for kind in range(2):
                for dst, place in ((qT, 2 * kind), (newT, 2 * kind + 1)):
                    sp.dma_start(dst[:, kind, :, :].rearrange("p c n -> p (c n)"),
                                 qk_turned[place, TP, :, :]).then_inc(tables_in, 16)

            def load(r, u, b):
                sp.wait_ge(mixed, 2 * b + 2)
                for kind, (k, v, rows) in enumerate((("cache_diff_k", "cache_diff_v", VD), ("cache_sb_k", "cache_sb_v", VS))):
                    for dst, name in ((cached[:, u, kind, :, :], k), (values[:, u, kind, 0:2, :], v)):
                        sp.dma_start(dst, ins[name][bass.ds(b, 1), :, :]
                                     .rearrange("a (j p) n -> p (a j) n", p=P)).then_inc(batch_in[u], 16)
                    sp.dma_start(values[0:S, u, kind, 2, :],
                                 new_rows[rows][bass.ds(TP * P + b * S, S), :]).then_inc(batch_in[u], 16)
            batches(sp, load)

        @block.gpsimd
        def _(pool):
            prime(pool, stored_free, by=1)

            def store(r, u, b):
                pool.wait_ge(taken, 2 * b + 6)
                pool.dma_start(heads[TP, bass.ds(b * S, S), :], out_rows[:, u, :]).then_inc(stored[u], 16)
                pool.wait_ge(stored[u], 16 * r + 16)
                pool.sem_inc(stored_free, 1)
            batches(pool, store)
            for u in range(2):
                pool.wait_ge(stored[u], 16 * (B // 2))

        @block.tensor
        def _(pe):
            prime(pe, mixed, by=4)
            prime(pe, scores_done, by=3)
            prime(pe, w_turned, by=2)
            prime(pe, folded, by=2)

            def batch(r, u, b):
                pe.wait_ge(batch_in[u], 96 * r + 96)
                for kind in range(2):
                    for blk in range(2):
                        m = 2 * kind + blk
                        pe.wait_ge(k_taken, 4 * b + m + 1)
                        for c in range(4):
                            mm = nc.tensor.transpose(k_ps[:, m % 2, c * P:(c + 1) * P],
                                                     cached[:, u, kind, blk, c * P:(c + 1) * P], const.ident)
                        mm.then_inc(k_turned, 1)
                for j in range(3):
                    kind = j // 2
                    pe.wait_ge(k_taken, 4 * b + 2 * kind + 4)
                    pe.wait_ge(new_taken, 2 * b + kind + 1)
                    pe.wait_ge(queries_done, 3 * b + j + 1)
                    if j < 2:
                        pe.wait_ge(prob_done, 2 * b + j + 1)
                    else:
                        pe.wait_ge(expo_done, b + 1)
                    for c in range(4):
                        mm = nc.tensor.matmul(score_ps[:, j, 0:KEYS], queries[:, j, c, :], kT[:, kind, c, :],
                                              start=(c == 0), stop=(c == 3 and j < 2))
                    if j == 2:
                        mm = nc.tensor.matmul(score_ps[:, j, PAST:KEYS], const.ident, late_mask[:, :],
                                              start=False, stop=True)
                    mm.then_inc(scores_done, 1)
                for kind, w, ready in ((0, prob[:, 0, :], weights_done), (1, stick[:, :], stick_done)):
                    pe.wait_ge(ready, b + 1)
                    pe.wait_ge(wT_done, 4 * b + 2 * kind + 1)
                    for k in range(3):
                        n = min(P, KEYS - k * P)
                        mm = nc.tensor.transpose(turn_ps[0:n, k * P:(k + 1) * P], w[:, k * P:k * P + n], const.ident)
                    mm.then_inc(w_turned, 1)
                    pe.wait_ge(wT_done, 4 * b + 2 * kind + 3)
                    pe.wait_ge(own_done, 2 * b + kind + 1)
                    for k in range(3):
                        n = min(P, KEYS - k * P)
                        mm = nc.tensor.matmul(mix_ps[:, :], wT[0:n, kind, k * P:(k + 1) * P],
                                              values[0:n, u, kind, k, :], start=(k == 0), stop=(k == 2))
                    mm.then_inc(mixed, 1)
                    pe.wait_ge(own_done, 2 * b + kind + 2)
                    pe.wait_ge(taken, 2 * b + kind + 4)
                    nc.tensor.matmul(fold_ps[0:S, :], fold[:, :], own[:, kind, :],
                                     start=True, stop=True).then_inc(folded, 1)
            batches(pe, batch)

        @block.scalar
        def _(act):
            prime(act, prob_done, by=2)
            prime(act, k_taken, by=2)
            prime(act, wT_done, by=1)
            prime(act, taken, by=4)

            def batch(r, u, b):
                for m in range(4):
                    act.wait_ge(k_turned, 4 * b + m + 1)
                    act.wait_ge(scores_done, 3 * b + 3)
                    nc.scalar.copy(kT[:, m // 2, :, (m % 2) * P:(m % 2 + 1) * P],
                                   k_ps[:, m % 2, :].rearrange("p (c n) -> p c n", n=P)).then_inc(k_taken, 1)
                for c in range(2):
                    act.wait_ge(max_done, 2 * b + c + 1)
                    act.wait_ge(w_turned, 2 * b + 1)
                    nc.scalar.activation(prob[:, c, :], score_ps[:, c, 0:KEYS], ACT.Exp, bias=neg_max[:, c:c + 1],
                                         accum_out=total[:, c:c + 1]).then_inc(prob_done, 1)
                act.wait_ge(scores_done, 3 * b + 6)
                act.wait_ge(scan_done, b + 1)
                nc.scalar.activation(soft[:, :], score_ps[:, 2, 0:KEYS], ACT.Abs).then_inc(abs_done, 1)
                act.wait_ge(abs_done, b + 1)
                nc.scalar.activation(soft[:, :], soft[:, :], ACT.Exp, scale=-1.0).then_inc(exp_done, 1)
                act.wait_ge(exp_done, b + 1)
                nc.scalar.activation(soft[:, :], soft[:, :], ACT.Ln, bias=const.one).then_inc(log_done, 1)
                for kind in range(2):
                    if kind == 1:
                        act.wait_ge(expo_done, b + 2)
                        nc.scalar.activation(stick[:, :], stick[:, :], ACT.Exp).then_inc(stick_done, 1)
                    act.wait_ge(w_turned, 2 * b + kind + 3)
                    act.wait_ge(mixed, 2 * b + kind + 3)
                    nc.scalar.copy(wT[:, kind, 0:2 * P], turn_ps[:, 0:2 * P]).then_inc(wT_done, 1)
                    nc.scalar.copy(wT[0:S, kind, 2 * P:3 * P], turn_ps[0:S, 2 * P:3 * P]).then_inc(wT_done, 1)
                    act.wait_ge(folded, 2 * b + kind + 3)
                    act.wait_ge(stored_free, b + 1)
                    nc.scalar.copy(out_rows[:, u, kind * W:(kind + 1) * W], fold_ps[0:S, :]).then_inc(taken, 1)
            batches(act, batch)

        @block.vector
        def _(dve):
            prime(dve, expo_done, scan_done, own_done)
            nc.vector.memset(zeros[:, :], 0.0).then_inc(zeroed, 1)
            dve.wait_ge(zeroed, 1)
            dve.wait_ge(tables_in, 8 * 16)

            def batch(r, u, b):
                at = bass.ds(b * S, S)
                dve.wait_ge(scores_done, 3 * b + 3)
                for kind in range(2):
                    nc.vector.tensor_copy(kT[:, kind, :, PAST:KEYS], newT[:, kind, :, at]).then_inc(new_taken, 1)
                for j in range(3):
                    nc.vector.tensor_tensor(
                        queries[:, j, :, :].rearrange("p c (h q) -> p c h q", q=S),
                        qT[:, j // 2, :, at].unsqueeze(2).broadcast_to((P, 4, 8, S)),
                        half_mask[:, j, :, :].unsqueeze(3).broadcast_to((P, 4, 8, S)), ALU.mult).then_inc(queries_done, 1)
                for c in range(2):
                    dve.wait_ge(scores_done, 3 * b + c + 4)
                    nc.vector.tensor_reduce(neg_max[:, c:c + 1], score_ps[:, c, 0:KEYS], AX.X, ALU.max,
                                            negate=True).then_inc(max_done, 1)
                dve.wait_ge(prob_done, 2 * b + 4)
                nc.vector.reciprocal(share[:, :], total[:, :]).then_inc(share_done, 1)
                dve.wait_ge(share_done, b + 1)
                nc.vector.tensor_scalar(prob[:, 1, :], prob[:, 1, :], share[:, 1:2], const.lam,
                                        ALU.mult, ALU.mult).then_inc(part_done, 1)
                dve.wait_ge(part_done, b + 1)
                nc.vector.scalar_tensor_tensor(prob[:, 0, :], prob[:, 0, :], share[:, 0:1], prob[:, 1, :],
                                               ALU.mult, ALU.subtract).then_inc(weights_done, 1)
                z = score_ps[:, 2, 0:KEYS]
                dve.wait_ge(log_done, b + 1)
                nc.vector.scalar_tensor_tensor(soft[:, :], z, 0.0, soft[:, :], ALU.max, ALU.add).then_inc(soft_done, 1)
                dve.wait_ge(soft_done, b + 1)
                dve.wait_ge(w_turned, 2 * b + 2)
                nc.vector.tensor_tensor_scan(stick[:, ::-1], soft[:, ::-1], zeros[:, :], 0.0,
                                             ALU.add, ALU.add).then_inc(scan_done, 1)
                dve.wait_ge(scan_done, b + 2)
                nc.vector.tensor_tensor(stick[:, :], z, stick[:, :], ALU.subtract).then_inc(expo_done, 1)
                for kind in range(2):
                    dve.wait_ge(mixed, 2 * b + kind + 5)
                    dve.wait_ge(folded, 2 * b + kind + 1)
                    nc.vector.tensor_tensor(own[:, kind, :], mix_ps[:, :], head_mask[:, :], ALU.mult).then_inc(own_done, 1)
            batches(dve, batch)


HEADS, TOP, SIDE = 8, 16, 128
ROWS = HEADS * TOP
FIRST = 0
U_RING, V_RING, DIAGS = 4, 8, 4


def route_and_sum_experts(nc, const, ins, heads, summed):
    with ExitStack() as ctx:
        def sb(name, shape, dt=F32):
            return ctx.enter_context(nc.sbuf_tensor(name, shape, dt))

        def psum(name, shape):
            return ctx.enter_context(nc.psum_tensor(name, shape, F32))

        sem = stage_semaphores(nc, ctx)

        w_out = sb("w_out_sb", [P, KC, D])
        w_query = sb("w_query_sb", [P, KC, 2 * D])
        u_rows = [sb(f"u_rows{n}", [P, D]) for n in range(U_RING)]
        v_rows = [sb(f"v_rows{n}", [P, D]) for n in range(V_RING)]
        c_rows = sb("c_rows", [P, D])
        idx_now = sb("idx_now", [P, ROWS], U32)
        gate_now = sb("gate_now", [P, ROWS])
        dots = sb("dots", [P, 2, TOP])
        gelus = sb("gelus", [P, 2, TOP])
        coef = sb("coef", [P, 2, TOP])
        diag = sb("diag", [P, DIAGS, P])
        keysT = sb("keysT", [P, 2, P])
        gain = sb("ffn_gain", [P, D])
        sub_gain = sb("sub_gain", [P, 64])
        steps16 = sb("steps16", [P, TOP])
        x = sb("rx", [P, D])
        mix = sb("mix", [P, D])
        inT = sb("inT", [P, KC, P])
        keys = inT[:, 0:2, :]
        c = sb("c", [P, D])
        query = sb("query", [P, 2, W])
        queryT = sb("queryT", [P, 2, W])
        sum_out = queryT
        scores = sb("scores", [P, 16, SIDE])
        spare = sb("spare", [P, 16, SIDE])
        work = spare[:, 0:D // SIDE, :].rearrange("p m n -> p (m n)")
        top = sb("top", [P, 16, TOP])
        pos = sb("pos", [P, 16, TOP], U32)
        posf = sb("posf", [P, 16, TOP])
        val = sb("val", [P, HEADS, TOP])
        sel = sb("sel", [P, HEADS, TOP], U32)
        part = sb("part", [P, 2, HEADS, TOP], U32)
        partf = sb("partf", [P, 2, HEADS, TOP])
        picked = sb("picked", [P, 2, HEADS, TOP])
        idx_tile = sb("idx_tile", [P, ROWS], U32)
        gate_tile = sb("gate_tile", [P, ROWS])
        stat = sb("rstat", [P, 4, 8])
        sum_ps = psum("sum_ps", [P, D])
        turn_ps = psum("rturn_ps", [P, D])
        acc_ps = psum("acc_ps", [P, 2, W])
        qT_ps = psum("qT_ps", [P, W])
        score_ps = psum("rscore_ps", [P, W])

        tables_in = sem("rtables_in")
        out_w_in = sem("out_w_in")
        query_w_in = sem("query_w_in")
        x_in = sem("rx_in")
        mix_in = sem("mix_in")
        keys_turned = sem("keys_turned")
        keys_done = sem("keys_done")
        self_done = sem("rself_done")
        mean_done = sem("rmean_done")
        rstd_done = sem("rrstd_done")
        mix_done = sem("mix_done")
        turned = sem("rturned")
        inT_done = sem("inT_done")
        acc_done = sem("acc_done")
        h_done = sem("h_done")
        c_done = sem("c_done")
        query_done = sem("query_done")
        query_turned = sem("query_turned")
        queryT_done = sem("queryT_done")
        scored = sem("scored")
        scores_done = sem("rscores_done")
        shifted = sem("shifted")
        raised = sem("raised")
        idx_done = sem("idx_done")
        gates_done = sem("gates_done")
        idx_taken = sem("idx_taken")
        gates_taken = sem("gates_taken")
        c_taken = sem("c_taken")
        opened = sem("opened")
        u_in = [sem(f"u_in{n}") for n in range(U_RING)]
        v_in = [sem(f"v_in{n}") for n in range(V_RING)]
        u_used = sem("u_used")
        v_used = sem("v_used")
        gelu_done = sem("gelu_done")
        coef_done = sem("coef_done")
        diag_done = sem("diag_done")
        sum_taken = sem("sum_taken")
        sum_stored = sem("sum_stored")
        sum_free = sem("sum_free")
        block = ctx.enter_context(nc.Block())
        SELF = 23

        @block.sync
        def _(sp):
            for dst, src in ((gain[:, :], bass.AP(ins["g_ffn"].tensor, 0, [[0, P], [1, D]])),
                             (sub_gain[:, :], bass.AP(ins["g_subln"].tensor, 0, [[0, P], [1, 64]])),
                             (steps16[:, :], ins["steps16"]),
                             (keys[:, :, :], ins["sub_keys"].rearrange("s n d -> n s d"))):
                sp.dma_start(dst, src).then_inc(tables_in, 16)
            sp.dma_start(x[:, :], ins["x_all"][0:P, :]).then_inc(x_in, 16)
            sp.dma_start(mix[:, :], heads[0]).then_inc(mix_in, 16)
            sp.dma_start(w_out[:, :, :], ins["w_out"].rearrange("(k p) n -> p k n", p=P)).then_inc(out_w_in, 16)
            sp.dma_start(w_query[:, :, :], ins["w_query"].rearrange("(k p) n -> p k n", p=P)).then_inc(query_w_in, 16)
            prime(sp, sum_free, by=2)

            def store(e):
                sp.wait_ge(sum_taken, e + 2)
                sp.dma_start(summed[bass.ds(e, 1), :, :].rearrange("a p n -> (a p) n"),
                             sum_out[:, :, :].rearrange("p a n -> p (a n)")).then_inc(sum_stored, 16)
                sp.wait_ge(sum_stored, e * 16 + 16)
                sp.sem_inc(sum_free, 1)

            with sp.Fori(1, T) as t:
                sp.wait_ge(turned, 2 * t + 1)
                sp.dma_start(mix[:, :], heads[bass.ds(t, 1), :, :].rearrange("a p n -> (a p) n")).then_inc(mix_in, 16)
                sp.wait_ge(opened, t)
                sp.dma_start(x[:, :], ins["x_all"][bass.ds(t * P, P), :]).then_inc(x_in, 16)
                store(t - 1)
            store(T - 1)

        @block.gpsimd
        def _(pool):
            def power(t, n):
                width = (8, 1)[n]
                pool.wait_ge(mean_done, 2 * t + (n + 1))
                nc.gpsimd.tensor_tensor(stat[:, 2, 0:width], stat[:, 1, 0:width],
                                        const.minus_half.broadcast_to((P, width)), ALU.pow).then_inc(rstd_done, 1)

            def take_idx(e, part, a, b):
                pool.wait_ge(idx_done, e + 2)
                wait_apart(pool, const, v_used, e * ROWS + (V_RING if part else 1))
                nc.gpsimd.tensor_copy(idx_now[:, a * TOP:b * TOP],
                                      idx_tile[:, a * TOP:b * TOP]).then_inc(idx_taken, 1)
                pool.wait_ge(idx_taken, 2 * e + part + 1)

            def gather(e, a, rows, ring, used, landed, table):
                wait_apart(pool, const, used, e * ROWS + (a + 1))
                pool.indirect_dma_start(rows[a % ring][:, :], None, ins[table],
                                        bass.IndirectOffsetOnAxis(ap=idx_now[:, a:a + 1], axis=0)
                                        ).then_inc(landed[a % ring], 16)

            def weigh(e, s):
                if s == 0:
                    wait_apart(pool, const, gates_done, e + 2)
                    nc.gpsimd.tensor_copy(gate_now[:, :], gate_tile[:, :]).then_inc(gates_taken, 1)
                    pool.wait_ge(gates_taken, e + 1)
                pool.wait_ge(gelu_done, e * HEADS + (s + 1))
                nc.gpsimd.tensor_tensor(coef[:, s % 2, :], gelus[:, s % 2, :], gate_now[:, s * TOP:(s + 1) * TOP],
                                        ALU.mult).then_inc(coef_done, 1)

            def tile(e, t):
                for s in range(HEADS):
                    if s < 2:
                        take_idx(e, s, *((0, HEADS - 1), (HEADS - 1, HEADS))[s])
                    for k in range(TOP):
                        gather(e, s * TOP + k, u_rows, U_RING, u_used, u_in, "expert_u")
                    for k in range(TOP):
                        if k == V_RING:
                            weigh(e, s)
                            if t is not None and s < 2:
                                power(t, s)
                        gather(e, s * TOP + k, v_rows, V_RING, v_used, v_in, "expert_v")

            for n in range(2):
                power(0, n)
            with pool.Fori(1, T) as t:
                tile(t - 1, t)
            tile(T - 1, None)

        @block.tensor
        def _(pe):
            pe.wait_ge(tables_in, 64)
            for s in range(2):
                mm = nc.tensor.transpose(qT_ps[:, s * P:(s + 1) * P], keys[:, s, :], const.ident)
            mm.then_inc(keys_turned, 1)
            prime(pe, turned, by=2)
            prime(pe, scored, query_turned, by=4)
            prime(pe, v_used, by=V_RING)
            pe.wait_ge(keys_done, 1)

            def turn(src, ready, t, n):
                pe.wait_ge(*ready)
                for k in range(KC):
                    mm = nc.tensor.transpose(turn_ps[:, k * P:(k + 1) * P], src[:, k * P:(k + 1) * P], const.ident)
                mm.then_inc(turned, 1)
                pe.wait_ge(inT_done, 2 * t + n)

            def product(weights, half, bank):
                for k in range(KC):
                    mm = nc.tensor.matmul(acc_ps[:, bank, :], inT[:, k, :], weights[:, k, half * W:(half + 1) * W],
                                          start=(k == 0), stop=(k == KC - 1))
                mm.then_inc(acc_done, 1)

            def project_heads(t):
                turn(mix, (mix_done, t + 1), t, 1)
                pe.wait_ge(out_w_in, 16)
                pe.wait_ge(query_done, 4 * t + 4)
                for n in range(2):
                    product(w_out, n, n)

            def queries(t, g):
                if g == 0:
                    turn(c, (c_done, t + 2), t, 2)
                    pe.wait_ge(query_w_in, 16)
                if g < 2:
                    pe.wait_ge(h_done, t + 2)
                else:
                    pe.wait_ge(query_done, 4 * t + (g + 3))
                product(w_query, g, g % 2)

            def match(t, g):
                pe.wait_ge(query_done, 4 * t + (g + 5))
                pe.wait_ge(queryT_done, 4 * t + (g + 4))
                for m in range(4):
                    mm = nc.tensor.transpose(qT_ps[:, m * P:(m + 1) * P],
                                             query[:, g % 2, m * P:(m + 1) * P], const.ident)
                mm.then_inc(query_turned, 1)
                pe.wait_ge(queryT_done, 4 * t + (g + 5))
                pe.wait_ge(scores_done, 4 * t + (g + 4))
                for m in range(4):
                    mm = nc.tensor.matmul(score_ps[:, m * P:(m + 1) * P], queryT[:, g % 2, m * P:(m + 1) * P],
                                          keysT[:, m % 2, :], start=True, stop=True)
                mm.then_inc(scored, 1)

            def open_sum(e):
                pe.wait_ge(h_done, e + 2)
                pe.wait_ge(sum_taken, e + 1)
                for n in range(2):
                    mm = nc.tensor.matmul(sum_ps[:, n * W:(n + 1) * W], const.ident, x[:, n * W:(n + 1) * W],
                                          start=True, stop=False, skip_group_check=True)
                mm.then_inc(opened, 1)

            def add_rows(e, s):
                for k in range(TOP):
                    a = s * TOP + k
                    pe.wait_ge(v_in[a % V_RING], e * (ROWS // V_RING * 16) + (a // V_RING + 1) * 16)
                    pe.wait_ge(diag_done, e * ROWS + (a + 1))
                    for n in range(2):
                        mm = nc.tensor.matmul(sum_ps[:, n * W:(n + 1) * W], diag[:, a % DIAGS, :],
                                              v_rows[a % V_RING][:, n * W:(n + 1) * W],
                                              start=False, stop=(k == TOP - 1), skip_group_check=True)
                    mm.then_inc(v_used, 1)

            def tile(e, t):
                for s in range(HEADS):
                    if s == 0:
                        open_sum(e)
                    elif t is not None:
                        if s == 1:
                            project_heads(t)
                        elif s == 2:
                            queries(t, 0)
                            queries(t, 1)
                            match(t, 0)
                        elif s == 3:
                            queries(t, 2)
                            match(t, 1)
                            queries(t, 3)
                            match(t, 2)
                            match(t, 3)
                    add_rows(e, s)

            project_heads(0)
            for g in range(4):
                queries(0, g)
                if g:
                    match(0, g - 1)
            match(0, 3)
            with pe.Fori(1, T) as t:
                tile(t - 1, t)
            tile(T - 1, None)

        @block.scalar
        def _(act):
            prime(act, query_done, queryT_done, scores_done, by=4)
            prime(act, sum_taken)
            act.wait_ge(keys_turned, 1)
            nc.scalar.copy(keysT[:, :, :].rearrange("p s n -> p (s n)"), qT_ps[:, 0:2 * P]).then_inc(keys_done, 1)

            def take_turned(t, n):
                act.wait_ge(turned, 2 * t + (n + 3))
                nc.scalar.copy(inT[:, :, :].rearrange("p k n -> p (k n)"), turn_ps[:, :]).then_inc(inT_done, 1)

            def take_query(t, g):
                act.wait_ge(acc_done, 6 * t + (g + 3))
                act.wait_ge(query_turned, 4 * t + (g + 3))
                nc.scalar.copy(query[:, g % 2, :], acc_ps[:, g % 2, :]).then_inc(query_done, 1)

            def take_scores(t, g):
                act.wait_ge(query_turned, 4 * t + (g + 5))
                act.wait_ge(scored, 4 * t + (g + 3))
                if g == 0:
                    act.wait_ge(sum_free, t + 1)
                nc.scalar.copy(queryT[:, g % 2, :], qT_ps[:, :]).then_inc(queryT_done, 1)
                act.wait_ge(scored, 4 * t + (g + 5))
                if g == 0:
                    act.wait_ge(idx_done, t + 1)
                nc.scalar.copy(scores[:, 4 * g:4 * g + 4, :].rearrange("p m n -> p (m n)"),
                               score_ps[:, :]).then_inc(scores_done, 1)

            def exponents(t):
                act.wait_ge(shifted, t + 1)
                nc.scalar.activation(picked[:, 1, :, :], picked[:, 1, :, :], ACT.Exp).then_inc(raised, 1)

            def take_tokens(e):
                act.wait_ge(c_done, e + 2)
                act.wait_ge(u_used, e * ROWS + U_RING)
                nc.scalar.copy(c_rows[:, :], c[:, :]).then_inc(c_taken, 1)

            def spread(e, s):
                act.wait_ge(u_used, e * ROWS + ((s + 1) * TOP + U_RING))
                nc.scalar.activation(gelus[:, s % 2, :], dots[:, s % 2, :], ACT.Gelu).then_inc(gelu_done, 1)
                act.wait_ge(coef_done, e * HEADS + (s + 1))
                for k in range(TOP):
                    a = s * TOP + k
                    act.wait_ge(v_used, e * ROWS + (a + 1 + V_RING - DIAGS))
                    nc.scalar.mul(diag[:, a % DIAGS, :], const.ident, coef[:, s % 2, k:k + 1]).then_inc(diag_done, 1)

            def close_sum(e):
                act.wait_ge(v_used, e * ROWS + (ROWS + V_RING))
                act.wait_ge(sum_free, e + 2)
                nc.scalar.copy(sum_out[:, :, :].rearrange("p a n -> p (a n)"), sum_ps[:, :]).then_inc(sum_taken, 1)

            def tile(e, t):
                take_tokens(e)
                for s in range(HEADS):
                    if t is not None:
                        if s == 1:
                            take_turned(t, 0)
                        elif s == 2:
                            take_turned(t, 1)
                            take_query(t, 0)
                            take_query(t, 1)
                            take_scores(t, 0)
                        elif s == 3:
                            take_query(t, 2)
                            take_scores(t, 1)
                            take_query(t, 3)
                            take_scores(t, 2)
                            take_scores(t, 3)
                        elif s == 7:
                            exponents(t)
                    spread(e, s)
                close_sum(e)

            take_turned(0, 0)
            take_turned(0, 1)
            for g in range(4):
                take_query(0, g)
                if g:
                    take_scores(0, g - 1)
            take_scores(0, 3)
            exponents(0)
            with act.Fori(1, T) as t:
                tile(t - 1, t)
            tile(T - 1, None)

        @block.vector
        def _(dve):
            prime(dve, h_done, c_done, idx_done, gates_done)
            prime(dve, u_used, by=U_RING)
            dve.wait_ge(tables_in, 64)
            at = [0]

            def chain(t, done):
                at[0] += 1
                done.then_inc(self_done, 1)
                wait_apart(dve, const, self_done, t * SELF + at[0])

            def by_head(a):
                return a.rearrange("p (h d) -> p h d", d=64)

            def norm_heads(t):
                at[0] = 0
                dve.wait_ge(mix_in, t * 16 + 16)
                diff = mix[:, 0:W]
                chain(t, nc.vector.tensor_tensor(work[:, 0:W], diff, diff, ALU.mult))
                chain(t, nc.vector.tensor_reduce(stat[:, 0, :], by_head(work[:, 0:W]), AX.X, ALU.add))
                nc.vector.tensor_scalar(stat[:, 1, :], stat[:, 0, :], 1.0 / 64, 1e-5, ALU.mult,
                                        ALU.add).then_inc(mean_done, 1)
                dve.wait_ge(rstd_done, 2 * t + 1)
                chain(t, nc.vector.tensor_tensor(by_head(work[:, 0:W]), by_head(diff),
                                                 stat[:, 2, :].unsqueeze(2).broadcast_to((P, 8, 64)), ALU.mult))
                nc.vector.scalar_tensor_tensor(by_head(diff), by_head(work[:, 0:W]), 1.0 - LAMBDA_START,
                                               sub_gain[:, :].unsqueeze(1).broadcast_to((P, 8, 64)),
                                               ALU.mult, ALU.mult).then_inc(mix_done, 1)

            def norm_tokens(t):
                dve.wait_ge(x_in, t * 16 + 16)
                dve.wait_ge(acc_done, 6 * t + 2)
                nc.vector.tensor_tensor(x[:, :], x[:, :], acc_ps[:, :, :].rearrange("p a n -> p (a n)"),
                                        ALU.add).then_inc(h_done, 1)
                dve.wait_ge(h_done, t + 2)
                chain(t, nc.vector.tensor_tensor_reduce(work, x[:, :], x[:, :], 1.0, 0.0, ALU.mult, ALU.add,
                                                        stat[:, 0, 0:1]))
                nc.vector.tensor_scalar(stat[:, 1, 0:1], stat[:, 0, 0:1], 1.0 / D, EPS,
                                        ALU.mult, ALU.add).then_inc(mean_done, 1)
                dve.wait_ge(rstd_done, 2 * t + 2)
                if t is not FIRST:
                    dve.wait_ge(c_taken, t)
                nc.vector.scalar_tensor_tensor(c[:, :], x[:, :], stat[:, 2, 0:1], gain[:, :],
                                               ALU.mult, ALU.mult).then_inc(c_done, 1)

            def best8(t, src, rest, vals):
                n = src.shape[1]
                for m in range(n):
                    last = nc.vector.max(vals[:, m, 0:8], src[:, m, :])
                chain(t, last)
                for m in range(n):
                    last = nc.vector.match_replace(rest[:, m, :], vals[:, m, 0:8], src[:, m, :], -3e38)
                chain(t, last)

            def next8(t, src, rest, vals, places):
                n = src.shape[1]
                for m in range(n):
                    last = nc.vector.max(vals[:, m, 8:16], rest[:, m, :])
                for m in range(n):
                    last = nc.vector.max_index(places[:, m, 0:8], vals[:, m, 0:8], src[:, m, :])
                chain(t, last)
                for m in range(n):
                    last = nc.vector.max_index(places[:, m, 8:16], vals[:, m, 8:16], rest[:, m, :])
                chain(t, last)

            wide = scores[:, :, :].rearrange("p m n -> p (m n)")
            spare_wide = spare[:, :, :].rearrange("p m n -> p (m n)")
            of_sides = (scores[:, :, :], spare[:, :, :], top[:, :, :])
            of_sums = (wide.rearrange("p (h n) -> p h n", h=HEADS), spare_wide.rearrange("p (h n) -> p h n", h=HEADS),
                       val[:, :, :])

            def best_sides(t):
                wait_apart(dve, const, scores_done, 4 * t + 8)
                best8(t, *of_sides)

            def best_sums(t):
                next8(t, *of_sides, pos[:, :, :])
                sides = top[:, :, :].rearrange("p (h s) a -> p h s a", s=2)
                grid = wide.rearrange("p (h a b) -> p h a b", a=TOP, b=TOP)
                chain(t, nc.vector.tensor_tensor(grid, sides[:, :, 0, :].unsqueeze(3).broadcast_to((P, HEADS, TOP, TOP)),
                                                 sides[:, :, 1, :].unsqueeze(2).broadcast_to((P, HEADS, TOP, TOP)),
                                                 ALU.add))

            def places_of_sums(t):
                best8(t, *of_sums)
                next8(t, *of_sums, sel[:, :, :])
                nc.vector.tensor_scalar(part[:, 0, :, :], sel[:, :, :], 4, None, ALU.logical_shift_right)

            def experts_of_places(t):
                nc.vector.tensor_copy(posf[:, :, :], pos[:, :, :])
                chain(t, nc.vector.tensor_scalar(part[:, 1, :, :], sel[:, :, :], 15, None, ALU.bitwise_and))
                chain(t, nc.vector.tensor_copy(partf[:, :, :, :], part[:, :, :, :]))
                keys_at = posf[:, :, :].rearrange("p (h s) a -> p h s a", s=2)
                for s in range(2):
                    buf = (wide, spare_wide)[s].rearrange("p (h k a) -> p h k a", k=TOP, a=TOP)
                    hk = buf.rearrange("p h k a -> p (h k) a")
                    chain(t, nc.vector.tensor_tensor(
                        hk, partf[:, s, :, :].rearrange("p h k -> p (h k)").unsqueeze(2).broadcast_to((P, P, TOP)),
                        steps16[:, :].unsqueeze(1).broadcast_to((P, P, TOP)), ALU.is_equal))
                    chain(t, nc.vector.tensor_tensor(buf, buf, keys_at[:, :, s, :].unsqueeze(2)
                                                     .broadcast_to((P, HEADS, TOP, TOP)), ALU.mult))
                    last = nc.vector.tensor_reduce(picked[:, s, :, :].rearrange("p h k -> p (h k)"), hk, AX.X, ALU.add)
                chain(t, last)
                chain(t, nc.vector.scalar_tensor_tensor(picked[:, 0, :, :], picked[:, 0, :, :], float(SIDE),
                                                        picked[:, 1, :, :], ALU.mult, ALU.add))
                if t is not FIRST:
                    dve.wait_ge(idx_taken, 2 * t)
                nc.vector.tensor_copy(idx_tile[:, :], picked[:, 0, :, :].rearrange("p h k -> p (h k)")
                                      ).then_inc(idx_done, 1)
                nc.vector.tensor_tensor(picked[:, 1, :, :], val[:, :, :], val[:, :, 0:1].broadcast_to((P, HEADS, TOP)),
                                        ALU.subtract).then_inc(shifted, 1)

            def gates(t):
                dve.wait_ge(raised, t + 1)
                chain(t, nc.vector.tensor_reduce(stat[:, 0, :], picked[:, 1, :, :], AX.X, ALU.add))
                chain(t, nc.vector.reciprocal(stat[:, 3, :], stat[:, 0, :]))
                if t is not FIRST:
                    dve.wait_ge(gates_taken, t)
                nc.vector.tensor_tensor(gate_tile[:, :].rearrange("p (h k) -> p h k", k=TOP),
                                        picked[:, 1, :, :], stat[:, 3, :].unsqueeze(2).broadcast_to((P, HEADS, TOP)),
                                        ALU.mult).then_inc(gates_done, 1)
                assert at[0] == SELF, at[0]

            parts = (norm_heads, norm_tokens, None, best_sides, best_sums, places_of_sums, experts_of_places, gates)

            def tile(e, t):
                dve.wait_ge(c_taken, e + 1)
                for s in range(HEADS):
                    for k in range(TOP):
                        a = s * TOP + k
                        dve.wait_ge(u_in[a % U_RING], e * (ROWS // U_RING * 16) + (a // U_RING + 1) * 16)
                        row = u_rows[a % U_RING][:, :]
                        nc.vector.tensor_tensor_reduce(row, row, c_rows[:, :], 1.0, 0.0, ALU.mult, ALU.add,
                                                       dots[:, s % 2, k:k + 1]).then_inc(u_used, 1)
                    if t is not None and s != 2:
                        parts[s](t)

            for s in range(HEADS):
                if s != 2:
                    parts[s](FIRST)
            with dve.Fori(1, T) as t:
                tile(t - 1, t)
            tile(T - 1, None)


def finish(nc, const, ins, summed, y):
    with ExitStack() as ctx:
        def sb(name, shape, dt=F32):
            return ctx.enter_context(nc.sbuf_tensor(name, shape, dt))

        sem = stage_semaphores(nc, ctx)

        w_gate = sb("w_gate_sb", [P, KC, D])
        w_ple = sb("w_ple_sb", [P, 2, D])
        gains = sb("gains", [P, 2, D])
        h = [sb(f"fh{u}", [P, D]) for u in range(2)]
        p_rows = [sb(f"p_rows{u}", [P, 2, P]) for u in range(2)]
        pT = sb("pT", [P, 2, P])
        b = sb("fb", [P, D])
        bT = sb("bT", [P, KC, P])
        gate = sb("fgate", [P, D])
        squares = sb("fsquares", [P, D])
        y_sb = sb("y_sb", [P, D])
        stat = sb("fstat", [P, 2, 4])
        turn_ps = ctx.enter_context(nc.psum_tensor("fturn_ps", [P, D], F32))
        p_ps = ctx.enter_context(nc.psum_tensor("p_ps", [P, 2, P], F32))
        gate_ps = ctx.enter_context(nc.psum_tensor("gate_ps", [P, D], F32))
        ple_ps = ctx.enter_context(nc.psum_tensor("ple_ps", [P, D], F32))

        tables_in = sem("ftables_in")
        gate_w_in = sem("gate_w_in")
        ple_w_in = sem("ple_w_in")
        tile_in = [sem(f"ftile_in{u}") for u in range(2)]
        squared = sem("fsquared")
        mean_done = sem("fmean_done")
        rstd_done = sem("frstd_done")
        b_done = sem("b_done")
        turned = sem("fturned")
        taken = sem("ftaken")
        gate_summed = sem("gate_summed")
        ple_summed = sem("ple_summed")
        gate_done = sem("gate_done")
        mixed = sem("fmixed")
        added = sem("fadded")
        y_done = sem("y_done")
        y_out = sem("y_out")
        y_free = sem("y_free")
        block = ctx.enter_context(nc.Block())

        def tiles(eng, body):
            body(0, 0, None)
            with eng.Fori(0, TP // 2) as r:
                for u in (1, 2):
                    body(2 * r + u, u % 2, r)


        @block.sync
        def _(sp):
            for n, name in enumerate(("g_ple", "g_final")):
                sp.dma_start(gains[:, n, :], bass.AP(ins[name].tensor, 0, [[0, P], [1, D]])).then_inc(tables_in, 16)
            sp.dma_start(h[0][:, :], summed[0]).then_inc(tile_in[0], 16)
            sp.dma_start(p_rows[0][:, :, :].rearrange("p c n -> p (c n)"), ins["p_all"][0:P, :]).then_inc(tile_in[0], 16)
            sp.dma_start(w_ple[:, :, :], ins["w_ple"].rearrange("(k p) n -> p k n", p=P)).then_inc(ple_w_in, 16)
            sp.dma_start(w_gate[:, :, :], ins["w_pgate"].rearrange("(k p) n -> p k n", p=P)).then_inc(gate_w_in, 16)
            prime(sp, y_free)

            def store(t):
                sp.wait_ge(y_done, t + 2)
                sp.dma_start(y[bass.ds(t * P, P), :], y_sb[:, :]).then_inc(y_out, 16)
                sp.wait_ge(y_out, t * 16 + 16)
                sp.sem_inc(y_free, 1)

            with sp.Fori(0, TP // 2) as r:
                for u in (1, 2):
                    t = 2 * r + u
                    sp.wait_ge(y_done, t)
                    sp.dma_start(h[u % 2][:, :], summed[bass.ds(t, 1), :, :].rearrange("a p n -> (a p) n")
                                 ).then_inc(tile_in[u % 2], 16)
                    sp.dma_start(p_rows[u % 2][:, :, :].rearrange("p c n -> p (c n)"),
                                 ins["p_all"][bass.ds(t * P, P), :]).then_inc(tile_in[u % 2], 16)
                    store(t - 1)
            store(TP)

        @block.gpsimd
        def _(pool):
            def power(n, count):
                pool.wait_ge(mean_done, count)
                nc.gpsimd.tensor_tensor(stat[:, n, 2:3], stat[:, n, 1:2], const.minus_half, ALU.pow).then_inc(rstd_done, 1)

            power(0, 1)
            with pool.Fori(0, TP // 2) as r:
                for u in (1, 2):
                    t = 2 * r + u
                    power(0, 2 * t)
                    power(1, 2 * t + 1)
            power(1, 2 * T)

        @block.tensor
        def _(pe):
            prime(pe, turned, by=2)
            prime(pe, gate_summed)

            def tile(t, u, r):
                pe.wait_ge(tile_in[u], 32 if r is None else 32 * r + (32 if u else 64))
                pe.wait_ge(taken, 2 * t + 1)
                for k in range(2):
                    mm = nc.tensor.transpose(p_ps[:, k, :], p_rows[u][:, k, :], const.ident)
                mm.then_inc(turned, 1)
                pe.wait_ge(b_done, t + 1)
                for k in range(KC):
                    mm = nc.tensor.transpose(turn_ps[:, k * P:(k + 1) * P], b[:, k * P:(k + 1) * P], const.ident)
                mm.then_inc(turned, 1)
                pe.wait_ge(taken, 2 * t + 2)
                pe.wait_ge(ple_w_in, 16)
                pe.wait_ge(mixed, t + 1)
                for n in range(2):
                    for k in range(2):
                        mm = nc.tensor.matmul(ple_ps[:, n * W:(n + 1) * W], pT[:, k, :], w_ple[:, k, n * W:(n + 1) * W],
                                              start=(k == 0), stop=(k == 1))
                mm.then_inc(ple_summed, 1)
                pe.wait_ge(taken, 2 * t + 3)
                pe.wait_ge(gate_w_in, 16)
                pe.wait_ge(gate_done, t + 1)
                for n in range(2):
                    for k in range(KC):
                        mm = nc.tensor.matmul(gate_ps[:, n * W:(n + 1) * W], bT[:, k, :], w_gate[:, k, n * W:(n + 1) * W],
                                              start=(k == 0), stop=(k == KC - 1))
                mm.then_inc(gate_summed, 1)
            tiles(pe, tile)

        @block.scalar
        def _(act):
            prime(act, taken, gate_done)

            def tile(t, u, r):
                act.wait_ge(turned, 2 * t + 3)
                act.wait_ge(gate_summed, t + 1)
                nc.scalar.copy(pT[:, :, :], p_ps[:, :, :]).then_inc(taken, 1)
                act.wait_ge(turned, 2 * t + 4)
                nc.scalar.copy(bT[:, :, :].rearrange("p k n -> p (k n)"), turn_ps[:, :]).then_inc(taken, 1)
                act.wait_ge(gate_summed, t + 2)
                act.wait_ge(mixed, t + 1)
                nc.scalar.activation(gate[:, :], gate_ps[:, :], ACT.Sigmoid).then_inc(gate_done, 1)
            tiles(act, tile)

        @block.vector
        def _(dve):
            prime(dve, mixed, y_done)
            dve.wait_ge(tables_in, 32)

            def norm(n, u, dst, done, count, free=None):
                nc.vector.tensor_tensor_reduce(squares[:, :], h[u][:, :], h[u][:, :], 1.0, 0.0, ALU.mult, ALU.add,
                                               stat[:, n, 0:1]).then_inc(squared, 1)
                dve.wait_ge(squared, count)
                nc.vector.tensor_scalar(stat[:, n, 1:2], stat[:, n, 0:1], 1.0 / D, EPS,
                                        ALU.mult, ALU.add).then_inc(mean_done, 1)
                dve.wait_ge(rstd_done, count)
                if free:
                    dve.wait_ge(*free)
                nc.vector.scalar_tensor_tensor(dst, h[u][:, :], stat[:, n, 2:3], gains[:, n, :],
                                               ALU.mult, ALU.mult).then_inc(done, 1)

            def close(t, u, count):
                dve.wait_ge(gate_done, t + 2)
                dve.wait_ge(ple_summed, t + 1)
                nc.vector.tensor_tensor(squares[:, :], gate[:, :], ple_ps[:, :], ALU.mult).then_inc(mixed, 1)
                dve.wait_ge(mixed, t + 2)
                nc.vector.tensor_tensor(h[u][:, :], h[u][:, :], squares[:, :], ALU.add).then_inc(added, 1)
                dve.wait_ge(added, t + 1)
                norm(1, u, y_sb[:, :], y_done, count, (y_free, t + 1))

            dve.wait_ge(tile_in[0], 32)
            norm(0, 0, b[:, :], b_done, 1)
            with dve.Fori(0, TP // 2) as r:
                for u in (1, 2):
                    t = 2 * r + u
                    wait_apart(dve, const, tile_in[u % 2], 32 * r + 32 * u)
                    dve.wait_ge(turned, 2 * t + 2)
                    norm(0, u % 2, b[:, :], b_done, 2 * t)
                    close(t - 1, 1 - u % 2, 2 * t + 1)
            close(TP, 0, 2 * T)


def shape_constants():
    import numpy as np

    pos = np.concatenate([np.arange(TP * P), np.tile(256 + np.arange(16), 8)]).astype(np.float32)
    inv = np.float32(10000.0) ** (-np.arange(0, 32, 2, dtype=np.float32) / np.float32(32))
    ang = pos[:, None] * inv[None, :].astype(np.float32)
    cos, sin = np.cos(ang), np.sin(ang)
    q, k = np.arange(P)[:, None], np.arange(P)[None, :]
    at, chunk, head = np.arange(P)[:, None, None], np.arange(4)[None, :, None], np.arange(8)[None, None, :]
    own_head = head == 2 * chunk + at // 64
    own_half = np.stack([own_head & (at % 64 < 32), own_head & (at % 64 >= 32), own_head], axis=1)
    return {
        "rope": np.concatenate([cos, cos, -sin, sin], axis=1).astype(np.float32),
        "steps16": np.tile(np.arange(16, dtype=np.float32), (P, 1)),
        "identity": np.eye(P, dtype=np.float32),
        "chunk_mask": np.where(k // 64 > q // 64, HIDDEN, 0).astype(np.float32),
        "strict_mask": np.where(k >= q, HIDDEN, 0).astype(np.float32),
        "half_mask": own_half.astype(np.float32).reshape(P, -1),
        "head_mask": (q // 16 == np.arange(W)[None, :] // 64).astype(np.float32),
        "fold": (q % 16 == np.arange(16)[None, :]).astype(np.float32),
        "late_mask": np.where(np.arange(16)[None, :] >= q % 16, HIDDEN, 0).astype(np.float32),
    }


HIDDEN = -1e30
LAMBDA_START = 0.8 - 0.6


class Const:
    pass


def load_constants(nc, ctx, ins):
    c = Const()
    c.ident = ctx.enter_context(nc.sbuf_tensor("ident", [P, P], F32))[:, :]
    c.chunk_mask = ctx.enter_context(nc.sbuf_tensor("chunk_mask", [P, P], F32))[:, :]
    c.strict_mask = ctx.enter_context(nc.sbuf_tensor("strict_mask", [P, P], F32))[:, :]
    c.one = ctx.enter_context(nc.sbuf_tensor("one", [P, 1], F32))[:, :]
    c.lam = ctx.enter_context(nc.sbuf_tensor("lam", [P, 1], F32))[:, :]
    vectors = ctx.enter_context(nc.sbuf_tensor("lambda_vectors", [P, 2, 64], F32))
    sums = ctx.enter_context(nc.sbuf_tensor("lambda_sums", [P, 2], F32))
    raised = ctx.enter_context(nc.semaphore("lambda_raised"))
    c.minus_half = ctx.enter_context(nc.sbuf_tensor("minus_half", [P, 1], F32))[:, :]
    loaded = ctx.enter_context(nc.semaphore("shared_loaded"))
    filled = ctx.enter_context(nc.semaphore("shared_filled"))
    c.passed = {e.engine: ctx.enter_context(nc.semaphore(f"passed{n}"))
                for n, e in enumerate((nc.vector, nc.gpsimd))}
    with nc.Block() as block:
        @block.sync
        def _(sp):
            for dst, name in ((c.ident, "identity"), (c.chunk_mask, "chunk_mask"), (c.strict_mask, "strict_mask")):
                sp.dma_start(dst, ins[name]).then_inc(loaded, 16)
            sp.dma_start(vectors[:, :, :].rearrange("p a d -> p (a d)"),
                         bass.AP(ins["lambdas"].tensor, 0, [[0, P], [1, P]])).then_inc(loaded, 16)

        @block.vector
        def _(dve):
            nc.vector.memset(c.minus_half, -0.5)
            nc.vector.memset(c.one, 1.0)
            dve.wait_ge(loaded, 64)
            nc.vector.tensor_tensor(vectors[:, 0, :], vectors[:, 0, :], vectors[:, 1, :], ALU.mult).then_inc(filled, 1)
            dve.wait_ge(filled, 1)
            nc.vector.tensor_reduce(sums[:, :], vectors[:, 0, :].rearrange("p (a d) -> p a d", a=2), AX.X,
                                    ALU.add).then_inc(filled, 1)
            dve.wait_ge(raised, 1)
            nc.vector.scalar_tensor_tensor(c.lam, sums[:, 0:1], LAMBDA_START, sums[:, 1:2], ALU.add,
                                           ALU.subtract).then_inc(filled, 1)
            dve.wait_ge(filled, 3)

        @block.scalar
        def _(act):
            act.wait_ge(filled, 2)
            nc.scalar.activation(sums[:, :], sums[:, :], ACT.Exp).then_inc(raised, 1)
    return c


def build(nc, ins, outs):
    with ExitStack() as ctx:
        const = load_constants(nc, ctx, ins)
        qk_turned = nc.dram_tensor("qk_turned", (4, T, P, W), F32, kind="Internal").ap()
        new_rows = {KD: outs["new_dk"], VD: outs["new_dv"], KS: outs["new_sk"], VS: outs["new_sv"]}
        project_inputs(nc, const, ins["x_all"], ins["g_mix"], ins["w_in"], ins["rope"], new_rows, qk_turned)
        heads = nc.dram_tensor("heads", (T, P, D), F32, kind="Internal").ap()
        attend_prompt(nc, const, qk_turned, new_rows, heads)
        attend_samples(nc, const, ins, qk_turned, new_rows, heads)
        summed = nc.dram_tensor("summed", (T, P, D), F32, kind="Internal").ap()
        route_and_sum_experts(nc, const, ins, heads, summed)
        finish(nc, const, ins, summed, outs["y"])


def kernel(**inputs):
    import numpy as _np
    import concourse.bacc as _bacc
    from concourse import mybir as _mybir
    from concourse.bass_utils import run_bass_kernel_spmd as _run

    def rows(*names):
        return _np.concatenate([_np.asarray(inputs[n]).reshape(-1, inputs[n].shape[-1]) for n in names])

    arrays = {
        "x_all": rows("x_prompt", "x_sample"),
        "p_all": rows("p_prompt", "p_sample"),
        "lambdas": _np.concatenate([_np.asarray(inputs[n]) for n in
                                    ("lambda_q1", "lambda_q2", "lambda_k1", "lambda_k2")]),
        **shape_constants(),
    }
    for n in ("cache_diff_k", "cache_diff_v", "cache_sb_k", "cache_sb_v"):
        arrays[n] = _np.asarray(inputs[n]).reshape(8, 256, W)
    for n in ("w_in", "w_out", "w_query", "w_pgate", "w_ple", "sub_keys", "expert_u", "expert_v"):
        arrays[n] = _np.asarray(inputs[n])[0]
    for n in ("g_mix", "g_subln", "g_ffn", "g_ple", "g_final"):
        arrays[n] = _np.asarray(inputs[n]).reshape(1, -1)
    arrays = {f"{n}_in": _np.ascontiguousarray(a) for n, a in arrays.items()}

    nc = _bacc.Bacc("TRN2", target_bir_lowering=False, num_devices=1)
    ins = {n[:-3]: nc.dram_tensor(n, a.shape, _mybir.dt.from_np(a.dtype), kind="ExternalInput").ap()
           for n, a in arrays.items()}
    outs = {n: nc.dram_tensor(n, (T * P, D if n == "y" else W), _mybir.dt.float32, kind="ExternalOutput").ap()
            for n in ("y", "new_dk", "new_dv", "new_sk", "new_sv")}
    build(nc, ins, outs)
    r = _run(nc, [arrays], core_ids=[0]).results[0]
    prompt = TP * P
    got = [r["y"][:prompt].reshape(1, prompt, D), r["y"][prompt:].reshape(8, 16, D)]
    for rows_of, shape in ((slice(0, prompt), (1, 1, prompt, 8, 64)), (slice(prompt, None), (1, 8, 16, 8, 64))):
        got += [r[n][rows_of].reshape(shape) for n in ("new_dk", "new_dv", "new_sk", "new_sv")]
    return tuple(got)
```

```python
from contextlib import ExitStack

import concourse.bass as bass
from concourse import mybir

F32 = mybir.dt.float32
U32 = mybir.dt.uint32
ALU = mybir.AluOpType
ACT = mybir.ActivationFunctionType
AX = mybir.AxisListType

P = 128
D = 1024
KC = D // P
W = 512
TP = 8
T = TP + 1
EPS = 1e-6
QD, KD, VD, QS, KS, VS = range(6)
TURNED = {QD: 0, KD: 1, QS: 2, KS: 3}


def stage_semaphores(nc, ctx):
    taken = []

    def clear():
        nc.clear_and_free_semaphores(taken)
        nc.all_engine_barrier()

    def sem(name):
        taken.append(nc.alloc_semaphore(name))
        return taken[-1]

    ctx.callback(clear)
    return sem


def prime(eng, *sems, by=1):
    for s in sems:
        eng.sem_inc(s, by)


def wait_apart(eng, const, sem, value):
    eng.wait_ge(sem, value)
    eng.sem_inc(const.passed[eng.engine], 1)


def project_inputs(nc, const, x_all, g_mix, w_in, rope, new_rows, qk_turned):
    with ExitStack() as ctx:
        def sb(name, shape, dt=F32):
            return ctx.enter_context(nc.sbuf_tensor(name, shape, dt))

        sem = stage_semaphores(nc, ctx)

        weights = sb("weights", [P, KC, 6 * W])
        x = sb("x", [P, D])
        squares = sb("squares", [P, D])
        a = sb("a", [P, D])
        aT = sb("aT", [P, KC, P])
        gain = sb("gain", [P, D])
        rope_tab = sb("rope_tab", [P, T, 64])
        rows = sb("rows", [P, 6, W])
        turned = sb("turned", [P, 4, W])
        rot = sb("rot", [P, 2, W])
        stat = sb("stat", [P, 4])
        turn_ps = ctx.enter_context(nc.psum_tensor("turn_ps", [P, D], F32))
        proj_ps = ctx.enter_context(nc.psum_tensor("proj_ps", [P, 3, W], F32))
        kind_ps = ctx.enter_context(nc.psum_tensor("kind_ps", [P, 2, W], F32))

        consts_in = sem("consts_in")
        w_in_sem = [sem(f"w_landed{g}") for g in range(6)]
        x_in = sem("x_in")
        sum_done = sem("sum_done")
        mean_done = sem("mean_done")
        rstd_done = sem("rstd_done")
        a_done = sem("a_done")
        turn_done = sem("turn_done")
        aT_done = sem("aT_done")
        proj_done = sem("proj_done")
        rot_done = sem("rot_done")
        rows_done = [sem(f"rows_done{k}") for k in range(6)]
        rows_turned = [sem(f"rows_turned{k}") for k in range(4)]
        turned_done = [sem(f"turned_done{k}") for k in range(4)]
        rows_out = [sem(f"rows_out{k}") for k in range(6)]
        turned_out = [sem(f"turned_out{k}") for k in range(4)]
        tile_stored = sem("tile_stored")
        block = ctx.enter_context(nc.Block())

        @block.sync
        def _(sp):
            sp.dma_start(gain[:, :], bass.AP(g_mix.tensor, 0, [[0, P], [1, D]])).then_inc(consts_in, 16)
            sp.dma_start(rope_tab[:, :, :], rope.rearrange("(t p) c -> p t c", p=P)).then_inc(consts_in, 16)
            for g in range(6):
                sp.dma_start(weights[:, :, g * W:(g + 1) * W],
                             w_in[:, g * W:(g + 1) * W].rearrange("(k p) n -> p k n", p=P)).then_inc(w_in_sem[g], 16)
            prime(sp, tile_stored)
            with sp.Fori(0, T) as t:
                for k in (KD, VD, KS, VS):
                    sp.wait_ge(rows_done[k], t + 2)
                    sp.dma_start(new_rows[k][bass.ds(t * P, P), :], rows[:, k, :]).then_inc(rows_out[k], 16)
                for k in (QD, KD, QS, KS):
                    n = TURNED[k]
                    sp.wait_ge(turned_done[n], t + 2)
                    sp.dma_start(qk_turned[n, bass.ds(t, 1), :, :].rearrange("a p n -> p (a n)"),
                                 turned[:, n, :]).then_inc(turned_out[n], 16)
                for k in (KD, VD, KS, VS):
                    sp.wait_ge(rows_out[k], t * 16 + 16)
                for n in range(4):
                    sp.wait_ge(turned_out[n], t * 16 + 16)
                sp.sem_inc(tile_stored, 1)

        @block.gpsimd
        def _(pool):
            with pool.Fori(0, T) as t:
                pool.wait_ge(a_done, t + 1)
                pool.dma_start(x[:, :], x_all[bass.ds(t * P, P), :]).then_inc(x_in, 16)
                pool.wait_ge(mean_done, t + 1)
                nc.gpsimd.tensor_tensor(stat[:, 2:3], stat[:, 1:2], const.minus_half, ALU.pow).then_inc(rstd_done, 1)

        @block.tensor
        def _(pe):
            prime(pe, turn_done, *rows_turned)
            with pe.Fori(0, T) as t:
                pe.wait_ge(a_done, t + 2)
                for k in range(KC):
                    last = nc.tensor.transpose(turn_ps[:, k * P:(k + 1) * P], a[:, k * P:(k + 1) * P], const.ident)
                last.then_inc(turn_done, 1)
                pe.wait_ge(aT_done, t + 1)

                def project(g):
                    pe.wait_ge(w_in_sem[g], 16)
                    pe.wait_ge(rows_done[(g + 3) % 6], t + 1 + g // 3)
                    for k in range(KC):
                        mm = nc.tensor.matmul(proj_ps[:, g % 3, :], aT[:, k, :], weights[:, k, g * W:(g + 1) * W],
                                              start=(k == 0), stop=(k == KC - 1))
                    mm.then_inc(proj_done, 1)

                def turn(kind):
                    n = TURNED[kind]
                    pe.wait_ge(rows_done[kind], t + 2)
                    pe.wait_ge(turned_done[(n + 2) % 4], t + 1 + n // 2)
                    for c in range(4):
                        mm = nc.tensor.transpose(kind_ps[:, n % 2, c * P:(c + 1) * P],
                                                 rows[:, kind, c * P:(c + 1) * P], const.ident)
                    mm.then_inc(rows_turned[n], 1)

                project(QD)
                project(KD)
                project(VD)
                turn(QD)
                project(QS)
                turn(KD)
                project(KS)
                project(VS)
                turn(QS)
                turn(KS)

        @block.scalar
        def _(act):
            prime(act, *(rows_done[g] for g in (VD, QS, KS, VS)), turned_done[2], turned_done[3])
            with act.Fori(0, T) as t:
                act.wait_ge(turn_done, t + 2)
                nc.scalar.copy(aT[:, :, :].rearrange("p k n -> p (k n)"), turn_ps[:, :]).then_inc(aT_done, 1)
                for g in (VD, QS, KS, VS):
                    act.wait_ge(proj_done, t * 6 + (g + 1))
                    if g != QS:
                        act.wait_ge(tile_stored, t + 1)
                    if g in TURNED:
                        act.wait_ge(rows_turned[TURNED[g]], t + 1)
                    nc.scalar.mul(rows[:, g, :], proj_ps[:, g % 3, :],
                                  0.125 if g == QS else 1.0).then_inc(rows_done[g], 1)
                for n in (2, 3):
                    act.wait_ge(rows_turned[n], t + 2)
                    act.wait_ge(tile_stored, t + 1)
                    nc.scalar.copy(turned[:, n, :], kind_ps[:, n % 2, :]).then_inc(turned_done[n], 1)

        @block.vector
        def _(dve):
            prime(dve, a_done, rows_done[QD], rows_done[KD], turned_done[0], turned_done[1])
            with dve.Fori(0, T) as t:
                dve.wait_ge(x_in, t * 16 + 16)
                nc.vector.tensor_tensor_reduce(squares[:, :], x[:, :], x[:, :], 1.0, 0.0, ALU.mult, ALU.add,
                                               stat[:, 0:1]).then_inc(sum_done, 1)
                dve.wait_ge(sum_done, t + 1)
                nc.vector.tensor_scalar(stat[:, 1:2], stat[:, 0:1], 1.0 / D, EPS, ALU.mult, ALU.add).then_inc(mean_done, 1)
                dve.wait_ge(rstd_done, t + 1)
                dve.wait_ge(consts_in, 32)
                dve.wait_ge(turn_done, t + 1)
                nc.vector.scalar_tensor_tensor(a[:, :], x[:, :], stat[:, 2:3], gain[:, :],
                                               ALU.mult, ALU.mult).then_inc(a_done, 1)
                for g in (QD, KD):
                    dve.wait_ge(proj_done, t * 6 + (g + 1))
                    src = proj_ps[:, g % 3, :].rearrange("p (h c d) -> p h c d", c=2, d=16)
                    out = rot[:, 1, :].rearrange("p (h c d) -> p h c d", c=2, d=16)
                    both = rot[:, 0, :].rearrange("p (h d) -> p h d", d=32)
                    cos = rope_tab[:, bass.ds(t, 1), 0:32].broadcast_to((P, 16, 32))
                    nc.vector.tensor_tensor(both, proj_ps[:, g % 3, :].rearrange("p (h d) -> p h d", d=32), cos,
                                            ALU.mult)
                    for c in range(2):
                        sin = rope_tab[:, bass.ds(t, 1), 32 + 16 * c:48 + 16 * c].broadcast_to((P, 16, 16))
                        mm = nc.vector.tensor_tensor(out[:, :, c, :], src[:, :, 1 - c, :], sin, ALU.mult)
                    mm.then_inc(rot_done, 1)
                    dve.wait_ge(rot_done, t * 2 + (g + 1))
                    if g == KD:
                        dve.wait_ge(tile_stored, t + 1)
                    dve.wait_ge(rows_turned[g], t + 1)
                    nc.vector.tensor_tensor(rows[:, g, :], rot[:, 0, :], rot[:, 1, :], ALU.add).then_inc(rows_done[g], 1)
                    dve.wait_ge(rows_done[g], t + 2)
                for n in (0, 1):
                    dve.wait_ge(rows_turned[n], t + 2)
                    dve.wait_ge(tile_stored, t + 1)
                    nc.vector.tensor_scalar(turned[:, n, :], kind_ps[:, n % 2, :], 32 ** -0.5 if n == 0 else 1.0,
                                            None, ALU.mult).then_inc(turned_done[n], 1)


def attend_samples(nc, const, ins, qk_turned, new_rows, heads):
    B, S, PAST = 8, 16, 256
    KEYS = PAST + S
    with ExitStack() as ctx:
        def sb(name, shape, dt=F32):
            return ctx.enter_context(nc.sbuf_tensor(name, shape, dt))

        sem = stage_semaphores(nc, ctx)

        cached = sb("cached", [P, 2, 2, 2, W])
        values = sb("values", [P, 2, 2, 3, W])
        qT = sb("qT", [P, 2, 4, P])
        newT = sb("newT", [P, 2, 4, P])
        kT = sb("kT", [P, 2, 4, KEYS])
        queries = sb("queries", [P, 3, 4, P])
        half_mask = sb("half_mask", [P, 3, 4, 8])
        head_mask = sb("head_mask", [P, W])
        fold = sb("fold", [P, S])
        late_mask = sb("late_mask", [P, S])
        prob = sb("sprob", [P, 2, KEYS])
        soft = sb("ssoft", [P, KEYS])
        stick = sb("sstick", [P, KEYS])
        zeros = sb("szeros", [P, KEYS])
        wT = sb("swT", [P, 2, 3 * P])
        own = sb("own", [P, 2, W])
        neg_max = sb("sneg_max", [P, 2])
        total = sb("stotal", [P, 2])
        share = sb("sshare", [P, 2])
        out_rows = sb("out_rows", [S, 2, D])
        k_ps = ctx.enter_context(nc.psum_tensor("k_ps", [P, 2, W], F32))
        score_ps = ctx.enter_context(nc.psum_tensor("sscore_ps", [P, 3, W], F32))
        turn_ps = ctx.enter_context(nc.psum_tensor("sturn_ps", [P, W], F32))
        mix_ps = ctx.enter_context(nc.psum_tensor("mix_ps", [P, W], F32))
        fold_ps = ctx.enter_context(nc.psum_tensor("fold_ps", [P, W], F32))

        tables_in = sem("tables_in")
        batch_in = [sem(f"batch_in{u}") for u in range(2)]
        zeroed = sem("zeroed")
        k_turned = sem("k_turned")
        k_taken = sem("k_taken")
        new_taken = sem("new_taken")
        queries_done = sem("queries_done")
        scores_done = sem("sscores_done")
        max_done = sem("smax_done")
        prob_done = sem("sprob_done")
        share_done = sem("sshare_done")
        part_done = sem("spart_done")
        weights_done = sem("sweights_done")
        abs_done = sem("sabs_done")
        exp_done = sem("sexp_done")
        log_done = sem("slog_done")
        soft_done = sem("ssoft_done")
        scan_done = sem("sscan_done")
        expo_done = sem("sexpo_done")
        stick_done = sem("sstick_done")
        w_turned = sem("sw_turned")
        wT_done = sem("swT_done")
        mixed = sem("mixed")
        own_done = sem("own_done")
        folded = sem("folded")
        taken = sem("taken")
        stored = [sem(f"sstored{u}") for u in range(2)]
        stored_free = sem("stored_free")
        block = ctx.enter_context(nc.Block())

        def batches(eng, body):
            with eng.Fori(0, B // 2) as r:
                for u in range(2):
                    body(r, u, 2 * r + u)

        @block.sync
        def _(sp):
            for a, name in ((half_mask[:, :, :, :].rearrange("p a c h -> p (a c h)"), "half_mask"),
                            (head_mask[:, :], "head_mask"), (fold[:, :], "fold"), (late_mask[:, :], "late_mask")):
                sp.dma_start(a, ins[name]).then_inc(tables_in, 16)
            for kind in range(2):
                for dst, place in ((qT, 2 * kind), (newT, 2 * kind + 1)):
                    sp.dma_start(dst[:, kind, :, :].rearrange("p c n -> p (c n)"),
                                 qk_turned[place, TP, :, :]).then_inc(tables_in, 16)

            def load(r, u, b):
                sp.wait_ge(mixed, 2 * b + 2)
                for kind, (k, v, rows) in enumerate((("cache_diff_k", "cache_diff_v", VD), ("cache_sb_k", "cache_sb_v", VS))):
                    for dst, name in ((cached[:, u, kind, :, :], k), (values[:, u, kind, 0:2, :], v)):
                        sp.dma_start(dst, ins[name][bass.ds(b, 1), :, :]
                                     .rearrange("a (j p) n -> p (a j) n", p=P)).then_inc(batch_in[u], 16)
                    sp.dma_start(values[0:S, u, kind, 2, :],
                                 new_rows[rows][bass.ds(TP * P + b * S, S), :]).then_inc(batch_in[u], 16)
            batches(sp, load)

        @block.gpsimd
        def _(pool):
            prime(pool, stored_free, by=1)

            def store(r, u, b):
                pool.wait_ge(taken, 2 * b + 6)
                pool.dma_start(heads[bass.ds(b * S, S), :], out_rows[:, u, :]).then_inc(stored[u], 16)
                pool.wait_ge(stored[u], 16 * r + 16)
                pool.sem_inc(stored_free, 1)
            batches(pool, store)
            for u in range(2):
                pool.wait_ge(stored[u], 16 * (B // 2))

        @block.tensor
        def _(pe):
            prime(pe, mixed, by=4)
            prime(pe, scores_done, by=3)
            prime(pe, w_turned, by=2)
            prime(pe, folded, by=2)

            def batch(r, u, b):
                pe.wait_ge(batch_in[u], 96 * r + 96)
                for kind in range(2):
                    for blk in range(2):
                        m = 2 * kind + blk
                        pe.wait_ge(k_taken, 4 * b + m + 1)
                        for c in range(4):
                            mm = nc.tensor.transpose(k_ps[:, m % 2, c * P:(c + 1) * P],
                                                     cached[:, u, kind, blk, c * P:(c + 1) * P], const.ident)
                        mm.then_inc(k_turned, 1)
                for j in range(3):
                    kind = j // 2
                    pe.wait_ge(k_taken, 4 * b + 2 * kind + 4)
                    pe.wait_ge(new_taken, 2 * b + kind + 1)
                    pe.wait_ge(queries_done, 3 * b + j + 1)
                    if j < 2:
                        pe.wait_ge(prob_done, 2 * b + j + 1)
                    else:
                        pe.wait_ge(expo_done, b + 1)
                    for c in range(4):
                        mm = nc.tensor.matmul(score_ps[:, j, 0:KEYS], queries[:, j, c, :], kT[:, kind, c, :],
                                              start=(c == 0), stop=(c == 3 and j < 2))
                    if j == 2:
                        mm = nc.tensor.matmul(score_ps[:, j, PAST:KEYS], const.ident, late_mask[:, :],
                                              start=False, stop=True)
                    mm.then_inc(scores_done, 1)
                for kind, w, ready in ((0, prob[:, 0, :], weights_done), (1, stick[:, :], stick_done)):
                    pe.wait_ge(ready, b + 1)
                    pe.wait_ge(wT_done, 4 * b + 2 * kind + 1)
                    for k in range(3):
                        n = min(P, KEYS - k * P)
                        mm = nc.tensor.transpose(turn_ps[0:n, k * P:(k + 1) * P], w[:, k * P:k * P + n], const.ident)
                    mm.then_inc(w_turned, 1)
                    pe.wait_ge(wT_done, 4 * b + 2 * kind + 3)
                    pe.wait_ge(own_done, 2 * b + kind + 1)
                    for k in range(3):
                        n = min(P, KEYS - k * P)
                        mm = nc.tensor.matmul(mix_ps[:, :], wT[0:n, kind, k * P:(k + 1) * P],
                                              values[0:n, u, kind, k, :], start=(k == 0), stop=(k == 2))
                    mm.then_inc(mixed, 1)
                    pe.wait_ge(own_done, 2 * b + kind + 2)
                    pe.wait_ge(taken, 2 * b + kind + 4)
                    nc.tensor.matmul(fold_ps[0:S, :], fold[:, :], own[:, kind, :],
                                     start=True, stop=True).then_inc(folded, 1)
            batches(pe, batch)

        @block.scalar
        def _(act):
            prime(act, prob_done, by=2)
            prime(act, k_taken, by=2)
            prime(act, wT_done, by=1)
            prime(act, taken, by=4)

            def batch(r, u, b):
                for m in range(4):
                    act.wait_ge(k_turned, 4 * b + m + 1)
                    act.wait_ge(scores_done, 3 * b + 3)
                    nc.scalar.copy(kT[:, m // 2, :, (m % 2) * P:(m % 2 + 1) * P],
                                   k_ps[:, m % 2, :].rearrange("p (c n) -> p c n", n=P)).then_inc(k_taken, 1)
                for c in range(2):
                    act.wait_ge(max_done, 2 * b + c + 1)
                    act.wait_ge(w_turned, 2 * b + 1)
                    nc.scalar.activation(prob[:, c, :], score_ps[:, c, 0:KEYS], ACT.Exp, bias=neg_max[:, c:c + 1],
                                         accum_out=total[:, c:c + 1]).then_inc(prob_done, 1)
                act.wait_ge(scores_done, 3 * b + 6)
                act.wait_ge(scan_done, b + 1)
                nc.scalar.activation(soft[:, :], score_ps[:, 2, 0:KEYS], ACT.Abs).then_inc(abs_done, 1)
                act.wait_ge(abs_done, b + 1)
                nc.scalar.activation(soft[:, :], soft[:, :], ACT.Exp, scale=-1.0).then_inc(exp_done, 1)
                act.wait_ge(exp_done, b + 1)
                nc.scalar.activation(soft[:, :], soft[:, :], ACT.Ln, bias=const.one).then_inc(log_done, 1)
                for kind in range(2):
                    if kind == 1:
                        act.wait_ge(expo_done, b + 2)
                        nc.scalar.activation(stick[:, :], stick[:, :], ACT.Exp).then_inc(stick_done, 1)
                    act.wait_ge(w_turned, 2 * b + kind + 3)
                    act.wait_ge(mixed, 2 * b + kind + 3)
                    nc.scalar.copy(wT[:, kind, 0:2 * P], turn_ps[:, 0:2 * P]).then_inc(wT_done, 1)
                    nc.scalar.copy(wT[0:S, kind, 2 * P:3 * P], turn_ps[0:S, 2 * P:3 * P]).then_inc(wT_done, 1)
                    act.wait_ge(folded, 2 * b + kind + 3)
                    act.wait_ge(stored_free, b + 1)
                    nc.scalar.copy(out_rows[:, u, kind * W:(kind + 1) * W], fold_ps[0:S, :]).then_inc(taken, 1)
            batches(act, batch)

        @block.vector
        def _(dve):
            prime(dve, expo_done, scan_done, own_done)
            nc.vector.memset(zeros[:, :], 0.0).then_inc(zeroed, 1)
            dve.wait_ge(zeroed, 1)
            dve.wait_ge(tables_in, 8 * 16)

            def batch(r, u, b):
                at = bass.ds(b * S, S)
                dve.wait_ge(scores_done, 3 * b + 3)
                for kind in range(2):
                    nc.vector.tensor_copy(kT[:, kind, :, PAST:KEYS], newT[:, kind, :, at]).then_inc(new_taken, 1)
                for j in range(3):
                    nc.vector.tensor_tensor(
                        queries[:, j, :, :].rearrange("p c (h q) -> p c h q", q=S),
                        qT[:, j // 2, :, at].unsqueeze(2).broadcast_to((P, 4, 8, S)),
                        half_mask[:, j, :, :].unsqueeze(3).broadcast_to((P, 4, 8, S)), ALU.mult).then_inc(queries_done, 1)
                for c in range(2):
                    dve.wait_ge(scores_done, 3 * b + c + 4)
                    nc.vector.tensor_reduce(neg_max[:, c:c + 1], score_ps[:, c, 0:KEYS], AX.X, ALU.max,
                                            negate=True).then_inc(max_done, 1)
                dve.wait_ge(prob_done, 2 * b + 4)
                nc.vector.reciprocal(share[:, :], total[:, :]).then_inc(share_done, 1)
                dve.wait_ge(share_done, b + 1)
                nc.vector.tensor_scalar(prob[:, 1, :], prob[:, 1, :], share[:, 1:2], const.lam,
                                        ALU.mult, ALU.mult).then_inc(part_done, 1)
                dve.wait_ge(part_done, b + 1)
                nc.vector.scalar_tensor_tensor(prob[:, 0, :], prob[:, 0, :], share[:, 0:1], prob[:, 1, :],
                                               ALU.mult, ALU.subtract).then_inc(weights_done, 1)
                z = score_ps[:, 2, 0:KEYS]
                dve.wait_ge(log_done, b + 1)
                nc.vector.scalar_tensor_tensor(soft[:, :], z, 0.0, soft[:, :], ALU.max, ALU.add).then_inc(soft_done, 1)
                dve.wait_ge(soft_done, b + 1)
                dve.wait_ge(w_turned, 2 * b + 2)
                nc.vector.tensor_tensor_scan(stick[:, ::-1], soft[:, ::-1], zeros[:, :], 0.0,
                                             ALU.add, ALU.add).then_inc(scan_done, 1)
                dve.wait_ge(scan_done, b + 2)
                nc.vector.tensor_tensor(stick[:, :], z, stick[:, :], ALU.subtract).then_inc(expo_done, 1)
                for kind in range(2):
                    dve.wait_ge(mixed, 2 * b + kind + 5)
                    dve.wait_ge(folded, 2 * b + kind + 1)
                    nc.vector.tensor_tensor(own[:, kind, :], mix_ps[:, :], head_mask[:, :], ALU.mult).then_inc(own_done, 1)
            batches(dve, batch)


HEADS, TOP, SIDE = 8, 16, 128
ROWS = HEADS * TOP
U_RING, V_RING, DIAGS = 4, 8, 4
V_AHEAD = V_RING + TOP


def tile_at(position):
    return TP if position == 0 else position - 1


def attend_and_sum_experts(nc, const, ins, qk_turned, new_rows, heads, summed):
    with ExitStack() as ctx:
        def sb(name, shape, dt=F32):
            return ctx.enter_context(nc.sbuf_tensor(name, shape, dt))

        def psum(name, shape):
            return ctx.enter_context(nc.psum_tensor(name, shape, F32))

        sem = stage_semaphores(nc, ctx)

        w_out = sb("w_out_sb", [P, KC, D])
        w_query = sb("w_query_sb", [P, KC, 2 * D])
        u_rows = [sb(f"u_rows{n}", [P, D]) for n in range(U_RING)]
        v_rows = [sb(f"v_rows{n}", [P, D]) for n in range(V_RING)]
        c_rows = sb("c_rows", [P, D])
        idx_now = sb("idx_now", [P, 2, TOP], U32)
        dots = sb("dots", [P, 2, TOP])
        gelus = sb("gelus", [P, 2, TOP])
        coef = sb("coef", [P, 2, TOP])
        diag = sb("diag", [P, DIAGS, P])
        keysT = sb("keysT", [P, 2, P])
        gain = sb("ffn_gain", [P, D])
        sub_gain = sb("sub_gain", [P, 64])
        steps16 = sb("steps16", [P, TOP])
        x = sb("rx", [P, D])
        mix = sb("mix", [P, D])
        qd = sb("qd", [P, 4, P])
        qs = sb("qs", [P, 2, P])
        neg_max = sb("neg_max", [P, 4])
        total = sb("total", [P, 4])
        share = sb("share", [P, 4])
        arena = sb("arena", [P, 9, D])

        def place(n, size=D, at=0):
            return arena[:, n:n + -(-(at + size) // D), :].rearrange("p a n -> p (a n)")[:, at:at + size]

        kd, ks, vd, vs = (place(n).rearrange("p (j k) -> p j k", k=P) for n in range(4))
        prob = [place(4 + n) for n in range(4)]
        soft = (prob[1], prob[0])
        stick = (prob[3], prob[2])
        wT = place(8)

        c = place(0)
        query = place(1).rearrange("p (a n) -> p a n", n=W)
        scores = place(2, 2 * D).rearrange("p (m n) -> p m n", n=SIDE)
        spare = place(4, 2 * D).rearrange("p (m n) -> p m n", n=SIDE)
        work = place(4)
        inT = place(6).rearrange("p (k n) -> p k n", n=P)
        keys = inT[:, 0:2, :]
        top, pos, posf, picked_at = (place(7, 2 * ROWS, at=2 * ROWS * n) for n in range(4))
        top = top.rearrange("p (m a) -> p m a", a=TOP)
        pos = pos.bitcast(U32).rearrange("p (m a) -> p m a", a=TOP)
        posf = posf.rearrange("p (m a) -> p m a", a=TOP)
        picked = picked_at.rearrange("p (s h k) -> p s h k", s=2, k=TOP)
        val = place(6, ROWS).rearrange("p (h k) -> p h k", k=TOP)
        sel = place(6, ROWS, at=ROWS).bitcast(U32).rearrange("p (h k) -> p h k", k=TOP)
        part = place(6, 2 * ROWS, at=2 * ROWS).bitcast(U32).rearrange("p (s h k) -> p s h k", s=2, k=TOP)
        partf = place(6, 2 * ROWS, at=4 * ROWS).rearrange("p (s h k) -> p s h k", s=2, k=TOP)
        expo = place(6, ROWS, at=6 * ROWS).rearrange("p (h k) -> p h k", k=TOP)
        queryT = place(8).rearrange("p (a n) -> p a n", n=W)
        sum_out = place(8)
        idx_tile = sb("idx_tile", [P, ROWS], U32)
        gate_tile = sb("gate_tile", [P, ROWS])
        stat = sb("rstat", [P, 4, 8])
        sum_ps = psum("sum_ps", [P, D])
        z_ps = psum("z_ps", [P, 2, D])
        group_ps = psum("group_ps", [P, W])
        out_ps = psum("out_ps", [P, W])
        turn_ps, acc_ps = z_ps[:, 0, :], z_ps[:, 1, :].rearrange("p (a n) -> p a n", n=W)
        qT_ps, score_ps = group_ps, out_ps

        tables_in = sem("rtables_in")
        out_w_in = sem("out_w_in")
        query_w_in = sem("query_w_in")
        x_in = sem("rx_in")
        mix_in = sem("mix_in")
        keys_turned = sem("keys_turned")
        keys_done = sem("keys_done")
        self_done = sem("rself_done")
        mean_done = sem("rmean_done")
        rstd_done = sem("rrstd_done")
        mix_done = sem("mix_done")
        turned = sem("rturned")
        inT_done = sem("inT_done")
        acc_done = sem("acc_done")
        h_done = sem("h_done")
        c_done = sem("c_done")
        query_done = sem("query_done")
        query_turned = sem("query_turned")
        queryT_done = sem("queryT_done")
        scored = sem("scored")
        scores_done = sem("rscores_done")
        shifted = sem("shifted")
        raised = sem("raised")
        idx_done = sem("idx_done")
        gates_done = sem("gates_done")
        idx_taken = sem("idx_taken")
        c_taken = sem("c_taken")
        opened = sem("opened")
        u_in = [sem(f"u_in{n}") for n in range(U_RING)]
        v_in = [sem(f"v_in{n}") for n in range(V_RING)]
        u_used = sem("u_used")
        v_used = sem("v_used")
        gelu_done = sem("gelu_done")
        coef_done = sem("coef_done")
        diag_done = sem("diag_done")
        sum_taken = sem("sum_taken")
        sum_stored = sem("sum_stored")
        sum_free = sem("sum_free")
        cleared = sem("cleared")
        kd_in = sem("kd_in")
        ks_in = sem("ks_in")
        vd_in = sem("vd_in")
        vs_in = sem("vs_in")
        z_done = sem("z_done")
        max_done = sem("max_done")
        prob_done = sem("prob_done")
        share_done = sem("share_done")
        part_done = sem("part_done")
        weights_done = sem("weights_done")
        abs_done = sem("abs_done")
        exp_done = sem("exp_done")
        log_done = sem("log_done")
        soft_done = sem("soft_done")
        scan_done = sem("scan_done")
        expo_done = sem("expo_done")
        stick_done = sem("stick_done")
        w_turned = sem("w_turned")
        wT_done = sem("wT_done")
        out_done = sem("out_done")
        rows_taken = sem("rows_taken")
        block = ctx.enter_context(nc.Block())

        def groups(i):
            return [(a, min(a + 4, i + 1)) for a in range(0, i + 1, 4)]

        def groups_before(i, m, h):
            return sum(16 * len(groups(j)) for j in range(i)) + (4 * m + h) * len(groups(i))

        def attending_steps(eng, body):
            with eng.Fori(0, 2) as r:
                for b in range(2):
                    body(2 * r + b, b)

        def all_steps(eng, body):
            with eng.Fori(0, HEADS // 2) as r:
                for b in range(2):
                    body(2 * r + b, b)

        SELF = 23

        @block.sync
        def _(sp):
            for dst, src in ((gain[:, :], bass.AP(ins["g_ffn"].tensor, 0, [[0, P], [1, D]])),
                             (sub_gain[:, :], bass.AP(ins["g_subln"].tensor, 0, [[0, P], [1, 64]])),
                             (steps16[:, :], ins["steps16"]),
                             (keys[:, :, :], ins["sub_keys"].rearrange("s n d -> n s d"))):
                sp.dma_start(dst, src).then_inc(tables_in, 16)
            sp.dma_start(x[:, :], ins["x_all"][TP * P:T * P, :]).then_inc(x_in, 16)
            sp.dma_start(mix[:, :], heads).then_inc(mix_in, 16)
            sp.dma_start(w_out[:, :, :], ins["w_out"].rearrange("(k p) n -> p k n", p=P)).then_inc(out_w_in, 16)
            sp.dma_start(w_query[:, :, :], ins["w_query"].rearrange("(k p) n -> p k n", p=P)).then_inc(query_w_in, 16)
            prime(sp, sum_free, by=2)

            def store(e):
                sp.wait_ge(sum_taken, e + 2)
                sp.dma_start(summed[tile_at(e)], sum_out).then_inc(sum_stored, 16)
                sp.wait_ge(sum_stored, e * 16 + 16)
                sp.sem_inc(sum_free, 1)

            sp.wait_ge(cleared, 2)
            for e in range(TP):
                i = tile_at(e + 1)
                if e:
                    store(e - 1)
                sp.wait_ge(gates_done, e + 2)
                sp.wait_ge(c_taken, e + 1)

                def load(m, b):
                    n = 4 * i + m
                    wait_apart(sp, const, z_done, 6 * n + 4)
                    sp.dma_start(kd[:, 0:i + 1, :], qk_turned[1, 0:i + 1, :, bass.ds(m * P, P)]
                                 .rearrange("j p k -> p j k")).then_inc(kd_in, 16)
                    for a in range(4):
                        sp.dma_start(qd[a * 32:(a + 1) * 32, a, :],
                                     qk_turned[0, i, a * 32:(a + 1) * 32, bass.ds(m * P, P)]).then_inc(kd_in, 16)
                    wait_apart(sp, const, z_done, 6 * n + 6)
                    sp.dma_start(ks[:, 0:i + 1, :], qk_turned[3, 0:i + 1, :, bass.ds(m * P, P)]
                                 .rearrange("j p k -> p j k")).then_inc(ks_in, 16)
                    for a in range(2):
                        sp.dma_start(qs[a * 64:(a + 1) * 64, a, :],
                                     qk_turned[2, i, a * 64:(a + 1) * 64, bass.ds(m * P, P)]).then_inc(ks_in, 16)
                    for v, kind, landed, over in ((vd, VD, vd_in, 2), (vs, VS, vs_in, 4)):
                        wait_apart(sp, const, out_done, 4 * n + over)
                        sp.dma_start(v[:, 0:i + 1, :], new_rows[kind][0:(i + 1) * P, bass.ds(m * P, P)]
                                     .rearrange("(j p) d -> p j d", p=P)).then_inc(landed, 16)
                attending_steps(sp, load)
                sp.wait_ge(opened, e + 1)
                sp.dma_start(x[:, :], ins["x_all"][i * P:(i + 1) * P, :]).then_inc(x_in, 16)
            store(TP - 1)
            store(TP)

        @block.gpsimd
        def _(pool):
            def power(t, n):
                width = (8, 1)[n]
                pool.wait_ge(mean_done, 2 * t + (n + 1))
                nc.gpsimd.tensor_tensor(stat[:, 2, 0:width], stat[:, 1, 0:width],
                                        const.minus_half.broadcast_to((P, width)), ALU.pow).then_inc(rstd_done, 1)

            def take_idx(e, n, s, b):
                pool.wait_ge(idx_done, e + 2)
                pool.wait_ge(v_used, n * TOP + V_AHEAD - TOP)
                nc.gpsimd.tensor_copy(idx_now[:, b, :], idx_tile[:, bass.ds(s * TOP, TOP)]).then_inc(idx_taken, 1)
                pool.wait_ge(idx_taken, n + 1)

            def gather_u(n, b, first=0, end=TOP):
                for k in range(first, end):
                    wait_apart(pool, const, u_used, n * TOP + (k + 1))
                    pool.indirect_dma_start(u_rows[k % U_RING][:, :], None, ins["expert_u"],
                                            bass.IndirectOffsetOnAxis(ap=idx_now[:, b, k:k + 1], axis=0)
                                            ).then_inc(u_in[k % U_RING], 16)

            def gather_v(n, b, first, end):
                for k in range(first, end):
                    wait_apart(pool, const, v_used, n * TOP + (k + 1 + TOP))
                    pool.indirect_dma_start(v_rows[k % V_RING][:, :], None, ins["expert_v"],
                                            bass.IndirectOffsetOnAxis(ap=idx_now[:, b, k:k + 1], axis=0)
                                            ).then_inc(v_in[k % V_RING], 16)

            def weigh(e, n, s, b):
                pool.wait_ge(gates_done, e + 2)
                pool.wait_ge(gelu_done, n + 1)
                nc.gpsimd.tensor_tensor(coef[:, b, :], gelus[:, b, :], gate_tile[:, bass.ds(s * TOP, TOP)],
                                        ALU.mult).then_inc(coef_done, 1)

            def step(e, s, b):
                n = HEADS * e + s
                take_idx(e, n, s, b)
                gather_u(n, b)
                gather_v(n, b, 0, V_RING)
                weigh(e, n, s, b)
                gather_v(n, b, V_RING, TOP)

            nc.gpsimd.memset(qd[:, :, :], 0.0).then_inc(cleared, 1)
            nc.gpsimd.memset(qs[:, :, :], 0.0).then_inc(cleared, 1)
            for n in range(2):
                power(0, n)
            for e in range(TP):
                attending_steps(pool, lambda m, b: step(e, m, b))
                for s in range(4, HEADS):
                    n, b = HEADS * e + s, s % 2
                    take_idx(e, n, s, b)
                    gather_u(n, b, 0, 6)
                    if s == 4:
                        power(e + 1, 0)
                    gather_u(n, b, 6, TOP)
                    gather_v(n, b, 0, V_RING)
                    weigh(e, n, s, b)
                    if s == 4:
                        power(e + 1, 1)
                    gather_v(n, b, V_RING, TOP)
            all_steps(pool, lambda s, b: step(TP, s, b))

        @block.tensor
        def _(pe):
            pe.wait_ge(tables_in, 64)
            for s in range(2):
                mm = nc.tensor.transpose(qT_ps[:, s * P:(s + 1) * P], keys[:, s, :], const.ident)
            mm.then_inc(keys_turned, 1)
            prime(pe, turned, by=2)
            prime(pe, scored, query_turned, by=4)
            prime(pe, v_used, by=V_AHEAD)
            prime(pe, z_done, by=6)
            prime(pe, out_done, by=4)
            prime(pe, w_turned)
            pe.wait_ge(keys_done, 1)

            def turn(src, ready, t, n):
                pe.wait_ge(*ready)
                for k in range(KC):
                    mm = nc.tensor.transpose(turn_ps[:, k * P:(k + 1) * P], src[:, k * P:(k + 1) * P], const.ident)
                mm.then_inc(turned, 1)
                pe.wait_ge(inT_done, 2 * t + n)

            def product(weights, half, bank):
                for k in range(KC):
                    mm = nc.tensor.matmul(acc_ps[:, bank, :], inT[:, k, :], weights[:, k, half * W:(half + 1) * W],
                                          start=(k == 0), stop=(k == KC - 1))
                mm.then_inc(acc_done, 1)

            def project_heads(t):
                turn(mix, (mix_done, t + 1), t, 1)
                pe.wait_ge(out_w_in, 16)
                pe.wait_ge(query_done, 4 * t + 4)
                for n in range(2):
                    product(w_out, n, n)

            def queries(t, g):
                if g == 0:
                    turn(c, (c_done, t + 2), t, 2)
                    pe.wait_ge(query_w_in, 16)
                if g < 2:
                    pe.wait_ge(h_done, t + 2)
                else:
                    pe.wait_ge(query_done, 4 * t + (g + 3))
                product(w_query, g, g % 2)

            def match(t, g):
                pe.wait_ge(query_done, 4 * t + (g + 5))
                pe.wait_ge(queryT_done, 4 * t + (g + 4))
                for m in range(4):
                    mm = nc.tensor.transpose(qT_ps[:, m * P:(m + 1) * P],
                                             query[:, g % 2, m * P:(m + 1) * P], const.ident)
                mm.then_inc(query_turned, 1)
                pe.wait_ge(queryT_done, 4 * t + (g + 5))
                pe.wait_ge(scores_done, 4 * t + (g + 4))
                for m in range(4):
                    mm = nc.tensor.matmul(score_ps[:, m * P:(m + 1) * P], queryT[:, g % 2, m * P:(m + 1) * P],
                                          keysT[:, m % 2, :], start=True, stop=True)
                mm.then_inc(scored, 1)

            def open_sum(e):
                pe.wait_ge(h_done, e + 2)
                pe.wait_ge(sum_taken, e + 1)
                for n in range(2):
                    mm = nc.tensor.matmul(sum_ps[:, n * W:(n + 1) * W], const.ident, x[:, n * W:(n + 1) * W],
                                          start=True, stop=False, skip_group_check=True)
                mm.then_inc(opened, 1)

            def add_rows(n, b, first=0, end=TOP):
                for k in range(first, end):
                    pe.wait_ge(v_in[k % V_RING], n * (TOP // V_RING * 16) + (k // V_RING + 1) * 16)
                    pe.wait_ge(diag_done, n * TOP + (k + 1))
                    for half in range(2):
                        mm = nc.tensor.matmul(sum_ps[:, half * W:(half + 1) * W], diag[:, k % DIAGS, :],
                                              v_rows[k % V_RING][:, half * W:(half + 1) * W],
                                              start=False, stop=(k == TOP - 1), skip_group_check=True)
                    mm.then_inc(v_used, 1)

            def attention_scores(i, j, n):
                width = (i + 1) * P
                if j < 2:
                    pe.wait_ge(expo_done, 2 * n + (j + 1))
                else:
                    pe.wait_ge(prob_done, 4 * n + (j - 1))
                if j == 0:
                    pe.wait_ge(kd_in, 80 * n + 80)
                if j == 4:
                    pe.wait_ge(ks_in, 48 * n + 48)
                q, kt, mask = (qd[:, j, :], kd, const.chunk_mask) if j < 4 else (qs[:, j - 4, :], ks, const.strict_mask)
                for a in range(0, width, W):
                    w = min(W, width - a)
                    nc.tensor.matmul(z_ps[:, j % 2, a:a + w], q, kt.rearrange("p j k -> p (j k)")[:, a:a + w],
                                     start=True, stop=a + w < width)
                nc.tensor.matmul(z_ps[:, j % 2, i * P:width], const.ident, mask, start=False, stop=True
                                 ).then_inc(z_done, 1)

            def turn_weights(i, m, h, n):
                if h < 2:
                    pe.wait_ge(weights_done, 2 * n + (h + 1))
                else:
                    pe.wait_ge(stick_done, 2 * n + (h - 1))
                src = prob[2 * h] if h < 2 else stick[h - 2]
                for g, (a, z) in enumerate(groups(i)):
                    pe.wait_ge(wT_done, groups_before(i, m, h) + (g + 1))
                    for k in range(a, z):
                        mm = nc.tensor.transpose(group_ps[:, (k - a) * P:(k - a + 1) * P],
                                                 src[:, k * P:(k + 1) * P], const.ident)
                    mm.then_inc(w_turned, 1)

            def weigh_values(i, m, h, n):
                if h % 2 == 0:
                    pe.wait_ge(rows_taken, 2 * n + (h // 2 + 1))
                    pe.wait_ge((vd_in, vs_in)[h // 2], 16 * n + 16)
                pe.wait_ge(wT_done, groups_before(i, m, h) + (len(groups(i)) + 1))
                v = vd if h < 2 else vs
                for k in range(i + 1):
                    mm = nc.tensor.matmul(out_ps[:, 64 * h:64 * h + 64], wT[:, k * P:(k + 1) * P],
                                          v[:, k, 64 * (h % 2):64 * (h % 2) + 64], start=(k == 0), stop=(k == i))
                mm.then_inc(out_done, 1)

            def attending_step(e, m, b):
                i = tile_at(e + 1)
                n = 4 * i + m
                for j in range(6):
                    attention_scores(i, j, n)
                for h in range(2):
                    turn_weights(i, m, h, n)
                    weigh_values(i, m, h, n)
                rows = HEADS * e + m
                add_rows(rows, b, 0, 3)
                turn_weights(i, m, 2, n)
                add_rows(rows, b, 3, 5)
                weigh_values(i, m, 2, n)
                add_rows(rows, b, 5, 8)
                turn_weights(i, m, 3, n)
                add_rows(rows, b, 8, 10)
                weigh_values(i, m, 3, n)
                add_rows(rows, b, 10, TOP)

            def route_queries(t):
                for g in range(4):
                    queries(t, g)
                    if g:
                        match(t, g - 1)
                match(t, 3)

            project_heads(0)
            route_queries(0)
            for e in range(TP):
                open_sum(e)
                pe.wait_ge(scores_done, 4 * e + 8)
                attending_steps(pe, lambda m, b: attending_step(e, m, b))
                for s in range(4, HEADS):
                    if s == 4:
                        project_heads(e + 1)
                    elif s == 5:
                        route_queries(e + 1)
                    add_rows(HEADS * e + s, s % 2)
            open_sum(TP)
            all_steps(pe, lambda s, b: add_rows(HEADS * TP + s, b))

        @block.scalar
        def _(act):
            prime(act, query_done, queryT_done, scores_done, by=4)
            prime(act, sum_taken, wT_done)
            prime(act, rows_taken, by=2)
            act.wait_ge(keys_turned, 1)
            nc.scalar.copy(keysT[:, :, :].rearrange("p s n -> p (s n)"), qT_ps[:, 0:2 * P]).then_inc(keys_done, 1)

            def take_turned(t, n):
                act.wait_ge(turned, 2 * t + (n + 3))
                nc.scalar.copy(inT[:, :, :].rearrange("p k n -> p (k n)"), turn_ps).then_inc(inT_done, 1)

            def take_query(t, g):
                act.wait_ge(acc_done, 6 * t + (g + 3))
                act.wait_ge(query_turned, 4 * t + (g + 3))
                nc.scalar.copy(query[:, g % 2, :], acc_ps[:, g % 2, :]).then_inc(query_done, 1)

            def take_scores(t, g):
                act.wait_ge(query_turned, 4 * t + (g + 5))
                act.wait_ge(scored, 4 * t + (g + 3))
                nc.scalar.copy(queryT[:, g % 2, :], qT_ps[:, :]).then_inc(queryT_done, 1)
                act.wait_ge(scored, 4 * t + (g + 5))
                if g == 0:
                    act.wait_ge(idx_done, t + 1)
                nc.scalar.copy(scores[:, 4 * g:4 * g + 4, :].rearrange("p m n -> p (m n)"),
                               score_ps[:, :]).then_inc(scores_done, 1)

            def exponents(t):
                act.wait_ge(shifted, t + 1)
                nc.scalar.activation(expo[:, :, :], expo[:, :, :], ACT.Exp).then_inc(raised, 1)

            def take_tokens(e):
                act.wait_ge(c_done, e + 2)
                act.wait_ge(u_used, e * ROWS + U_RING)
                nc.scalar.copy(c_rows[:, :], c).then_inc(c_taken, 1)

            def raise_products(n, b):
                act.wait_ge(u_used, n * TOP + (TOP + U_RING))
                nc.scalar.activation(gelus[:, b, :], dots[:, b, :], ACT.Gelu).then_inc(gelu_done, 1)
                act.wait_ge(coef_done, n + 1)

            def spread(n, b, first=0, end=TOP):
                for k in range(first, end):
                    act.wait_ge(v_used, n * TOP + (k + 1 - DIAGS + V_AHEAD))
                    nc.scalar.mul(diag[:, k % DIAGS, :], const.ident, coef[:, b, k:k + 1]).then_inc(diag_done, 1)

            def close_sum(e):
                act.wait_ge(v_used, e * ROWS + (ROWS + V_AHEAD))
                act.wait_ge(sum_free, e + 2)
                nc.scalar.copy(sum_out, sum_ps[:, :]).then_inc(sum_taken, 1)

            def softmax_top(i, c, m, n):
                act.wait_ge(max_done, 4 * n + (c + 1))
                if c < 2:
                    act.wait_ge(scan_done, 2 * n + (2 - c))
                else:
                    act.wait_ge(w_turned, groups_before(i, m, 0) + 1)
                width = (i + 1) * P
                nc.scalar.activation(prob[c][:, 0:width], z_ps[:, c % 2, 0:width], ACT.Exp,
                                     bias=neg_max[:, c:c + 1], accum_out=total[:, c:c + 1]).then_inc(prob_done, 1)

            def log_term(i, s, n):
                act.wait_ge(z_done, 6 * n + (11 + s))
                act.wait_ge(weights_done, 2 * n + 1)
                u = soft[s][:, 0:(i + 1) * P]
                nc.scalar.activation(u, z_ps[:, s, 0:(i + 1) * P], ACT.Abs).then_inc(abs_done, 1)
                act.wait_ge(abs_done, 2 * n + (s + 1))
                nc.scalar.activation(u, u, ACT.Exp, scale=-1.0).then_inc(exp_done, 1)
                act.wait_ge(exp_done, 2 * n + (s + 1))
                nc.scalar.activation(u, u, ACT.Ln, bias=const.one).then_inc(log_done, 1)

            def take_weights(i, m, h, n):
                act.wait_ge(out_done, 4 * n + (h + 4))
                for g, (a, z) in enumerate(groups(i)):
                    act.wait_ge(w_turned, groups_before(i, m, h) + (g + 2))
                    nc.scalar.copy(wT[:, a * P:z * P], group_ps[:, 0:(z - a) * P]).then_inc(wT_done, 1)

            def take_out(kind, m, n):
                act.wait_ge(out_done, 4 * n + (2 * kind + 6))
                nc.scalar.copy(mix[:, bass.ds(m * P + kind * W, P)], out_ps[:, kind * P:(kind + 1) * P]
                               ).then_inc(rows_taken, 1)

            def raise_stick(i, s, n):
                act.wait_ge(expo_done, 2 * n + (s + 3))
                e = stick[s][:, 0:(i + 1) * P]
                nc.scalar.activation(e, e, ACT.Exp).then_inc(stick_done, 1)

            def attending_step(e, m, b):
                i = tile_at(e + 1)
                n = 4 * i + m
                for c in range(4):
                    softmax_top(i, c, m, n)
                log_term(i, 0, n)
                take_weights(i, m, 0, n)
                log_term(i, 1, n)
                take_weights(i, m, 1, n)
                take_out(0, m, n)
                raise_stick(i, 0, n)
                rows = HEADS * e + m
                raise_products(rows, b)
                spread(rows, b, 0, 4)
                take_weights(i, m, 2, n)
                spread(rows, b, 4, 6)
                raise_stick(i, 1, n)
                spread(rows, b, 6, 9)
                take_weights(i, m, 3, n)
                spread(rows, b, 9, 13)
                take_out(1, m, n)
                spread(rows, b, 13, TOP)

            def route_queries(t):
                take_turned(t, 1)
                for g in range(4):
                    take_query(t, g)
                    if g:
                        take_scores(t, g - 1)
                take_scores(t, 3)

            take_turned(0, 0)
            route_queries(0)
            exponents(0)
            for e in range(TP):
                take_tokens(e)
                act.wait_ge(sum_free, e + 2)
                attending_steps(act, lambda m, b: attending_step(e, m, b))
                for s in range(4, HEADS):
                    if s == 4:
                        take_turned(e + 1, 0)
                    elif s == 5:
                        route_queries(e + 1)
                    elif s == 7:
                        exponents(e + 1)
                    raise_products(HEADS * e + s, s % 2)
                    spread(HEADS * e + s, s % 2)
                close_sum(e)
            take_tokens(TP)

            def last_step(s, b):
                raise_products(HEADS * TP + s, b)
                spread(HEADS * TP + s, b)
            all_steps(act, last_step)
            close_sum(TP)

        @block.vector
        def _(dve):
            prime(dve, h_done, c_done, idx_done, gates_done)
            prime(dve, u_used, by=U_RING)
            prime(dve, expo_done, scan_done, by=2)
            dve.wait_ge(tables_in, 64)
            at = [0]

            def chain(t, done):
                at[0] += 1
                done.then_inc(self_done, 1)
                wait_apart(dve, const, self_done, t * SELF + at[0])

            def by_head(a):
                return a.rearrange("p (h d) -> p h d", d=64)

            def norm_heads(t):
                at[0] = 0
                if t == 0:
                    dve.wait_ge(mix_in, 16)
                else:
                    dve.wait_ge(rows_taken, 8 * t + 2)
                diff = mix[:, 0:W]
                chain(t, nc.vector.tensor_tensor(work[:, 0:W], diff, diff, ALU.mult))
                chain(t, nc.vector.tensor_reduce(stat[:, 0, :], by_head(work[:, 0:W]), AX.X, ALU.add))
                nc.vector.tensor_scalar(stat[:, 1, :], stat[:, 0, :], 1.0 / 64, 1e-5, ALU.mult,
                                        ALU.add).then_inc(mean_done, 1)
                dve.wait_ge(rstd_done, 2 * t + 1)
                chain(t, nc.vector.tensor_tensor(by_head(work[:, 0:W]), by_head(diff),
                                                 stat[:, 2, :].unsqueeze(2).broadcast_to((P, 8, 64)), ALU.mult))
                nc.vector.scalar_tensor_tensor(by_head(diff), by_head(work[:, 0:W]), 1.0 - LAMBDA_START,
                                               sub_gain[:, :].unsqueeze(1).broadcast_to((P, 8, 64)),
                                               ALU.mult, ALU.mult).then_inc(mix_done, 1)

            def norm_tokens(t):
                dve.wait_ge(x_in, t * 16 + 16)
                dve.wait_ge(acc_done, 6 * t + 2)
                nc.vector.tensor_tensor(x[:, :], x[:, :], acc_ps[:, :, :].rearrange("p a n -> p (a n)"),
                                        ALU.add).then_inc(h_done, 1)
                dve.wait_ge(h_done, t + 2)
                chain(t, nc.vector.tensor_tensor_reduce(work, x[:, :], x[:, :], 1.0, 0.0, ALU.mult, ALU.add,
                                                        stat[:, 0, 0:1]))
                nc.vector.tensor_scalar(stat[:, 1, 0:1], stat[:, 0, 0:1], 1.0 / D, EPS,
                                        ALU.mult, ALU.add).then_inc(mean_done, 1)
                dve.wait_ge(rstd_done, 2 * t + 2)
                if t:
                    dve.wait_ge(c_taken, t)
                nc.vector.scalar_tensor_tensor(c, x[:, :], stat[:, 2, 0:1], gain[:, :],
                                               ALU.mult, ALU.mult).then_inc(c_done, 1)

            def best8(t, src, rest, vals):
                n = src.shape[1]
                for m in range(n):
                    last = nc.vector.max(vals[:, m, 0:8], src[:, m, :])
                chain(t, last)
                for m in range(n):
                    last = nc.vector.match_replace(rest[:, m, :], vals[:, m, 0:8], src[:, m, :], -3e38)
                chain(t, last)

            def next8(t, src, rest, vals, places):
                n = src.shape[1]
                for m in range(n):
                    last = nc.vector.max(vals[:, m, 8:16], rest[:, m, :])
                for m in range(n):
                    last = nc.vector.max_index(places[:, m, 0:8], vals[:, m, 0:8], src[:, m, :])
                chain(t, last)
                for m in range(n):
                    last = nc.vector.max_index(places[:, m, 8:16], vals[:, m, 8:16], rest[:, m, :])
                chain(t, last)

            wide = scores[:, :, :].rearrange("p m n -> p (m n)")
            spare_wide = spare[:, :, :].rearrange("p m n -> p (m n)")
            of_sides = (scores[:, :, :], spare[:, :, :], top[:, :, :])
            of_sums = (wide.rearrange("p (h n) -> p h n", h=HEADS), spare_wide.rearrange("p (h n) -> p h n", h=HEADS),
                       val[:, :, :])

            def best_sides(t):
                wait_apart(dve, const, scores_done, 4 * t + 8)
                best8(t, *of_sides)

            def best_sums(t):
                next8(t, *of_sides, pos[:, :, :])
                sides = top[:, :, :].rearrange("p (h s) a -> p h s a", s=2)
                grid = wide.rearrange("p (h a b) -> p h a b", a=TOP, b=TOP)
                chain(t, nc.vector.tensor_tensor(grid, sides[:, :, 0, :].unsqueeze(3).broadcast_to((P, HEADS, TOP, TOP)),
                                                 sides[:, :, 1, :].unsqueeze(2).broadcast_to((P, HEADS, TOP, TOP)),
                                                 ALU.add))

            def places_of_sums(t):
                best8(t, *of_sums)
                next8(t, *of_sums, sel[:, :, :])
                nc.vector.tensor_tensor(expo[:, :, :], val[:, :, :], val[:, :, 0:1].broadcast_to((P, HEADS, TOP)),
                                        ALU.subtract).then_inc(shifted, 1)
                nc.vector.tensor_scalar(part[:, 0, :, :], sel[:, :, :], 4, None, ALU.logical_shift_right)

            def experts_of_places(t):
                nc.vector.tensor_copy(posf[:, :, :], pos[:, :, :])
                chain(t, nc.vector.tensor_scalar(part[:, 1, :, :], sel[:, :, :], 15, None, ALU.bitwise_and))
                chain(t, nc.vector.tensor_copy(partf[:, :, :, :], part[:, :, :, :]))
                keys_at = posf[:, :, :].rearrange("p (h s) a -> p h s a", s=2)
                for s in range(2):
                    buf = (wide, spare_wide)[s].rearrange("p (h k a) -> p h k a", k=TOP, a=TOP)
                    hk = buf.rearrange("p h k a -> p (h k) a")
                    chain(t, nc.vector.tensor_tensor(
                        hk, partf[:, s, :, :].rearrange("p h k -> p (h k)").unsqueeze(2).broadcast_to((P, P, TOP)),
                        steps16[:, :].unsqueeze(1).broadcast_to((P, P, TOP)), ALU.is_equal))
                    chain(t, nc.vector.tensor_tensor(buf, buf, keys_at[:, :, s, :].unsqueeze(2)
                                                     .broadcast_to((P, HEADS, TOP, TOP)), ALU.mult))
                    last = nc.vector.tensor_reduce(picked[:, s, :, :].rearrange("p h k -> p (h k)"), hk, AX.X, ALU.add)
                chain(t, last)
                chain(t, nc.vector.scalar_tensor_tensor(picked[:, 0, :, :], picked[:, 0, :, :], float(SIDE),
                                                        picked[:, 1, :, :], ALU.mult, ALU.add))
                if t:
                    dve.wait_ge(idx_taken, HEADS * t)
                nc.vector.tensor_copy(idx_tile[:, :], picked[:, 0, :, :].rearrange("p h k -> p (h k)")
                                      ).then_inc(idx_done, 1)

            def gates(t):
                dve.wait_ge(raised, t + 1)
                chain(t, nc.vector.tensor_reduce(stat[:, 0, :], expo[:, :, :], AX.X, ALU.add))
                chain(t, nc.vector.reciprocal(stat[:, 3, :], stat[:, 0, :]))
                if t:
                    dve.wait_ge(coef_done, HEADS * t)
                nc.vector.tensor_tensor(gate_tile[:, :].rearrange("p (h k) -> p h k", k=TOP),
                                        expo[:, :, :], stat[:, 3, :].unsqueeze(2).broadcast_to((P, HEADS, TOP)),
                                        ALU.mult).then_inc(gates_done, 1)
                assert at[0] == SELF, at[0]

            def reduce(n, b, first=0, end=TOP):
                for k in range(first, end):
                    dve.wait_ge(u_in[k % U_RING], n * (TOP // U_RING * 16) + (k // U_RING + 1) * 16)
                    row = u_rows[k % U_RING][:, :]
                    nc.vector.tensor_tensor_reduce(row, row, c_rows[:, :], 1.0, 0.0, ALU.mult, ALU.add,
                                                   dots[:, b, k:k + 1]).then_inc(u_used, 1)

            def maximum(i, c, n):
                dve.wait_ge(z_done, 6 * n + (c + 7))
                nc.vector.tensor_reduce(neg_max[:, c:c + 1], z_ps[:, c % 2, 0:(i + 1) * P], AX.X, ALU.max,
                                        negate=True).then_inc(max_done, 1)

            def subtract_half(i, h, n):
                dve.wait_ge(prob_done, 4 * n + (2 * h + 2))
                nc.vector.reciprocal(share[:, 2 * h:2 * h + 2], total[:, 2 * h:2 * h + 2]).then_inc(share_done, 1)
                dve.wait_ge(share_done, 2 * n + (h + 1))
                b2 = prob[2 * h + 1][:, 0:(i + 1) * P]
                nc.vector.tensor_scalar(b2, b2, share[:, 2 * h + 1:2 * h + 2], const.lam,
                                        ALU.mult, ALU.mult).then_inc(part_done, 1)
                dve.wait_ge(part_done, 2 * n + (h + 1))
                b1 = prob[2 * h][:, 0:(i + 1) * P]
                nc.vector.scalar_tensor_tensor(b1, b1, share[:, 2 * h:2 * h + 1], b2,
                                               ALU.mult, ALU.subtract).then_inc(weights_done, 1)

            def break_stick(i, m, s, n):
                width = (i + 1) * P
                z, u, e = z_ps[:, s, 0:width], soft[s][:, 0:width], stick[s][:, 0:width]
                dve.wait_ge(log_done, 2 * n + (s + 1))
                nc.vector.scalar_tensor_tensor(u, z, 0.0, u, ALU.max, ALU.add).then_inc(soft_done, 1)
                dve.wait_ge(soft_done, 2 * n + (s + 1))
                if s == 1:
                    dve.wait_ge(w_turned, groups_before(i, m, 2) + 1)
                nc.vector.tensor_tensor_scan(e[:, ::-1], u[:, ::-1], const.zero.broadcast_to((P, width)), 0.0,
                                             ALU.add, ALU.add).then_inc(scan_done, 1)
                dve.wait_ge(scan_done, 2 * n + (s + 3))
                nc.vector.tensor_tensor(e, z, e, ALU.subtract).then_inc(expo_done, 1)

            def attending_step(e, m, b):
                i = tile_at(e + 1)
                n = 4 * i + m
                rows = HEADS * e + m
                reduce(rows, b, 0, 3)
                maximum(i, 0, n)
                maximum(i, 1, n)
                reduce(rows, b, 3, 5)
                maximum(i, 2, n)
                maximum(i, 3, n)
                reduce(rows, b, 5, 6)
                subtract_half(i, 0, n)
                reduce(rows, b, 6, 8)
                subtract_half(i, 1, n)
                reduce(rows, b, 8, 13)
                break_stick(i, m, 0, n)
                reduce(rows, b, 13, TOP)
                break_stick(i, m, 1, n)

            norm_heads(0)
            norm_tokens(0)
            best_sides(0)
            best_sums(0)
            places_of_sums(0)
            experts_of_places(0)
            gates(0)
            for e in range(TP):
                dve.wait_ge(c_taken, e + 1)
                attending_steps(dve, lambda m, b: attending_step(e, m, b))
                for s in range(4, HEADS):
                    n, b, t = HEADS * e + s, s % 2, e + 1
                    reduce(n, b, 0, 3)
                    if s == 4:
                        norm_heads(t)
                    reduce(n, b, 3, TOP)
                    if s == 4:
                        norm_tokens(t)
                    elif s == 5:
                        best_sides(t)
                        best_sums(t)
                    elif s == 6:
                        places_of_sums(t)
                    else:
                        experts_of_places(t)
                        gates(t)
            dve.wait_ge(c_taken, T)
            all_steps(dve, lambda s, b: reduce(HEADS * TP + s, b))


def finish(nc, const, ins, summed, y):
    with ExitStack() as ctx:
        def sb(name, shape, dt=F32):
            return ctx.enter_context(nc.sbuf_tensor(name, shape, dt))

        sem = stage_semaphores(nc, ctx)

        w_gate = sb("w_gate_sb", [P, KC, D])
        w_ple = sb("w_ple_sb", [P, 2, D])
        gains = sb("gains", [P, 2, D])
        h = [sb(f"fh{u}", [P, D]) for u in range(2)]
        p_rows = [sb(f"p_rows{u}", [P, 2, P]) for u in range(2)]
        pT = sb("pT", [P, 2, P])
        b = sb("fb", [P, D])
        bT = sb("bT", [P, KC, P])
        gate = sb("fgate", [P, D])
        squares = sb("fsquares", [P, D])
        y_sb = sb("y_sb", [P, D])
        stat = sb("fstat", [P, 2, 4])
        turn_ps = ctx.enter_context(nc.psum_tensor("fturn_ps", [P, D], F32))
        p_ps = ctx.enter_context(nc.psum_tensor("p_ps", [P, 2, P], F32))
        gate_ps = ctx.enter_context(nc.psum_tensor("gate_ps", [P, D], F32))
        ple_ps = ctx.enter_context(nc.psum_tensor("ple_ps", [P, D], F32))

        tables_in = sem("ftables_in")
        gate_w_in = sem("gate_w_in")
        ple_w_in = sem("ple_w_in")
        tile_in = [sem(f"ftile_in{u}") for u in range(2)]
        squared = sem("fsquared")
        mean_done = sem("fmean_done")
        rstd_done = sem("frstd_done")
        b_done = sem("b_done")
        turned = sem("fturned")
        taken = sem("ftaken")
        gate_summed = sem("gate_summed")
        ple_summed = sem("ple_summed")
        gate_done = sem("gate_done")
        mixed = sem("fmixed")
        added = sem("fadded")
        y_done = sem("y_done")
        y_out = sem("y_out")
        y_free = sem("y_free")
        block = ctx.enter_context(nc.Block())

        def tiles(eng, body):
            body(0, 0, None)
            with eng.Fori(0, TP // 2) as r:
                for u in (1, 2):
                    body(2 * r + u, u % 2, r)


        @block.sync
        def _(sp):
            for n, name in enumerate(("g_ple", "g_final")):
                sp.dma_start(gains[:, n, :], bass.AP(ins[name].tensor, 0, [[0, P], [1, D]])).then_inc(tables_in, 16)
            sp.dma_start(h[0][:, :], summed[0]).then_inc(tile_in[0], 16)
            sp.dma_start(p_rows[0][:, :, :].rearrange("p c n -> p (c n)"), ins["p_all"][0:P, :]).then_inc(tile_in[0], 16)
            sp.dma_start(w_ple[:, :, :], ins["w_ple"].rearrange("(k p) n -> p k n", p=P)).then_inc(ple_w_in, 16)
            sp.dma_start(w_gate[:, :, :], ins["w_pgate"].rearrange("(k p) n -> p k n", p=P)).then_inc(gate_w_in, 16)
            prime(sp, y_free)

            def store(t):
                sp.wait_ge(y_done, t + 2)
                sp.dma_start(y[bass.ds(t * P, P), :], y_sb[:, :]).then_inc(y_out, 16)
                sp.wait_ge(y_out, t * 16 + 16)
                sp.sem_inc(y_free, 1)

            with sp.Fori(0, TP // 2) as r:
                for u in (1, 2):
                    t = 2 * r + u
                    sp.wait_ge(y_done, t)
                    sp.dma_start(h[u % 2][:, :], summed[bass.ds(t, 1), :, :].rearrange("a p n -> (a p) n")
                                 ).then_inc(tile_in[u % 2], 16)
                    sp.dma_start(p_rows[u % 2][:, :, :].rearrange("p c n -> p (c n)"),
                                 ins["p_all"][bass.ds(t * P, P), :]).then_inc(tile_in[u % 2], 16)
                    store(t - 1)
            store(TP)

        @block.gpsimd
        def _(pool):
            def power(n, count):
                pool.wait_ge(mean_done, count)
                nc.gpsimd.tensor_tensor(stat[:, n, 2:3], stat[:, n, 1:2], const.minus_half, ALU.pow).then_inc(rstd_done, 1)

            power(0, 1)
            with pool.Fori(0, TP // 2) as r:
                for u in (1, 2):
                    t = 2 * r + u
                    power(0, 2 * t)
                    power(1, 2 * t + 1)
            power(1, 2 * T)

        @block.tensor
        def _(pe):
            prime(pe, turned, by=2)
            prime(pe, gate_summed)

            def tile(t, u, r):
                pe.wait_ge(tile_in[u], 32 if r is None else 32 * r + (32 if u else 64))
                pe.wait_ge(taken, 2 * t + 1)
                for k in range(2):
                    mm = nc.tensor.transpose(p_ps[:, k, :], p_rows[u][:, k, :], const.ident)
                mm.then_inc(turned, 1)
                pe.wait_ge(b_done, t + 1)
                for k in range(KC):
                    mm = nc.tensor.transpose(turn_ps[:, k * P:(k + 1) * P], b[:, k * P:(k + 1) * P], const.ident)
                mm.then_inc(turned, 1)
                pe.wait_ge(taken, 2 * t + 2)
                pe.wait_ge(ple_w_in, 16)
                pe.wait_ge(mixed, t + 1)
                for n in range(2):
                    for k in range(2):
                        mm = nc.tensor.matmul(ple_ps[:, n * W:(n + 1) * W], pT[:, k, :], w_ple[:, k, n * W:(n + 1) * W],
                                              start=(k == 0), stop=(k == 1))
                mm.then_inc(ple_summed, 1)
                pe.wait_ge(taken, 2 * t + 3)
                pe.wait_ge(gate_w_in, 16)
                pe.wait_ge(gate_done, t + 1)
                for n in range(2):
                    for k in range(KC):
                        mm = nc.tensor.matmul(gate_ps[:, n * W:(n + 1) * W], bT[:, k, :], w_gate[:, k, n * W:(n + 1) * W],
                                              start=(k == 0), stop=(k == KC - 1))
                mm.then_inc(gate_summed, 1)
            tiles(pe, tile)

        @block.scalar
        def _(act):
            prime(act, taken, gate_done)

            def tile(t, u, r):
                act.wait_ge(turned, 2 * t + 3)
                act.wait_ge(gate_summed, t + 1)
                nc.scalar.copy(pT[:, :, :], p_ps[:, :, :]).then_inc(taken, 1)
                act.wait_ge(turned, 2 * t + 4)
                nc.scalar.copy(bT[:, :, :].rearrange("p k n -> p (k n)"), turn_ps[:, :]).then_inc(taken, 1)
                act.wait_ge(gate_summed, t + 2)
                act.wait_ge(mixed, t + 1)
                nc.scalar.activation(gate[:, :], gate_ps[:, :], ACT.Sigmoid).then_inc(gate_done, 1)
            tiles(act, tile)

        @block.vector
        def _(dve):
            prime(dve, mixed, y_done)
            dve.wait_ge(tables_in, 32)

            def norm(n, u, dst, done, count, free=None):
                nc.vector.tensor_tensor_reduce(squares[:, :], h[u][:, :], h[u][:, :], 1.0, 0.0, ALU.mult, ALU.add,
                                               stat[:, n, 0:1]).then_inc(squared, 1)
                dve.wait_ge(squared, count)
                nc.vector.tensor_scalar(stat[:, n, 1:2], stat[:, n, 0:1], 1.0 / D, EPS,
                                        ALU.mult, ALU.add).then_inc(mean_done, 1)
                dve.wait_ge(rstd_done, count)
                if free:
                    dve.wait_ge(*free)
                nc.vector.scalar_tensor_tensor(dst, h[u][:, :], stat[:, n, 2:3], gains[:, n, :],
                                               ALU.mult, ALU.mult).then_inc(done, 1)

            def close(t, u, count):
                dve.wait_ge(gate_done, t + 2)
                dve.wait_ge(ple_summed, t + 1)
                nc.vector.tensor_tensor(squares[:, :], gate[:, :], ple_ps[:, :], ALU.mult).then_inc(mixed, 1)
                dve.wait_ge(mixed, t + 2)
                nc.vector.tensor_tensor(h[u][:, :], h[u][:, :], squares[:, :], ALU.add).then_inc(added, 1)
                dve.wait_ge(added, t + 1)
                norm(1, u, y_sb[:, :], y_done, count, (y_free, t + 1))

            dve.wait_ge(tile_in[0], 32)
            norm(0, 0, b[:, :], b_done, 1)
            with dve.Fori(0, TP // 2) as r:
                for u in (1, 2):
                    t = 2 * r + u
                    wait_apart(dve, const, tile_in[u % 2], 32 * r + 32 * u)
                    dve.wait_ge(turned, 2 * t + 2)
                    norm(0, u % 2, b[:, :], b_done, 2 * t)
                    close(t - 1, 1 - u % 2, 2 * t + 1)
            close(TP, 0, 2 * T)


def shape_constants():
    import numpy as np

    pos = np.concatenate([np.arange(TP * P), np.tile(256 + np.arange(16), 8)]).astype(np.float32)
    inv = np.float32(10000.0) ** (-np.arange(0, 32, 2, dtype=np.float32) / np.float32(32))
    ang = pos[:, None] * inv[None, :].astype(np.float32)
    cos, sin = np.cos(ang), np.sin(ang)
    q, k = np.arange(P)[:, None], np.arange(P)[None, :]
    at, chunk, head = np.arange(P)[:, None, None], np.arange(4)[None, :, None], np.arange(8)[None, None, :]
    own_head = head == 2 * chunk + at // 64
    own_half = np.stack([own_head & (at % 64 < 32), own_head & (at % 64 >= 32), own_head], axis=1)
    return {
        "rope": np.concatenate([cos, cos, -sin, sin], axis=1).astype(np.float32),
        "steps16": np.tile(np.arange(16, dtype=np.float32), (P, 1)),
        "identity": np.eye(P, dtype=np.float32),
        "chunk_mask": np.where(k // 64 > q // 64, HIDDEN, 0).astype(np.float32),
        "strict_mask": np.where(k >= q, HIDDEN, 0).astype(np.float32),
        "half_mask": own_half.astype(np.float32).reshape(P, -1),
        "head_mask": (q // 16 == np.arange(W)[None, :] // 64).astype(np.float32),
        "fold": (q % 16 == np.arange(16)[None, :]).astype(np.float32),
        "late_mask": np.where(np.arange(16)[None, :] >= q % 16, HIDDEN, 0).astype(np.float32),
    }


HIDDEN = -1e30
LAMBDA_START = 0.8 - 0.6


class Const:
    pass


def load_constants(nc, ctx, ins):
    c = Const()
    c.ident = ctx.enter_context(nc.sbuf_tensor("ident", [P, P], F32))[:, :]
    c.chunk_mask = ctx.enter_context(nc.sbuf_tensor("chunk_mask", [P, P], F32))[:, :]
    c.strict_mask = ctx.enter_context(nc.sbuf_tensor("strict_mask", [P, P], F32))[:, :]
    c.one = ctx.enter_context(nc.sbuf_tensor("one", [P, 1], F32))[:, :]
    c.zero = ctx.enter_context(nc.sbuf_tensor("zero", [P, 1], F32))[:, :]
    c.lam = ctx.enter_context(nc.sbuf_tensor("lam", [P, 1], F32))[:, :]
    vectors = ctx.enter_context(nc.sbuf_tensor("lambda_vectors", [P, 2, 64], F32))
    sums = ctx.enter_context(nc.sbuf_tensor("lambda_sums", [P, 2], F32))
    raised = ctx.enter_context(nc.semaphore("lambda_raised"))
    c.minus_half = ctx.enter_context(nc.sbuf_tensor("minus_half", [P, 1], F32))[:, :]
    loaded = ctx.enter_context(nc.semaphore("shared_loaded"))
    filled = ctx.enter_context(nc.semaphore("shared_filled"))
    c.passed = {e.engine: ctx.enter_context(nc.semaphore(f"passed{n}"))
                for n, e in enumerate((nc.vector, nc.gpsimd, nc.sync))}
    with nc.Block() as block:
        @block.sync
        def _(sp):
            for dst, name in ((c.ident, "identity"), (c.chunk_mask, "chunk_mask"), (c.strict_mask, "strict_mask")):
                sp.dma_start(dst, ins[name]).then_inc(loaded, 16)
            sp.dma_start(vectors[:, :, :].rearrange("p a d -> p (a d)"),
                         bass.AP(ins["lambdas"].tensor, 0, [[0, P], [1, P]])).then_inc(loaded, 16)

        @block.vector
        def _(dve):
            nc.vector.memset(c.minus_half, -0.5)
            nc.vector.memset(c.one, 1.0)
            nc.vector.memset(c.zero, 0.0)
            dve.wait_ge(loaded, 64)
            nc.vector.tensor_tensor(vectors[:, 0, :], vectors[:, 0, :], vectors[:, 1, :], ALU.mult).then_inc(filled, 1)
            dve.wait_ge(filled, 1)
            nc.vector.tensor_reduce(sums[:, :], vectors[:, 0, :].rearrange("p (a d) -> p a d", a=2), AX.X,
                                    ALU.add).then_inc(filled, 1)
            dve.wait_ge(raised, 1)
            nc.vector.scalar_tensor_tensor(c.lam, sums[:, 0:1], LAMBDA_START, sums[:, 1:2], ALU.add,
                                           ALU.subtract).then_inc(filled, 1)
            dve.wait_ge(filled, 3)

        @block.scalar
        def _(act):
            act.wait_ge(filled, 2)
            nc.scalar.activation(sums[:, :], sums[:, :], ACT.Exp).then_inc(raised, 1)
    return c


def build(nc, ins, outs):
    with ExitStack() as ctx:
        const = load_constants(nc, ctx, ins)
        qk_turned = nc.dram_tensor("qk_turned", (4, T, P, W), F32, kind="Internal").ap()
        new_rows = {KD: outs["new_dk"], VD: outs["new_dv"], KS: outs["new_sk"], VS: outs["new_sv"]}
        project_inputs(nc, const, ins["x_all"], ins["g_mix"], ins["w_in"], ins["rope"], new_rows, qk_turned)
        heads = nc.dram_tensor("sample_heads", (P, D), F32, kind="Internal").ap()
        attend_samples(nc, const, ins, qk_turned, new_rows, heads)
        summed = nc.dram_tensor("summed", (T, P, D), F32, kind="Internal").ap()
        attend_and_sum_experts(nc, const, ins, qk_turned, new_rows, heads, summed)
        finish(nc, const, ins, summed, outs["y"])


def kernel(**inputs):
    import numpy as _np
    import concourse.bacc as _bacc
    from concourse import mybir as _mybir
    from concourse.bass_utils import run_bass_kernel_spmd as _run

    def rows(*names):
        return _np.concatenate([_np.asarray(inputs[n]).reshape(-1, inputs[n].shape[-1]) for n in names])

    arrays = {
        "x_all": rows("x_prompt", "x_sample"),
        "p_all": rows("p_prompt", "p_sample"),
        "lambdas": _np.concatenate([_np.asarray(inputs[n]) for n in
                                    ("lambda_q1", "lambda_q2", "lambda_k1", "lambda_k2")]),
        **shape_constants(),
    }
    for n in ("cache_diff_k", "cache_diff_v", "cache_sb_k", "cache_sb_v"):
        arrays[n] = _np.asarray(inputs[n]).reshape(8, 256, W)
    for n in ("w_in", "w_out", "w_query", "w_pgate", "w_ple", "sub_keys", "expert_u", "expert_v"):
        arrays[n] = _np.asarray(inputs[n])[0]
    for n in ("g_mix", "g_subln", "g_ffn", "g_ple", "g_final"):
        arrays[n] = _np.asarray(inputs[n]).reshape(1, -1)
    arrays = {f"{n}_in": _np.ascontiguousarray(a) for n, a in arrays.items()}

    nc = _bacc.Bacc("TRN2", target_bir_lowering=False, num_devices=1)
    ins = {n[:-3]: nc.dram_tensor(n, a.shape, _mybir.dt.from_np(a.dtype), kind="ExternalInput").ap()
           for n, a in arrays.items()}
    outs = {n: nc.dram_tensor(n, (T * P, D if n == "y" else W), _mybir.dt.float32, kind="ExternalOutput").ap()
            for n in ("y", "new_dk", "new_dv", "new_sk", "new_sv")}
    build(nc, ins, outs)
    r = _run(nc, [arrays], core_ids=[0]).results[0]
    prompt = TP * P
    got = [r["y"][:prompt].reshape(1, prompt, D), r["y"][prompt:].reshape(8, 16, D)]
    for rows_of, shape in ((slice(0, prompt), (1, 1, prompt, 8, 64)), (slice(prompt, None), (1, 8, 16, 8, 64))):
        got += [r[n][rows_of].reshape(shape) for n in ("new_dk", "new_dv", "new_sk", "new_sv")]
    return tuple(got)
```

```python
from contextlib import ExitStack

import concourse.bass as bass
from concourse import mybir

F32 = mybir.dt.float32
U32 = mybir.dt.uint32
ALU = mybir.AluOpType
ACT = mybir.ActivationFunctionType
AX = mybir.AxisListType

P = 128
D = 1024
KC = D // P
W = 512
TP = 8
T = TP + 1
EPS = 1e-6
QD, KD, VD, QS, KS, VS = range(6)
TURNED = {QD: 0, KD: 1, QS: 2, KS: 3}


def stage_semaphores(nc, ctx):
    taken = []

    def clear():
        nc.clear_and_free_semaphores(taken)
        nc.all_engine_barrier()

    def sem(name):
        taken.append(nc.alloc_semaphore(name))
        return taken[-1]

    ctx.callback(clear)
    return sem


def prime(eng, *sems, by=1):
    for s in sems:
        eng.sem_inc(s, by)


def wait_apart(eng, const, sem, value):
    eng.wait_ge(sem, value)
    eng.sem_inc(const.passed[eng.engine], 1)


def project_inputs(nc, const, x_all, g_mix, w_in, rope, new_rows, qk_turned):
    with ExitStack() as ctx:
        def sb(name, shape, dt=F32):
            return ctx.enter_context(nc.sbuf_tensor(name, shape, dt))

        sem = stage_semaphores(nc, ctx)

        weights = sb("weights", [P, KC, 6 * W])
        x = sb("x", [P, D])
        squares = sb("squares", [P, D])
        a = sb("a", [P, D])
        aT = sb("aT", [P, KC, P])
        gain = sb("gain", [P, D])
        rope_tab = sb("rope_tab", [P, T, 64])
        rows = sb("rows", [P, 6, W])
        turned = sb("turned", [P, 4, W])
        rot = sb("rot", [P, 2, W])
        stat = sb("stat", [P, 4])
        turn_ps = ctx.enter_context(nc.psum_tensor("turn_ps", [P, D], F32))
        proj_ps = ctx.enter_context(nc.psum_tensor("proj_ps", [P, 3, W], F32))
        kind_ps = ctx.enter_context(nc.psum_tensor("kind_ps", [P, 2, W], F32))

        consts_in = sem("consts_in")
        w_in_sem = [sem(f"w_landed{g}") for g in range(6)]
        x_in = sem("x_in")
        sum_done = sem("sum_done")
        mean_done = sem("mean_done")
        rstd_done = sem("rstd_done")
        a_done = sem("a_done")
        turn_done = sem("turn_done")
        aT_done = sem("aT_done")
        proj_done = sem("proj_done")
        rot_done = sem("rot_done")
        rows_done = [sem(f"rows_done{k}") for k in range(6)]
        rows_turned = [sem(f"rows_turned{k}") for k in range(4)]
        turned_done = [sem(f"turned_done{k}") for k in range(4)]
        rows_out = [sem(f"rows_out{k}") for k in range(6)]
        turned_out = [sem(f"turned_out{k}") for k in range(4)]
        tile_stored = sem("tile_stored")
        block = ctx.enter_context(nc.Block())

        @block.sync
        def _(sp):
            sp.dma_start(gain[:, :], bass.AP(g_mix.tensor, 0, [[0, P], [1, D]])).then_inc(consts_in, 16)
            sp.dma_start(rope_tab[:, :, :], rope.rearrange("(t p) c -> p t c", p=P)).then_inc(consts_in, 16)
            for g in range(6):
                sp.dma_start(weights[:, :, g * W:(g + 1) * W],
                             w_in[:, g * W:(g + 1) * W].rearrange("(k p) n -> p k n", p=P)).then_inc(w_in_sem[g], 16)
            prime(sp, tile_stored)
            with sp.Fori(0, T) as t:
                for k in (KD, VD, KS, VS):
                    sp.wait_ge(rows_done[k], t + 2)
                    sp.dma_start(new_rows[k][bass.ds(t * P, P), :], rows[:, k, :]).then_inc(rows_out[k], 16)
                for k in (QD, KD, QS, KS):
                    n = TURNED[k]
                    wait_apart(sp, const, turned_done[n], t + 2)
                    sp.dma_start(qk_turned[n, :, :, bass.ds(t, 1), :].rearrange("c p a k -> p c (a k)"),
                                 turned[:, n, :].rearrange("p (c k) -> p c k", k=P)).then_inc(turned_out[n], 16)
                for k in (KD, VD, KS, VS):
                    sp.wait_ge(rows_out[k], t * 16 + 16)
                for n in range(4):
                    sp.wait_ge(turned_out[n], t * 16 + 16)
                sp.sem_inc(tile_stored, 1)

        @block.gpsimd
        def _(pool):
            with pool.Fori(0, T) as t:
                pool.wait_ge(a_done, t + 1)
                pool.dma_start(x[:, :], x_all[bass.ds(t * P, P), :]).then_inc(x_in, 16)
                pool.wait_ge(mean_done, t + 1)
                nc.gpsimd.tensor_tensor(stat[:, 2:3], stat[:, 1:2], const.minus_half, ALU.pow).then_inc(rstd_done, 1)

        @block.tensor
        def _(pe):
            prime(pe, turn_done, *rows_turned)
            with pe.Fori(0, T) as t:
                pe.wait_ge(a_done, t + 2)
                for k in range(KC):
                    last = nc.tensor.transpose(turn_ps[:, k * P:(k + 1) * P], a[:, k * P:(k + 1) * P], const.ident)
                last.then_inc(turn_done, 1)
                pe.wait_ge(aT_done, t + 1)

                def project(g):
                    pe.wait_ge(w_in_sem[g], 16)
                    pe.wait_ge(rows_done[(g + 3) % 6], t + 1 + g // 3)
                    for k in range(KC):
                        mm = nc.tensor.matmul(proj_ps[:, g % 3, :], aT[:, k, :], weights[:, k, g * W:(g + 1) * W],
                                              start=(k == 0), stop=(k == KC - 1))
                    mm.then_inc(proj_done, 1)

                def turn(kind):
                    n = TURNED[kind]
                    pe.wait_ge(rows_done[kind], t + 2)
                    pe.wait_ge(turned_done[(n + 2) % 4], t + 1 + n // 2)
                    for c in range(4):
                        mm = nc.tensor.transpose(kind_ps[:, n % 2, c * P:(c + 1) * P],
                                                 rows[:, kind, c * P:(c + 1) * P], const.ident)
                    mm.then_inc(rows_turned[n], 1)

                project(QD)
                project(KD)
                project(VD)
                turn(QD)
                project(QS)
                turn(KD)
                project(KS)
                project(VS)
                turn(QS)
                turn(KS)

        @block.scalar
        def _(act):
            prime(act, *(rows_done[g] for g in (VD, QS, KS, VS)), turned_done[2], turned_done[3])
            with act.Fori(0, T) as t:
                act.wait_ge(turn_done, t + 2)
                nc.scalar.copy(aT[:, :, :].rearrange("p k n -> p (k n)"), turn_ps[:, :]).then_inc(aT_done, 1)
                for g in (VD, QS, KS, VS):
                    act.wait_ge(proj_done, t * 6 + (g + 1))
                    if g != QS:
                        act.wait_ge(tile_stored, t + 1)
                    if g in TURNED:
                        act.wait_ge(rows_turned[TURNED[g]], t + 1)
                    nc.scalar.mul(rows[:, g, :], proj_ps[:, g % 3, :],
                                  0.125 if g == QS else 1.0).then_inc(rows_done[g], 1)
                for n in (2, 3):
                    act.wait_ge(rows_turned[n], t + 2)
                    act.wait_ge(tile_stored, t + 1)
                    nc.scalar.copy(turned[:, n, :], kind_ps[:, n % 2, :]).then_inc(turned_done[n], 1)

        @block.vector
        def _(dve):
            prime(dve, a_done, rows_done[QD], rows_done[KD], turned_done[0], turned_done[1])
            with dve.Fori(0, T) as t:
                dve.wait_ge(x_in, t * 16 + 16)
                nc.vector.tensor_tensor_reduce(squares[:, :], x[:, :], x[:, :], 1.0, 0.0, ALU.mult, ALU.add,
                                               stat[:, 0:1]).then_inc(sum_done, 1)
                dve.wait_ge(sum_done, t + 1)
                nc.vector.tensor_scalar(stat[:, 1:2], stat[:, 0:1], 1.0 / D, EPS, ALU.mult, ALU.add).then_inc(mean_done, 1)
                dve.wait_ge(rstd_done, t + 1)
                dve.wait_ge(consts_in, 32)
                dve.wait_ge(turn_done, t + 1)
                nc.vector.scalar_tensor_tensor(a[:, :], x[:, :], stat[:, 2:3], gain[:, :],
                                               ALU.mult, ALU.mult).then_inc(a_done, 1)
                for g in (QD, KD):
                    dve.wait_ge(proj_done, t * 6 + (g + 1))
                    src = proj_ps[:, g % 3, :].rearrange("p (h c d) -> p h c d", c=2, d=16)
                    out = rot[:, 1, :].rearrange("p (h c d) -> p h c d", c=2, d=16)
                    both = rot[:, 0, :].rearrange("p (h d) -> p h d", d=32)
                    cos = rope_tab[:, bass.ds(t, 1), 0:32].broadcast_to((P, 16, 32))
                    nc.vector.tensor_tensor(both, proj_ps[:, g % 3, :].rearrange("p (h d) -> p h d", d=32), cos,
                                            ALU.mult)
                    for c in range(2):
                        sin = rope_tab[:, bass.ds(t, 1), 32 + 16 * c:48 + 16 * c].broadcast_to((P, 16, 16))
                        mm = nc.vector.tensor_tensor(out[:, :, c, :], src[:, :, 1 - c, :], sin, ALU.mult)
                    mm.then_inc(rot_done, 1)
                    dve.wait_ge(rot_done, t * 2 + (g + 1))
                    if g == KD:
                        dve.wait_ge(tile_stored, t + 1)
                    dve.wait_ge(rows_turned[g], t + 1)
                    nc.vector.tensor_tensor(rows[:, g, :], rot[:, 0, :], rot[:, 1, :], ALU.add).then_inc(rows_done[g], 1)
                    dve.wait_ge(rows_done[g], t + 2)
                for n in (0, 1):
                    dve.wait_ge(rows_turned[n], t + 2)
                    dve.wait_ge(tile_stored, t + 1)
                    nc.vector.tensor_scalar(turned[:, n, :], kind_ps[:, n % 2, :], 32 ** -0.5 if n == 0 else 1.0,
                                            None, ALU.mult).then_inc(turned_done[n], 1)


def attend_samples(nc, const, ins, qk_turned, new_rows, heads):
    B, S, PAST = 8, 16, 256
    KEYS = PAST + S
    with ExitStack() as ctx:
        def sb(name, shape, dt=F32):
            return ctx.enter_context(nc.sbuf_tensor(name, shape, dt))

        sem = stage_semaphores(nc, ctx)

        cached = sb("cached", [P, 2, 2, 2, W])
        values = sb("values", [P, 2, 2, 3, W])
        qT = sb("qT", [P, 2, 4, P])
        newT = sb("newT", [P, 2, 4, P])
        kT = sb("kT", [P, 2, 4, KEYS])
        queries = sb("queries", [P, 3, 4, P])
        half_mask = sb("half_mask", [P, 3, 4, 8])
        head_mask = sb("head_mask", [P, W])
        fold = sb("fold", [P, S])
        late_mask = sb("late_mask", [P, S])
        prob = sb("sprob", [P, 2, KEYS])
        soft = sb("ssoft", [P, KEYS])
        stick = sb("sstick", [P, KEYS])
        zeros = sb("szeros", [P, KEYS])
        wT = sb("swT", [P, 2, 3 * P])
        own = sb("own", [P, 2, W])
        neg_max = sb("sneg_max", [P, 2])
        total = sb("stotal", [P, 2])
        share = sb("sshare", [P, 2])
        out_rows = sb("out_rows", [S, 2, D])
        k_ps = ctx.enter_context(nc.psum_tensor("k_ps", [P, 2, W], F32))
        score_ps = ctx.enter_context(nc.psum_tensor("sscore_ps", [P, 3, W], F32))
        turn_ps = ctx.enter_context(nc.psum_tensor("sturn_ps", [P, W], F32))
        mix_ps = ctx.enter_context(nc.psum_tensor("mix_ps", [P, W], F32))
        fold_ps = ctx.enter_context(nc.psum_tensor("fold_ps", [P, W], F32))

        tables_in = sem("tables_in")
        batch_in = [sem(f"batch_in{u}") for u in range(2)]
        zeroed = sem("zeroed")
        k_turned = sem("k_turned")
        k_taken = sem("k_taken")
        new_taken = sem("new_taken")
        queries_done = sem("queries_done")
        scores_done = sem("sscores_done")
        max_done = sem("smax_done")
        prob_done = sem("sprob_done")
        share_done = sem("sshare_done")
        part_done = sem("spart_done")
        weights_done = sem("sweights_done")
        abs_done = sem("sabs_done")
        exp_done = sem("sexp_done")
        log_done = sem("slog_done")
        soft_done = sem("ssoft_done")
        scan_done = sem("sscan_done")
        expo_done = sem("sexpo_done")
        stick_done = sem("sstick_done")
        w_turned = sem("sw_turned")
        wT_done = sem("swT_done")
        mixed = sem("mixed")
        own_done = sem("own_done")
        folded = sem("folded")
        taken = sem("taken")
        stored = [sem(f"sstored{u}") for u in range(2)]
        stored_free = sem("stored_free")
        block = ctx.enter_context(nc.Block())

        def batches(eng, body):
            with eng.Fori(0, B // 2) as r:
                for u in range(2):
                    body(r, u, 2 * r + u)

        @block.sync
        def _(sp):
            for a, name in ((half_mask[:, :, :, :].rearrange("p a c h -> p (a c h)"), "half_mask"),
                            (head_mask[:, :], "head_mask"), (fold[:, :], "fold"), (late_mask[:, :], "late_mask")):
                sp.dma_start(a, ins[name]).then_inc(tables_in, 16)
            for kind in range(2):
                for dst, place in ((qT, 2 * kind), (newT, 2 * kind + 1)):
                    sp.dma_start(dst[:, kind, :, :], qk_turned[place, :, :, TP, :].rearrange("c p k -> p c k")
                                 ).then_inc(tables_in, 16)

            def load(r, u, b):
                sp.wait_ge(mixed, 2 * b + 2)
                for kind, (k, v, rows) in enumerate((("cache_diff_k", "cache_diff_v", VD), ("cache_sb_k", "cache_sb_v", VS))):
                    for dst, name in ((cached[:, u, kind, :, :], k), (values[:, u, kind, 0:2, :], v)):
                        sp.dma_start(dst, ins[name][bass.ds(b, 1), :, :]
                                     .rearrange("a (j p) n -> p (a j) n", p=P)).then_inc(batch_in[u], 16)
                    sp.dma_start(values[0:S, u, kind, 2, :],
                                 new_rows[rows][bass.ds(TP * P + b * S, S), :]).then_inc(batch_in[u], 16)
            batches(sp, load)

        @block.gpsimd
        def _(pool):
            prime(pool, stored_free, by=1)

            def store(r, u, b):
                pool.wait_ge(taken, 2 * b + 6)
                pool.dma_start(heads[bass.ds(b * S, S), :], out_rows[:, u, :]).then_inc(stored[u], 16)
                pool.wait_ge(stored[u], 16 * r + 16)
                pool.sem_inc(stored_free, 1)
            batches(pool, store)
            for u in range(2):
                pool.wait_ge(stored[u], 16 * (B // 2))

        @block.tensor
        def _(pe):
            prime(pe, mixed, by=4)
            prime(pe, scores_done, by=3)
            prime(pe, w_turned, by=2)
            prime(pe, folded, by=2)

            def batch(r, u, b):
                pe.wait_ge(batch_in[u], 96 * r + 96)
                for kind in range(2):
                    for blk in range(2):
                        m = 2 * kind + blk
                        pe.wait_ge(k_taken, 4 * b + m + 1)
                        for c in range(4):
                            mm = nc.tensor.transpose(k_ps[:, m % 2, c * P:(c + 1) * P],
                                                     cached[:, u, kind, blk, c * P:(c + 1) * P], const.ident)
                        mm.then_inc(k_turned, 1)
                for j in range(3):
                    kind = j // 2
                    pe.wait_ge(k_taken, 4 * b + 2 * kind + 4)
                    pe.wait_ge(new_taken, 2 * b + kind + 1)
                    pe.wait_ge(queries_done, 3 * b + j + 1)
                    if j < 2:
                        pe.wait_ge(prob_done, 2 * b + j + 1)
                    else:
                        pe.wait_ge(expo_done, b + 1)
                    for c in range(4):
                        mm = nc.tensor.matmul(score_ps[:, j, 0:KEYS], queries[:, j, c, :], kT[:, kind, c, :],
                                              start=(c == 0), stop=(c == 3 and j < 2))
                    if j == 2:
                        mm = nc.tensor.matmul(score_ps[:, j, PAST:KEYS], const.ident, late_mask[:, :],
                                              start=False, stop=True)
                    mm.then_inc(scores_done, 1)
                for kind, w, ready in ((0, prob[:, 0, :], weights_done), (1, stick[:, :], stick_done)):
                    pe.wait_ge(ready, b + 1)
                    pe.wait_ge(wT_done, 4 * b + 2 * kind + 1)
                    for k in range(3):
                        n = min(P, KEYS - k * P)
                        mm = nc.tensor.transpose(turn_ps[0:n, k * P:(k + 1) * P], w[:, k * P:k * P + n], const.ident)
                    mm.then_inc(w_turned, 1)
                    pe.wait_ge(wT_done, 4 * b + 2 * kind + 3)
                    pe.wait_ge(own_done, 2 * b + kind + 1)
                    for k in range(3):
                        n = min(P, KEYS - k * P)
                        mm = nc.tensor.matmul(mix_ps[:, :], wT[0:n, kind, k * P:(k + 1) * P],
                                              values[0:n, u, kind, k, :], start=(k == 0), stop=(k == 2))
                    mm.then_inc(mixed, 1)
                    pe.wait_ge(own_done, 2 * b + kind + 2)
                    pe.wait_ge(taken, 2 * b + kind + 4)
                    nc.tensor.matmul(fold_ps[0:S, :], fold[:, :], own[:, kind, :],
                                     start=True, stop=True).then_inc(folded, 1)
            batches(pe, batch)

        @block.scalar
        def _(act):
            prime(act, prob_done, by=2)
            prime(act, k_taken, by=2)
            prime(act, wT_done, by=1)
            prime(act, taken, by=4)

            def batch(r, u, b):
                for m in range(4):
                    act.wait_ge(k_turned, 4 * b + m + 1)
                    act.wait_ge(scores_done, 3 * b + 3)
                    nc.scalar.copy(kT[:, m // 2, :, (m % 2) * P:(m % 2 + 1) * P],
                                   k_ps[:, m % 2, :].rearrange("p (c n) -> p c n", n=P)).then_inc(k_taken, 1)
                for c in range(2):
                    act.wait_ge(max_done, 2 * b + c + 1)
                    act.wait_ge(w_turned, 2 * b + 1)
                    nc.scalar.activation(prob[:, c, :], score_ps[:, c, 0:KEYS], ACT.Exp, bias=neg_max[:, c:c + 1],
                                         accum_out=total[:, c:c + 1]).then_inc(prob_done, 1)
                act.wait_ge(scores_done, 3 * b + 6)
                act.wait_ge(scan_done, b + 1)
                nc.scalar.activation(soft[:, :], score_ps[:, 2, 0:KEYS], ACT.Abs).then_inc(abs_done, 1)
                act.wait_ge(abs_done, b + 1)
                nc.scalar.activation(soft[:, :], soft[:, :], ACT.Exp, scale=-1.0).then_inc(exp_done, 1)
                act.wait_ge(exp_done, b + 1)
                nc.scalar.activation(soft[:, :], soft[:, :], ACT.Ln, bias=const.one).then_inc(log_done, 1)
                for kind in range(2):
                    if kind == 1:
                        act.wait_ge(expo_done, b + 2)
                        nc.scalar.activation(stick[:, :], stick[:, :], ACT.Exp).then_inc(stick_done, 1)
                    act.wait_ge(w_turned, 2 * b + kind + 3)
                    act.wait_ge(mixed, 2 * b + kind + 3)
                    nc.scalar.copy(wT[:, kind, 0:2 * P], turn_ps[:, 0:2 * P]).then_inc(wT_done, 1)
                    nc.scalar.copy(wT[0:S, kind, 2 * P:3 * P], turn_ps[0:S, 2 * P:3 * P]).then_inc(wT_done, 1)
                    act.wait_ge(folded, 2 * b + kind + 3)
                    act.wait_ge(stored_free, b + 1)
                    nc.scalar.copy(out_rows[:, u, kind * W:(kind + 1) * W], fold_ps[0:S, :]).then_inc(taken, 1)
            batches(act, batch)

        @block.vector
        def _(dve):
            prime(dve, expo_done, scan_done, own_done)
            nc.vector.memset(zeros[:, :], 0.0).then_inc(zeroed, 1)
            dve.wait_ge(zeroed, 1)
            dve.wait_ge(tables_in, 8 * 16)

            def batch(r, u, b):
                at = bass.ds(b * S, S)
                dve.wait_ge(scores_done, 3 * b + 3)
                for kind in range(2):
                    nc.vector.tensor_copy(kT[:, kind, :, PAST:KEYS], newT[:, kind, :, at]).then_inc(new_taken, 1)
                for j in range(3):
                    nc.vector.tensor_tensor(
                        queries[:, j, :, :].rearrange("p c (h q) -> p c h q", q=S),
                        qT[:, j // 2, :, at].unsqueeze(2).broadcast_to((P, 4, 8, S)),
                        half_mask[:, j, :, :].unsqueeze(3).broadcast_to((P, 4, 8, S)), ALU.mult).then_inc(queries_done, 1)
                for c in range(2):
                    dve.wait_ge(scores_done, 3 * b + c + 4)
                    nc.vector.tensor_reduce(neg_max[:, c:c + 1], score_ps[:, c, 0:KEYS], AX.X, ALU.max,
                                            negate=True).then_inc(max_done, 1)
                dve.wait_ge(prob_done, 2 * b + 4)
                nc.vector.reciprocal(share[:, :], total[:, :]).then_inc(share_done, 1)
                dve.wait_ge(share_done, b + 1)
                nc.vector.tensor_scalar(prob[:, 1, :], prob[:, 1, :], share[:, 1:2], const.lam,
                                        ALU.mult, ALU.mult).then_inc(part_done, 1)
                dve.wait_ge(part_done, b + 1)
                nc.vector.scalar_tensor_tensor(prob[:, 0, :], prob[:, 0, :], share[:, 0:1], prob[:, 1, :],
                                               ALU.mult, ALU.subtract).then_inc(weights_done, 1)
                z = score_ps[:, 2, 0:KEYS]
                dve.wait_ge(log_done, b + 1)
                nc.vector.scalar_tensor_tensor(soft[:, :], z, 0.0, soft[:, :], ALU.max, ALU.add).then_inc(soft_done, 1)
                dve.wait_ge(soft_done, b + 1)
                dve.wait_ge(w_turned, 2 * b + 2)
                nc.vector.tensor_tensor_scan(stick[:, ::-1], soft[:, ::-1], zeros[:, :], 0.0,
                                             ALU.add, ALU.add).then_inc(scan_done, 1)
                dve.wait_ge(scan_done, b + 2)
                nc.vector.tensor_tensor(stick[:, :], z, stick[:, :], ALU.subtract).then_inc(expo_done, 1)
                for kind in range(2):
                    dve.wait_ge(mixed, 2 * b + kind + 5)
                    dve.wait_ge(folded, 2 * b + kind + 1)
                    nc.vector.tensor_tensor(own[:, kind, :], mix_ps[:, :], head_mask[:, :], ALU.mult).then_inc(own_done, 1)
            batches(dve, batch)


HEADS, TOP, SIDE = 8, 16, 128
ROWS = HEADS * TOP
U_RING, V_RING, DIAGS = 4, 8, 4
V_AHEAD = V_RING + TOP
ATTEND = 1


def tile_at(position):
    return TP if position == 0 else position - 1


def attend_and_sum_experts(nc, const, ins, qk_turned, new_rows, heads, summed):
    with ExitStack() as ctx:
        def sb(name, shape, dt=F32):
            return ctx.enter_context(nc.sbuf_tensor(name, shape, dt))

        def psum(name, shape):
            return ctx.enter_context(nc.psum_tensor(name, shape, F32))

        sem = stage_semaphores(nc, ctx)

        w_out = sb("w_out_sb", [P, KC, D])
        w_query = sb("w_query_sb", [P, KC, 2 * D])
        u_rows = [sb(f"u_rows{n}", [P, D]) for n in range(U_RING)]
        v_rows = [sb(f"v_rows{n}", [P, D]) for n in range(V_RING)]
        c_rows = sb("c_rows", [P, D])
        idx_u = sb("idx_u", [P, 2, TOP], U32)
        idx_v = sb("idx_v", [P, 2, TOP], U32)
        gate_now = sb("gate_now", [P, 2, TOP])
        dots = sb("dots", [P, 2, TOP])
        gelus = sb("gelus", [P, 2, TOP])
        coef = sb("coef", [P, 2, TOP])
        diag = sb("diag", [P, DIAGS, P])
        keysT = sb("keysT", [P, 2, P])
        gain = sb("ffn_gain", [P, D])
        sub_gain = sb("sub_gain", [P, 64])
        steps16 = sb("steps16", [P, TOP])
        x = sb("rx", [P, D])
        mix = sb("mix", [P, D])
        qd = sb("qd", [P, 4, P])
        qs = sb("qs", [P, 2, P])
        neg_max = sb("neg_max", [P, 4])
        total = sb("total", [P, 4])
        share = sb("share", [P, 4])
        arena = sb("arena", [P, 9, D])

        def place(n, size=D, at=0):
            return arena[:, n:n + -(-(at + size) // D), :].rearrange("p a n -> p (a n)")[:, at:at + size]

        kd, ks, vd, vs = (place(n).rearrange("p (j k) -> p j k", k=P) for n in range(4))
        prob = [place(4 + n) for n in range(4)]
        soft = (prob[1], prob[0])
        stick = (prob[3], prob[2])
        wT = place(8)

        c = place(0)
        query = place(1).rearrange("p (a n) -> p a n", n=W)
        scores = place(2, 2 * D).rearrange("p (m n) -> p m n", n=SIDE)
        spare = place(4, 2 * D).rearrange("p (m n) -> p m n", n=SIDE)
        work = place(4)
        inT = place(6).rearrange("p (k n) -> p k n", n=P)
        keys = inT[:, 0:2, :]
        top, pos, posf, picked_at = (place(7, 2 * ROWS, at=2 * ROWS * n) for n in range(4))
        top = top.rearrange("p (m a) -> p m a", a=TOP)
        pos = pos.bitcast(U32).rearrange("p (m a) -> p m a", a=TOP)
        posf = posf.rearrange("p (m a) -> p m a", a=TOP)
        picked = picked_at.rearrange("p (s h k) -> p s h k", s=2, k=TOP)
        val = place(6, ROWS).rearrange("p (h k) -> p h k", k=TOP)
        sel = place(6, ROWS, at=ROWS).bitcast(U32).rearrange("p (h k) -> p h k", k=TOP)
        part = place(6, 2 * ROWS, at=2 * ROWS).bitcast(U32).rearrange("p (s h k) -> p s h k", s=2, k=TOP)
        partf = place(6, 2 * ROWS, at=4 * ROWS).rearrange("p (s h k) -> p s h k", s=2, k=TOP)
        expo = place(6, ROWS, at=6 * ROWS).rearrange("p (h k) -> p h k", k=TOP)
        queryT = place(8).rearrange("p (a n) -> p a n", n=W)
        sum_out = place(8)
        idx_tile = sb("idx_tile", [P, ROWS], U32)
        gate_tile = sb("gate_tile", [P, ROWS])
        stat = sb("rstat", [P, 4, 8])
        sum_ps = psum("sum_ps", [P, D])
        z_ps = psum("z_ps", [P, 2, D])
        group_ps = psum("group_ps", [P, W])
        out_ps = psum("out_ps", [P, W])
        turn_ps, acc_ps = z_ps[:, 0, :], z_ps[:, 1, :].rearrange("p (a n) -> p a n", n=W)
        qT_ps, score_ps = group_ps, out_ps

        tables_in = sem("rtables_in")
        out_w_in = sem("out_w_in")
        query_w_in = sem("query_w_in")
        x_in = sem("rx_in")
        mix_in = sem("mix_in")
        keys_turned = sem("keys_turned")
        keys_done = sem("keys_done")
        self_done = sem("rself_done")
        mean_done = sem("rmean_done")
        rstd_done = sem("rrstd_done")
        mix_done = sem("mix_done")
        turned = sem("rturned")
        inT_done = sem("inT_done")
        acc_done = sem("acc_done")
        h_done = sem("h_done")
        c_done = sem("c_done")
        query_done = sem("query_done")
        query_turned = sem("query_turned")
        queryT_done = sem("queryT_done")
        scored = sem("scored")
        scores_done = sem("rscores_done")
        shifted = sem("shifted")
        raised = sem("raised")
        idx_done = sem("idx_done")
        gates_done = sem("gates_done")
        idx_taken = sem("idx_taken")
        idx_moved = sem("idx_moved")
        gates_taken = sem("gates_taken")
        c_taken = sem("c_taken")
        opened = sem("opened")
        u_in = [sem(f"u_in{n}") for n in range(U_RING)]
        v_in = [sem(f"v_in{n}") for n in range(V_RING)]
        u_used = sem("u_used")
        v_used = sem("v_used")
        gelu_done = sem("gelu_done")
        coef_done = sem("coef_done")
        diag_done = sem("diag_done")
        sum_taken = sem("sum_taken")
        sum_stored = sem("sum_stored")
        cleared = sem("cleared")
        kd_in = sem("kd_in")
        ks_in = sem("ks_in")
        vd_in = sem("vd_in")
        vs_in = sem("vs_in")
        z_done = sem("z_done")
        max_done = sem("max_done")
        prob_done = sem("prob_done")
        share_done = sem("share_done")
        part_done = sem("part_done")
        weights_done = sem("weights_done")
        abs_done = sem("abs_done")
        exp_done = sem("exp_done")
        log_done = sem("log_done")
        soft_done = sem("soft_done")
        scan_done = sem("scan_done")
        expo_done = sem("expo_done")
        stick_done = sem("stick_done")
        w_turned = sem("w_turned")
        wT_done = sem("wT_done")
        out_done = sem("out_done")
        rows_taken = sem("rows_taken")
        block = ctx.enter_context(nc.Block())

        def groups(i):
            return [(a, min(a + 4, i + 1)) for a in range(0, i + 1, 4)]

        def groups_before(i, m, h):
            return sum(16 * len(groups(j)) for j in range(i)) + (4 * m + h) * len(groups(i))

        def attending_steps(eng, e, body):
            with eng.Fori(0, 2) as r:
                for b in range(2):
                    body(2 * r + b, b)

        def last_steps(eng, body):
            with eng.Fori(0, 3) as r:
                for b in range(2):
                    body(HEADS * TP + 2 * r + (b + 1), 2 * r + (b + 1), 1 - b)

        SELF = 35

        @block.sync
        def _(sp):
            for dst, src in ((gain[:, :], bass.AP(ins["g_ffn"].tensor, 0, [[0, P], [1, D]])),
                             (sub_gain[:, :], bass.AP(ins["g_subln"].tensor, 0, [[0, P], [1, 64]])),
                             (steps16[:, :], ins["steps16"]),
                             (keys[:, :, :], ins["sub_keys"].rearrange("s n d -> n s d"))):
                sp.dma_start(dst, src).then_inc(tables_in, 16)
            sp.dma_start(x[:, :], ins["x_all"][TP * P:T * P, :]).then_inc(x_in, 16)
            sp.dma_start(mix[:, :], heads).then_inc(mix_in, 16)
            sp.dma_start(w_out[:, :, :], ins["w_out"].rearrange("(k p) n -> p k n", p=P)).then_inc(out_w_in, 16)
            sp.dma_start(w_query[:, :, :], ins["w_query"].rearrange("(k p) n -> p k n", p=P)).then_inc(query_w_in, 16)

            sp.wait_ge(cleared, 2)
            for e in range(TP):
                i = tile_at(e + 1)
                sp.wait_ge(gates_done, e + 2)
                sp.wait_ge(c_taken, e + 1)

                def load(m, b):
                    n = 4 * i + m
                    wait_apart(sp, const, z_done, 6 * n + 4)
                    sp.dma_start(kd[:, 0:i + 1, :], qk_turned[1, bass.ds(m, 1), :, 0:i + 1, :]
                                 .rearrange("a p j k -> (a p) j k")).then_inc(kd_in, 16)
                    for a in range(4):
                        sp.dma_start(qd[a * 32:(a + 1) * 32, a, :],
                                     qk_turned[0, bass.ds(m, 1), a * 32:(a + 1) * 32, i, :]
                                     .rearrange("a p k -> (a p) k")).then_inc(kd_in, 16)
                    wait_apart(sp, const, z_done, 6 * n + 6)
                    sp.dma_start(ks[:, 0:i + 1, :], qk_turned[3, bass.ds(m, 1), :, 0:i + 1, :]
                                 .rearrange("a p j k -> (a p) j k")).then_inc(ks_in, 16)
                    for a in range(2):
                        sp.dma_start(qs[a * 64:(a + 1) * 64, a, :],
                                     qk_turned[2, bass.ds(m, 1), a * 64:(a + 1) * 64, i, :]
                                     .rearrange("a p k -> (a p) k")).then_inc(ks_in, 16)
                    for v, kind, landed, over in ((vd, VD, vd_in, 2), (vs, VS, vs_in, 4)):
                        wait_apart(sp, const, out_done, 4 * n + over)
                        sp.dma_start(v[:, 0:i + 1, :], new_rows[kind][0:(i + 1) * P, bass.ds(m * P, P)]
                                     .rearrange("(j p) d -> p j d", p=P)).then_inc(landed, 16)
                attending_steps(sp, e, load)
                sp.wait_ge(opened, e + 1)
                sp.dma_start(x[:, :], ins["x_all"][i * P:(i + 1) * P, :]).then_inc(x_in, 16)
            sp.wait_ge(sum_stored, 16 * T)

        @block.gpsimd
        def _(pool):
            def power(t, n):
                width = (8, 1)[n]
                pool.wait_ge(mean_done, 2 * t + (n + 1))
                nc.gpsimd.tensor_tensor(stat[:, 2, 0:width], stat[:, 1, 0:width],
                                        const.minus_half.broadcast_to((P, width)), ALU.pow).then_inc(rstd_done, 1)

            def take_idx(e, n, s, u):
                wait_apart(pool, const, v_used, n * TOP - 2 * TOP + V_AHEAD)
                nc.gpsimd.tensor_copy(idx_v[:, 1 - u, :], idx_u[:, 1 - u, :]).then_inc(idx_moved, 1)
                take_idx_u(e, n, s, u)
                pool.wait_ge(idx_moved, n)

            def take_idx_u(e, n, s, u):
                pool.wait_ge(idx_done, e + 2)
                nc.gpsimd.tensor_copy(idx_u[:, u, :], idx_tile[:, bass.ds(s * TOP, TOP)]).then_inc(idx_taken, 1)
                pool.wait_ge(idx_taken, n + 1)

            def gather_u(n, u, k):
                wait_apart(pool, const, u_used, n * TOP + (k + 1))
                pool.indirect_dma_start(u_rows[k % U_RING][:, :], None, ins["expert_u"],
                                        bass.IndirectOffsetOnAxis(ap=idx_u[:, u, k:k + 1], axis=0)
                                        ).then_inc(u_in[k % U_RING], 16)

            def gather_v(n, u, k):
                wait_apart(pool, const, v_used, n * TOP + (k + 1))
                pool.indirect_dma_start(v_rows[k % V_RING][:, :], None, ins["expert_v"],
                                        bass.IndirectOffsetOnAxis(ap=idx_v[:, 1 - u, k:k + 1], axis=0)
                                        ).then_inc(v_in[k % V_RING], 16)

            def gather(n, u, first, end):
                for k in range(first, end):
                    gather_u(n, u, k)
                    gather_v(n, u, k)

            def take_gates(e, n, s, u):
                wait_apart(pool, const, gates_done, e + 2)
                nc.gpsimd.tensor_copy(gate_now[:, u, :], gate_tile[:, bass.ds(s * TOP, TOP)]).then_inc(gates_taken, 1)

            def step(e, n, s, u):
                take_idx(e, n, s, u)
                gather(n, u, 0, 3)
                take_gates(e, n, s, u)
                gather(n, u, 3, TOP)

            nc.gpsimd.memset(qd[:, :, :], 0.0).then_inc(cleared, 1)
            nc.gpsimd.memset(qs[:, :, :], 0.0).then_inc(cleared, 1)
            for n in range(2):
                power(0, n)
            for e in range(TP):
                if e == 0:
                    take_idx_u(0, 0, 0, 0)
                    for k in range(TOP):
                        gather_u(0, 0, k)
                    take_gates(0, 0, 0, 0)
                else:
                    step(e, HEADS * e, 0, 0)
                attending_steps(pool, e, lambda m, b: step(e, HEADS * e + (m + ATTEND), m + ATTEND, 1 - b))
                n = HEADS * e + 5
                take_idx(e, n, 5, 1)
                gather(n, 1, 0, 3)
                take_gates(e, n, 5, 1)
                gather(n, 1, 3, 6)
                power(e + 1, 0)
                gather(n, 1, 6, 14)
                power(e + 1, 1)
                gather(n, 1, 14, TOP)
                step(e, n + 1, 6, 0)
                step(e, n + 2, 7, 1)
            step(TP, HEADS * TP, 0, 0)
            last_steps(pool, lambda n, s, u: step(TP, n, s, u))
            step(TP, HEADS * T - 1, HEADS - 1, 1)
            pool.wait_ge(v_used, HEADS * T * TOP - 2 * TOP + V_AHEAD)
            nc.gpsimd.tensor_copy(idx_v[:, 1, :], idx_u[:, 1, :]).then_inc(idx_moved, 1)
            pool.wait_ge(idx_moved, HEADS * T)
            for k in range(TOP):
                gather_v(HEADS * T, 0, k)

        @block.tensor
        def _(pe):
            pe.wait_ge(tables_in, 64)
            for s in range(2):
                mm = nc.tensor.transpose(qT_ps[:, s * P:(s + 1) * P], keys[:, s, :], const.ident)
            mm.then_inc(keys_turned, 1)
            prime(pe, turned, by=2)
            prime(pe, scored, query_turned, by=4)
            prime(pe, v_used, by=V_AHEAD)
            prime(pe, z_done, by=6)
            prime(pe, out_done, by=4)
            prime(pe, w_turned)
            pe.wait_ge(keys_done, 1)

            def turn(src, ready, t, n):
                pe.wait_ge(*ready)
                for k in range(KC):
                    mm = nc.tensor.transpose(turn_ps[:, k * P:(k + 1) * P], src[:, k * P:(k + 1) * P], const.ident)
                mm.then_inc(turned, 1)
                pe.wait_ge(inT_done, 2 * t + n)

            def product(weights, half, bank):
                for k in range(KC):
                    mm = nc.tensor.matmul(acc_ps[:, bank, :], inT[:, k, :], weights[:, k, half * W:(half + 1) * W],
                                          start=(k == 0), stop=(k == KC - 1))
                mm.then_inc(acc_done, 1)

            def project_heads(t):
                turn(mix, (mix_done, t + 1), t, 1)
                pe.wait_ge(out_w_in, 16)
                pe.wait_ge(query_done, 4 * t + 4)
                for n in range(2):
                    product(w_out, n, n)

            def queries(t, g):
                if g == 0:
                    turn(c, (c_done, t + 2), t, 2)
                    pe.wait_ge(query_w_in, 16)
                if g < 2:
                    pe.wait_ge(h_done, t + 2)
                else:
                    pe.wait_ge(query_done, 4 * t + (g + 3))
                product(w_query, g, g % 2)

            def match(t, g):
                pe.wait_ge(query_done, 4 * t + (g + 5))
                pe.wait_ge(queryT_done, 4 * t + (g + 4))
                for m in range(4):
                    mm = nc.tensor.transpose(qT_ps[:, m * P:(m + 1) * P],
                                             query[:, g % 2, m * P:(m + 1) * P], const.ident)
                mm.then_inc(query_turned, 1)
                pe.wait_ge(queryT_done, 4 * t + (g + 5))
                pe.wait_ge(scores_done, 4 * t + (g + 4))
                for m in range(4):
                    mm = nc.tensor.matmul(score_ps[:, m * P:(m + 1) * P], queryT[:, g % 2, m * P:(m + 1) * P],
                                          keysT[:, m % 2, :], start=True, stop=True)
                mm.then_inc(scored, 1)

            def open_sum(e):
                pe.wait_ge(h_done, e + 2)
                pe.wait_ge(sum_taken, e + 1)
                for n in range(2):
                    mm = nc.tensor.matmul(sum_ps[:, n * W:(n + 1) * W], const.ident, x[:, n * W:(n + 1) * W],
                                          start=True, stop=False, skip_group_check=True)
                mm.then_inc(opened, 1)

            def add_rows(step, first=0, end=TOP):
                n = step - 1
                for k in range(first, end):
                    pe.wait_ge(v_in[k % V_RING], n * (TOP // V_RING * 16) + (k // V_RING + 1) * 16)
                    pe.wait_ge(diag_done, n * TOP + (k + 1))
                    for half in range(2):
                        mm = nc.tensor.matmul(sum_ps[:, half * W:(half + 1) * W], diag[:, k % DIAGS, :],
                                              v_rows[k % V_RING][:, half * W:(half + 1) * W],
                                              start=False, stop=(k == TOP - 1), skip_group_check=True)
                    mm.then_inc(v_used, 1)

            def attention_scores(i, j, n):
                width = (i + 1) * P
                if j < 2:
                    pe.wait_ge(expo_done, 2 * n + (j + 1))
                else:
                    pe.wait_ge(prob_done, 4 * n + (j - 1))
                if j == 0:
                    pe.wait_ge(kd_in, 80 * n + 80)
                if j == 4:
                    pe.wait_ge(ks_in, 48 * n + 48)
                q, kt, mask = (qd[:, j, :], kd, const.chunk_mask) if j < 4 else (qs[:, j - 4, :], ks, const.strict_mask)
                for a in range(0, width, W):
                    w = min(W, width - a)
                    nc.tensor.matmul(z_ps[:, j % 2, a:a + w], q, kt.rearrange("p j k -> p (j k)")[:, a:a + w],
                                     start=True, stop=a + w < width)
                nc.tensor.matmul(z_ps[:, j % 2, i * P:width], const.ident, mask, start=False, stop=True
                                 ).then_inc(z_done, 1)

            def turn_weights(i, m, h, n):
                if h < 2:
                    pe.wait_ge(weights_done, 2 * n + (h + 1))
                else:
                    pe.wait_ge(stick_done, 2 * n + (h - 1))
                src = prob[2 * h] if h < 2 else stick[h - 2]
                for g, (a, z) in enumerate(groups(i)):
                    pe.wait_ge(wT_done, groups_before(i, m, h) + (g + 1))
                    for k in range(a, z):
                        mm = nc.tensor.transpose(group_ps[:, (k - a) * P:(k - a + 1) * P],
                                                 src[:, k * P:(k + 1) * P], const.ident)
                    mm.then_inc(w_turned, 1)

            def weigh_values(i, m, h, n):
                if h % 2 == 0:
                    pe.wait_ge(rows_taken, 2 * n + (h // 2 + 1))
                    pe.wait_ge((vd_in, vs_in)[h // 2], 16 * n + 16)
                pe.wait_ge(wT_done, groups_before(i, m, h) + (len(groups(i)) + 1))
                v = vd if h < 2 else vs
                for k in range(i + 1):
                    mm = nc.tensor.matmul(out_ps[:, 64 * h:64 * h + 64], wT[:, k * P:(k + 1) * P],
                                          v[:, k, 64 * (h % 2):64 * (h % 2) + 64], start=(k == 0), stop=(k == i))
                mm.then_inc(out_done, 1)

            def attending_step(e, m, b):
                i = tile_at(e + 1)
                n = 4 * i + m
                step = HEADS * e + (m + ATTEND)
                attention_scores(i, 0, n)
                attention_scores(i, 1, n)
                add_rows(step, 0, 2)
                attention_scores(i, 2, n)
                add_rows(step, 2, 3)
                attention_scores(i, 3, n)
                add_rows(step, 3, 4)
                attention_scores(i, 4, n)
                add_rows(step, 4, 6)
                attention_scores(i, 5, n)
                add_rows(step, 6, 7)
                turn_weights(i, m, 0, n)
                add_rows(step, 7, 9)
                weigh_values(i, m, 0, n)
                turn_weights(i, m, 1, n)
                add_rows(step, 9, 11)
                weigh_values(i, m, 1, n)
                add_rows(step, 11, 12)
                turn_weights(i, m, 2, n)
                add_rows(step, 12, 13)
                weigh_values(i, m, 2, n)
                add_rows(step, 13, 15)
                turn_weights(i, m, 3, n)
                add_rows(step, 15, 16)
                weigh_values(i, m, 3, n)

            def route_queries(t):
                for g in range(4):
                    queries(t, g)
                    if g:
                        match(t, g - 1)
                match(t, 3)

            project_heads(0)
            route_queries(0)
            for e in range(TP):
                if e:
                    add_rows(HEADS * e)
                open_sum(e)
                pe.wait_ge(scores_done, 4 * e + 8)
                attending_steps(pe, e, lambda m, b: attending_step(e, m, b))
                step, t = HEADS * e + 5, e + 1
                add_rows(step, 0, 6)
                project_heads(t)
                add_rows(step, 6, TOP)
                queries(t, 0)
                add_rows(step + 1, 0, 2)
                queries(t, 1)
                add_rows(step + 1, 2, 4)
                match(t, 0)
                queries(t, 2)
                add_rows(step + 1, 4, 7)
                match(t, 1)
                queries(t, 3)
                add_rows(step + 1, 7, 10)
                match(t, 2)
                match(t, 3)
                add_rows(step + 1, 10, TOP)
                add_rows(step + 2)
            add_rows(HEADS * TP)
            open_sum(TP)
            last_steps(pe, lambda n, s, u: add_rows(n))
            add_rows(HEADS * T - 1)
            add_rows(HEADS * T)

        @block.scalar
        def _(act):
            prime(act, query_done, queryT_done, scores_done, by=4)
            prime(act, sum_taken, wT_done)
            prime(act, rows_taken, by=2)
            act.wait_ge(keys_turned, 1)
            nc.scalar.copy(keysT[:, :, :].rearrange("p s n -> p (s n)"), qT_ps[:, 0:2 * P]).then_inc(keys_done, 1)

            def take_turned(t, n):
                act.wait_ge(turned, 2 * t + (n + 3))
                nc.scalar.copy(inT[:, :, :].rearrange("p k n -> p (k n)"), turn_ps).then_inc(inT_done, 1)

            def take_query(t, g):
                act.wait_ge(acc_done, 6 * t + (g + 3))
                act.wait_ge(query_turned, 4 * t + (g + 3))
                nc.scalar.copy(query[:, g % 2, :], acc_ps[:, g % 2, :]).then_inc(query_done, 1)

            def take_scores(t, g):
                act.wait_ge(query_turned, 4 * t + (g + 5))
                act.wait_ge(scored, 4 * t + (g + 3))
                nc.scalar.copy(queryT[:, g % 2, :], qT_ps[:, :]).then_inc(queryT_done, 1)
                act.wait_ge(scored, 4 * t + (g + 5))
                if g == 0:
                    act.wait_ge(idx_done, t + 1)
                nc.scalar.copy(scores[:, 4 * g:4 * g + 4, :].rearrange("p m n -> p (m n)"),
                               score_ps[:, :]).then_inc(scores_done, 1)

            def exponents(t):
                act.wait_ge(shifted, t + 1)
                nc.scalar.activation(expo[:, :, :], expo[:, :, :], ACT.Exp).then_inc(raised, 1)

            def take_tokens(e):
                act.wait_ge(c_done, e + 2)
                act.wait_ge(u_used, e * ROWS + U_RING)
                nc.scalar.copy(c_rows[:, :], c).then_inc(c_taken, 1)

            def raise_products(step, u):
                act.wait_ge(u_used, step * TOP + U_RING)
                nc.scalar.activation(gelus[:, 1 - u, :], dots[:, 1 - u, :], ACT.Gelu).then_inc(gelu_done, 1)

            def spread(step, u, first=0, end=TOP):
                if first == 0:
                    act.wait_ge(coef_done, step)
                for k in range(first, end):
                    act.wait_ge(v_used, step * TOP + (k + 1 - DIAGS + V_RING))
                    nc.scalar.mul(diag[:, k % DIAGS, :], const.ident, coef[:, 1 - u, k:k + 1]).then_inc(diag_done, 1)

            def close_sum(e):
                act.wait_ge(v_used, e * ROWS + (ROWS + V_AHEAD))
                nc.scalar.copy(sum_out, sum_ps[:, :]).then_inc(sum_taken, 1)
                act.wait_ge(sum_taken, e + 2)
                act.dma_start(summed[tile_at(e)], sum_out).then_inc(sum_stored, 16)

            def softmax_top(i, c, m, n):
                act.wait_ge(max_done, 4 * n + (c + 1))
                if c < 2:
                    act.wait_ge(scan_done, 2 * n + (2 - c))
                else:
                    act.wait_ge(w_turned, groups_before(i, m, 0) + 1)
                width = (i + 1) * P
                nc.scalar.activation(prob[c][:, 0:width], z_ps[:, c % 2, 0:width], ACT.Exp,
                                     bias=neg_max[:, c:c + 1], accum_out=total[:, c:c + 1]).then_inc(prob_done, 1)

            def log_term(i, s, n):
                act.wait_ge(z_done, 6 * n + (11 + s))
                act.wait_ge(weights_done, 2 * n + 1)
                u = soft[s][:, 0:(i + 1) * P]
                nc.scalar.activation(u, z_ps[:, s, 0:(i + 1) * P], ACT.Abs).then_inc(abs_done, 1)
                act.wait_ge(abs_done, 2 * n + (s + 1))
                nc.scalar.activation(u, u, ACT.Exp, scale=-1.0).then_inc(exp_done, 1)
                act.wait_ge(exp_done, 2 * n + (s + 1))
                nc.scalar.activation(u, u, ACT.Ln, bias=const.one).then_inc(log_done, 1)

            def take_weights(i, m, h, n):
                act.wait_ge(out_done, 4 * n + (h + 4))
                for g, (a, z) in enumerate(groups(i)):
                    act.wait_ge(w_turned, groups_before(i, m, h) + (g + 2))
                    nc.scalar.copy(wT[:, a * P:z * P], group_ps[:, 0:(z - a) * P]).then_inc(wT_done, 1)

            def take_out(kind, m, n):
                act.wait_ge(out_done, 4 * n + (2 * kind + 6))
                nc.scalar.copy(mix[:, bass.ds(m * P + kind * W, P)], out_ps[:, kind * P:(kind + 1) * P]
                               ).then_inc(rows_taken, 1)

            def raise_stick(i, s, n):
                act.wait_ge(expo_done, 2 * n + (s + 3))
                e = stick[s][:, 0:(i + 1) * P]
                nc.scalar.activation(e, e, ACT.Exp).then_inc(stick_done, 1)

            def attending_step(e, m, b):
                i = tile_at(e + 1)
                n = 4 * i + m
                step, u = HEADS * e + (m + ATTEND), 1 - b
                softmax_top(i, 0, m, n)
                softmax_top(i, 1, m, n)
                spread(step, u, 0, 4)
                softmax_top(i, 2, m, n)
                softmax_top(i, 3, m, n)
                spread(step, u, 4, 7)
                log_term(i, 0, n)
                spread(step, u, 7, 9)
                take_weights(i, m, 0, n)
                log_term(i, 1, n)
                spread(step, u, 9, 11)
                take_weights(i, m, 1, n)
                spread(step, u, 11, 12)
                take_out(0, m, n)
                raise_stick(i, 0, n)
                spread(step, u, 12, 13)
                take_weights(i, m, 2, n)
                spread(step, u, 13, 15)
                raise_stick(i, 1, n)
                spread(step, u, 15, TOP)
                raise_products(step + 1, 1 - u)
                take_weights(i, m, 3, n)
                take_out(1, m, n)

            def plain_step(step, u):
                spread(step, u)
                raise_products(step + 1, 1 - u)

            def route_queries(t):
                take_turned(t, 1)
                for g in range(4):
                    take_query(t, g)
                    if g:
                        take_scores(t, g - 1)
                take_scores(t, 3)

            take_turned(0, 0)
            route_queries(0)
            exponents(0)
            for e in range(TP):
                take_tokens(e)
                if e:
                    plain_step(HEADS * e, 0)
                    close_sum(e - 1)
                    act.wait_ge(sum_stored, 16 * e)
                else:
                    raise_products(1, 1)
                attending_steps(act, e, lambda m, b: attending_step(e, m, b))
                step, t = HEADS * e + 5, e + 1
                spread(step, 1, 0, 7)
                take_turned(t, 0)
                spread(step, 1, 7, TOP)
                raise_products(step + 1, 0)
                take_turned(t, 1)
                take_query(t, 0)
                spread(step + 1, 0, 0, 3)
                take_query(t, 1)
                spread(step + 1, 0, 3, 5)
                take_scores(t, 0)
                take_query(t, 2)
                spread(step + 1, 0, 5, 8)
                take_scores(t, 1)
                take_query(t, 3)
                spread(step + 1, 0, 8, 11)
                take_scores(t, 2)
                take_scores(t, 3)
                spread(step + 1, 0, 11, TOP)
                raise_products(step + 2, 1)
                spread(step + 2, 1, 0, 11)
                exponents(t)
                spread(step + 2, 1, 11, TOP)
                raise_products(step + 3, 0)
            take_tokens(TP)
            plain_step(HEADS * TP, 0)
            close_sum(TP - 1)
            last_steps(act, lambda n, s, u: plain_step(n, u))
            plain_step(HEADS * T - 1, 1)
            spread(HEADS * T, 0)
            act.wait_ge(sum_stored, 16 * TP)
            close_sum(TP)

        @block.vector
        def _(dve):
            prime(dve, h_done, c_done, idx_done, gates_done)
            prime(dve, u_used, by=U_RING)
            prime(dve, expo_done, scan_done, by=2)
            dve.wait_ge(tables_in, 64)
            at = [0]

            def chain(t, done):
                at[0] += 1
                done.then_inc(self_done, 1)
                wait_apart(dve, const, self_done, t * SELF + at[0])

            def by_head(a):
                return a.rearrange("p (h d) -> p h d", d=64)

            def norm_heads(t):
                at[0] = 0
                if t == 0:
                    dve.wait_ge(mix_in, 16)
                else:
                    dve.wait_ge(rows_taken, 8 * t + 2)
                diff = mix[:, 0:W]
                chain(t, nc.vector.tensor_tensor(work[:, 0:W], diff, diff, ALU.mult))
                chain(t, nc.vector.tensor_reduce(stat[:, 0, :], by_head(work[:, 0:W]), AX.X, ALU.add))
                nc.vector.tensor_scalar(stat[:, 1, :], stat[:, 0, :], 1.0 / 64, 1e-5, ALU.mult,
                                        ALU.add).then_inc(mean_done, 1)
                dve.wait_ge(rstd_done, 2 * t + 1)
                chain(t, nc.vector.tensor_tensor(by_head(work[:, 0:W]), by_head(diff),
                                                 stat[:, 2, :].unsqueeze(2).broadcast_to((P, 8, 64)), ALU.mult))
                nc.vector.scalar_tensor_tensor(by_head(diff), by_head(work[:, 0:W]), 1.0 - LAMBDA_START,
                                               sub_gain[:, :].unsqueeze(1).broadcast_to((P, 8, 64)),
                                               ALU.mult, ALU.mult).then_inc(mix_done, 1)

            def norm_tokens(t):
                dve.wait_ge(x_in, t * 16 + 16)
                dve.wait_ge(acc_done, 6 * t + 2)
                nc.vector.tensor_tensor(x[:, :], x[:, :], acc_ps[:, :, :].rearrange("p a n -> p (a n)"),
                                        ALU.add).then_inc(h_done, 1)
                dve.wait_ge(h_done, t + 2)
                chain(t, nc.vector.tensor_tensor_reduce(work, x[:, :], x[:, :], 1.0, 0.0, ALU.mult, ALU.add,
                                                        stat[:, 0, 0:1]))
                nc.vector.tensor_scalar(stat[:, 1, 0:1], stat[:, 0, 0:1], 1.0 / D, EPS,
                                        ALU.mult, ALU.add).then_inc(mean_done, 1)
                dve.wait_ge(rstd_done, 2 * t + 2)
                if t:
                    dve.wait_ge(c_taken, t)
                nc.vector.scalar_tensor_tensor(c, x[:, :], stat[:, 2, 0:1], gain[:, :],
                                               ALU.mult, ALU.mult).then_inc(c_done, 1)

            def best8(t, src, rest, vals):
                n = src.shape[1]
                for m in range(n):
                    last = nc.vector.max(vals[:, m, 0:8], src[:, m, :])
                chain(t, last)
                for m in range(n):
                    last = nc.vector.match_replace(rest[:, m, :], vals[:, m, 0:8], src[:, m, :], -3e38)
                chain(t, last)

            def next8(t, src, rest, vals, places):
                n = src.shape[1]
                for m in range(n):
                    last = nc.vector.max(vals[:, m, 8:16], rest[:, m, :])
                for m in range(n):
                    last = nc.vector.max_index(places[:, m, 0:8], vals[:, m, 0:8], src[:, m, :])
                chain(t, last)
                for m in range(n):
                    last = nc.vector.max_index(places[:, m, 8:16], vals[:, m, 8:16], rest[:, m, :])
                chain(t, last)

            wide = scores[:, :, :].rearrange("p m n -> p (m n)")
            spare_wide = spare[:, :, :].rearrange("p m n -> p (m n)")
            of_sums = (wide.rearrange("p (h n) -> p h n", h=HEADS), spare_wide.rearrange("p (h n) -> p h n", h=HEADS),
                       val[:, :, :])

            def best_sides(t, g):
                wait_apart(dve, const, scores_done, 4 * t + (5 + g))
                of = tuple(a[:, 4 * g:4 * g + 4, :] for a in (scores, spare, top))
                best8(t, *of)
                next8(t, *of, pos[:, 4 * g:4 * g + 4, :])

            def begin_sums(t):
                sides = top[:, :, :].rearrange("p (h s) a -> p h s a", s=2)
                grid = wide.rearrange("p (h a b) -> p h a b", a=TOP, b=TOP)
                chain(t, nc.vector.tensor_tensor(grid, sides[:, :, 0, :].unsqueeze(3).broadcast_to((P, HEADS, TOP, TOP)),
                                                 sides[:, :, 1, :].unsqueeze(2).broadcast_to((P, HEADS, TOP, TOP)),
                                                 ALU.add))

                best8(t, *of_sums)

            def places_of_sums(t):
                next8(t, *of_sums, sel[:, :, :])
                nc.vector.tensor_tensor(expo[:, :, :], val[:, :, :], val[:, :, 0:1].broadcast_to((P, HEADS, TOP)),
                                        ALU.subtract).then_inc(shifted, 1)
                nc.vector.tensor_scalar(part[:, 0, :, :], sel[:, :, :], 4, None, ALU.logical_shift_right)

            def key_of_side(t, s):
                if s == 0:
                    nc.vector.tensor_copy(posf[:, :, :], pos[:, :, :])
                    chain(t, nc.vector.tensor_scalar(part[:, 1, :, :], sel[:, :, :], 15, None, ALU.bitwise_and))
                    chain(t, nc.vector.tensor_copy(partf[:, :, :, :], part[:, :, :, :]))
                keys_at = posf[:, :, :].rearrange("p (h s) a -> p h s a", s=2)
                buf = (wide, spare_wide)[s].rearrange("p (h k a) -> p h k a", k=TOP, a=TOP)
                hk = buf.rearrange("p h k a -> p (h k) a")
                chain(t, nc.vector.tensor_tensor(
                    hk, partf[:, s, :, :].rearrange("p h k -> p (h k)").unsqueeze(2).broadcast_to((P, P, TOP)),
                    steps16[:, :].unsqueeze(1).broadcast_to((P, P, TOP)), ALU.is_equal))
                chain(t, nc.vector.tensor_tensor(buf, buf, keys_at[:, :, s, :].unsqueeze(2)
                                                 .broadcast_to((P, HEADS, TOP, TOP)), ALU.mult))
                last = nc.vector.tensor_reduce(picked[:, s, :, :].rearrange("p h k -> p (h k)"), hk, AX.X, ALU.add)
                if s:
                    chain(t, last)

            def experts_of_keys(t):
                chain(t, nc.vector.scalar_tensor_tensor(picked[:, 0, :, :], picked[:, 0, :, :], float(SIDE),
                                                        picked[:, 1, :, :], ALU.mult, ALU.add))
                if t:
                    dve.wait_ge(idx_taken, HEADS * t)
                nc.vector.tensor_copy(idx_tile[:, :], picked[:, 0, :, :].rearrange("p h k -> p (h k)")
                                      ).then_inc(idx_done, 1)

            def gates(t):
                dve.wait_ge(raised, t + 1)
                chain(t, nc.vector.tensor_reduce(stat[:, 0, :], expo[:, :, :], AX.X, ALU.add))
                chain(t, nc.vector.reciprocal(stat[:, 3, :], stat[:, 0, :]))
                if t:
                    dve.wait_ge(gates_taken, HEADS * t)
                nc.vector.tensor_tensor(gate_tile[:, :].rearrange("p (h k) -> p h k", k=TOP),
                                        expo[:, :, :], stat[:, 3, :].unsqueeze(2).broadcast_to((P, HEADS, TOP)),
                                        ALU.mult).then_inc(gates_done, 1)
                assert at[0] == SELF, at[0]

            def reduce(n, b, first=0, end=TOP):
                for k in range(first, end):
                    dve.wait_ge(u_in[k % U_RING], n * (TOP // U_RING * 16) + (k // U_RING + 1) * 16)
                    row = u_rows[k % U_RING][:, :]
                    nc.vector.tensor_tensor_reduce(row, row, c_rows[:, :], 1.0, 0.0, ALU.mult, ALU.add,
                                                   dots[:, b, k:k + 1]).then_inc(u_used, 1)

            def weigh(n, u):
                dve.wait_ge(gates_taken, n)
                dve.wait_ge(gelu_done, n)
                nc.vector.tensor_tensor(coef[:, 1 - u, :], gelus[:, 1 - u, :], gate_now[:, 1 - u, :],
                                        ALU.mult).then_inc(coef_done, 1)

            def plain_step(n, u):
                reduce(n, u, 0, 1)
                weigh(n, u)
                reduce(n, u, 1, TOP)

            def maximum(i, c, n):
                dve.wait_ge(z_done, 6 * n + (c + 7))
                nc.vector.tensor_reduce(neg_max[:, c:c + 1], z_ps[:, c % 2, 0:(i + 1) * P], AX.X, ALU.max,
                                        negate=True).then_inc(max_done, 1)

            def subtract_half(i, h, n):
                dve.wait_ge(prob_done, 4 * n + (2 * h + 2))
                nc.vector.reciprocal(share[:, 2 * h:2 * h + 2], total[:, 2 * h:2 * h + 2]).then_inc(share_done, 1)
                dve.wait_ge(share_done, 2 * n + (h + 1))
                b2 = prob[2 * h + 1][:, 0:(i + 1) * P]
                nc.vector.tensor_scalar(b2, b2, share[:, 2 * h + 1:2 * h + 2], const.lam,
                                        ALU.mult, ALU.mult).then_inc(part_done, 1)
                dve.wait_ge(part_done, 2 * n + (h + 1))
                b1 = prob[2 * h][:, 0:(i + 1) * P]
                nc.vector.scalar_tensor_tensor(b1, b1, share[:, 2 * h:2 * h + 1], b2,
                                               ALU.mult, ALU.subtract).then_inc(weights_done, 1)

            def break_stick(i, m, s, n):
                width = (i + 1) * P
                z, u, e = z_ps[:, s, 0:width], soft[s][:, 0:width], stick[s][:, 0:width]
                dve.wait_ge(log_done, 2 * n + (s + 1))
                nc.vector.scalar_tensor_tensor(u, z, 0.0, u, ALU.max, ALU.add).then_inc(soft_done, 1)
                dve.wait_ge(soft_done, 2 * n + (s + 1))
                if s == 1:
                    dve.wait_ge(w_turned, groups_before(i, m, 2) + 1)
                nc.vector.tensor_tensor_scan(e[:, ::-1], u[:, ::-1], const.zero.broadcast_to((P, width)), 0.0,
                                             ALU.add, ALU.add).then_inc(scan_done, 1)
                dve.wait_ge(scan_done, 2 * n + (s + 3))
                nc.vector.tensor_tensor(e, z, e, ALU.subtract).then_inc(expo_done, 1)

            def attending_step(e, m, b):
                i = tile_at(e + 1)
                n = 4 * i + m
                rows, u = HEADS * e + (m + ATTEND), 1 - b
                reduce(rows, u, 0, 1)
                weigh(rows, u)
                reduce(rows, u, 1, 2)
                maximum(i, 0, n)
                reduce(rows, u, 2, 3)
                maximum(i, 1, n)
                reduce(rows, u, 3, 5)
                maximum(i, 2, n)
                reduce(rows, u, 5, 6)
                maximum(i, 3, n)
                reduce(rows, u, 6, 7)
                subtract_half(i, 0, n)
                reduce(rows, u, 7, 9)
                subtract_half(i, 1, n)
                reduce(rows, u, 9, 11)
                break_stick(i, m, 0, n)
                reduce(rows, u, 11, 14)
                break_stick(i, m, 1, n)
                reduce(rows, u, 14, TOP)

            norm_heads(0)
            norm_tokens(0)
            for g in range(4):
                best_sides(0, g)
            begin_sums(0)
            places_of_sums(0)
            for s in range(2):
                key_of_side(0, s)
            experts_of_keys(0)
            gates(0)
            for e in range(TP):
                dve.wait_ge(c_taken, e + 1)
                if e:
                    plain_step(HEADS * e, 0)
                else:
                    reduce(0, 0)
                attending_steps(dve, e, lambda m, b: attending_step(e, m, b))
                n, t = HEADS * e + 5, e + 1
                reduce(n, 1, 0, 1)
                weigh(n, 1)
                reduce(n, 1, 1, 4)
                norm_heads(t)
                reduce(n, 1, 4, 12)
                norm_tokens(t)
                reduce(n, 1, 12, TOP)
                reduce(n + 1, 0, 0, 1)
                weigh(n + 1, 0)
                reduce(n + 1, 0, 1, 8)
                best_sides(t, 0)
                reduce(n + 1, 0, 8, 10)
                best_sides(t, 1)
                reduce(n + 1, 0, 10, 13)
                best_sides(t, 2)
                reduce(n + 1, 0, 13, 15)
                best_sides(t, 3)
                reduce(n + 1, 0, 15, TOP)
                reduce(n + 2, 1, 0, 1)
                weigh(n + 2, 1)
                reduce(n + 2, 1, 1, 2)
                begin_sums(t)
                reduce(n + 2, 1, 2, 5)
                places_of_sums(t)
                reduce(n + 2, 1, 5, 8)
                key_of_side(t, 0)
                reduce(n + 2, 1, 8, 11)
                key_of_side(t, 1)
                experts_of_keys(t)
                reduce(n + 2, 1, 11, 14)
                gates(t)
                reduce(n + 2, 1, 14, TOP)
            dve.wait_ge(c_taken, T)
            plain_step(HEADS * TP, 0)
            last_steps(dve, lambda n, s, u: plain_step(n, u))
            plain_step(HEADS * T - 1, 1)
            weigh(HEADS * T, 0)


def finish(nc, const, ins, summed, y):
    with ExitStack() as ctx:
        def sb(name, shape, dt=F32):
            return ctx.enter_context(nc.sbuf_tensor(name, shape, dt))

        sem = stage_semaphores(nc, ctx)

        w_gate = sb("w_gate_sb", [P, KC, D])
        w_ple = sb("w_ple_sb", [P, 2, D])
        gains = sb("gains", [P, 2, D])
        h = [sb(f"fh{u}", [P, D]) for u in range(2)]
        p_rows = [sb(f"p_rows{u}", [P, 2, P]) for u in range(2)]
        pT = sb("pT", [P, 2, P])
        b = sb("fb", [P, D])
        bT = sb("bT", [P, KC, P])
        gate = sb("fgate", [P, D])
        squares = sb("fsquares", [P, D])
        y_sb = sb("y_sb", [P, D])
        stat = sb("fstat", [P, 2, 4])
        turn_ps = ctx.enter_context(nc.psum_tensor("fturn_ps", [P, D], F32))
        p_ps = ctx.enter_context(nc.psum_tensor("p_ps", [P, 2, P], F32))
        gate_ps = ctx.enter_context(nc.psum_tensor("gate_ps", [P, D], F32))
        ple_ps = ctx.enter_context(nc.psum_tensor("ple_ps", [P, D], F32))

        tables_in = sem("ftables_in")
        gate_w_in = sem("gate_w_in")
        ple_w_in = sem("ple_w_in")
        tile_in = [sem(f"ftile_in{u}") for u in range(2)]
        squared = sem("fsquared")
        mean_done = sem("fmean_done")
        rstd_done = sem("frstd_done")
        b_done = sem("b_done")
        turned = sem("fturned")
        taken = sem("ftaken")
        gate_summed = sem("gate_summed")
        ple_summed = sem("ple_summed")
        gate_done = sem("gate_done")
        mixed = sem("fmixed")
        added = sem("fadded")
        y_done = sem("y_done")
        y_out = sem("y_out")
        y_free = sem("y_free")
        block = ctx.enter_context(nc.Block())

        def tiles(eng, body):
            body(0, 0, None)
            with eng.Fori(0, TP // 2) as r:
                for u in (1, 2):
                    body(2 * r + u, u % 2, r)


        @block.sync
        def _(sp):
            for n, name in enumerate(("g_ple", "g_final")):
                sp.dma_start(gains[:, n, :], bass.AP(ins[name].tensor, 0, [[0, P], [1, D]])).then_inc(tables_in, 16)
            sp.dma_start(h[0][:, :], summed[0]).then_inc(tile_in[0], 16)
            sp.dma_start(p_rows[0][:, :, :].rearrange("p c n -> p (c n)"), ins["p_all"][0:P, :]).then_inc(tile_in[0], 16)
            sp.dma_start(w_ple[:, :, :], ins["w_ple"].rearrange("(k p) n -> p k n", p=P)).then_inc(ple_w_in, 16)
            sp.dma_start(w_gate[:, :, :], ins["w_pgate"].rearrange("(k p) n -> p k n", p=P)).then_inc(gate_w_in, 16)
            prime(sp, y_free)

            def store(t):
                sp.wait_ge(y_done, t + 2)
                sp.dma_start(y[bass.ds(t * P, P), :], y_sb[:, :]).then_inc(y_out, 16)
                sp.wait_ge(y_out, t * 16 + 16)
                sp.sem_inc(y_free, 1)

            with sp.Fori(0, TP // 2) as r:
                for u in (1, 2):
                    t = 2 * r + u
                    sp.wait_ge(y_done, t)
                    sp.dma_start(h[u % 2][:, :], summed[bass.ds(t, 1), :, :].rearrange("a p n -> (a p) n")
                                 ).then_inc(tile_in[u % 2], 16)
                    sp.dma_start(p_rows[u % 2][:, :, :].rearrange("p c n -> p (c n)"),
                                 ins["p_all"][bass.ds(t * P, P), :]).then_inc(tile_in[u % 2], 16)
                    store(t - 1)
            store(TP)

        @block.gpsimd
        def _(pool):
            def power(n, count):
                pool.wait_ge(mean_done, count)
                nc.gpsimd.tensor_tensor(stat[:, n, 2:3], stat[:, n, 1:2], const.minus_half, ALU.pow).then_inc(rstd_done, 1)

            power(0, 1)
            with pool.Fori(0, TP // 2) as r:
                for u in (1, 2):
                    t = 2 * r + u
                    power(0, 2 * t)
                    power(1, 2 * t + 1)
            power(1, 2 * T)

        @block.tensor
        def _(pe):
            prime(pe, turned, by=2)
            prime(pe, gate_summed)

            def tile(t, u, r):
                pe.wait_ge(tile_in[u], 32 if r is None else 32 * r + (32 if u else 64))
                pe.wait_ge(taken, 2 * t + 1)
                for k in range(2):
                    mm = nc.tensor.transpose(p_ps[:, k, :], p_rows[u][:, k, :], const.ident)
                mm.then_inc(turned, 1)
                pe.wait_ge(b_done, t + 1)
                for k in range(KC):
                    mm = nc.tensor.transpose(turn_ps[:, k * P:(k + 1) * P], b[:, k * P:(k + 1) * P], const.ident)
                mm.then_inc(turned, 1)
                pe.wait_ge(taken, 2 * t + 2)
                pe.wait_ge(ple_w_in, 16)
                pe.wait_ge(mixed, t + 1)
                for n in range(2):
                    for k in range(2):
                        mm = nc.tensor.matmul(ple_ps[:, n * W:(n + 1) * W], pT[:, k, :], w_ple[:, k, n * W:(n + 1) * W],
                                              start=(k == 0), stop=(k == 1))
                mm.then_inc(ple_summed, 1)
                pe.wait_ge(taken, 2 * t + 3)
                pe.wait_ge(gate_w_in, 16)
                pe.wait_ge(gate_done, t + 1)
                for n in range(2):
                    for k in range(KC):
                        mm = nc.tensor.matmul(gate_ps[:, n * W:(n + 1) * W], bT[:, k, :], w_gate[:, k, n * W:(n + 1) * W],
                                              start=(k == 0), stop=(k == KC - 1))
                mm.then_inc(gate_summed, 1)
            tiles(pe, tile)

        @block.scalar
        def _(act):
            prime(act, taken, gate_done)

            def tile(t, u, r):
                act.wait_ge(turned, 2 * t + 3)
                act.wait_ge(gate_summed, t + 1)
                nc.scalar.copy(pT[:, :, :], p_ps[:, :, :]).then_inc(taken, 1)
                act.wait_ge(turned, 2 * t + 4)
                nc.scalar.copy(bT[:, :, :].rearrange("p k n -> p (k n)"), turn_ps[:, :]).then_inc(taken, 1)
                act.wait_ge(gate_summed, t + 2)
                act.wait_ge(mixed, t + 1)
                nc.scalar.activation(gate[:, :], gate_ps[:, :], ACT.Sigmoid).then_inc(gate_done, 1)
            tiles(act, tile)

        @block.vector
        def _(dve):
            prime(dve, mixed, y_done)
            dve.wait_ge(tables_in, 32)

            def norm(n, u, dst, done, count, free=None):
                nc.vector.tensor_tensor_reduce(squares[:, :], h[u][:, :], h[u][:, :], 1.0, 0.0, ALU.mult, ALU.add,
                                               stat[:, n, 0:1]).then_inc(squared, 1)
                dve.wait_ge(squared, count)
                nc.vector.tensor_scalar(stat[:, n, 1:2], stat[:, n, 0:1], 1.0 / D, EPS,
                                        ALU.mult, ALU.add).then_inc(mean_done, 1)
                dve.wait_ge(rstd_done, count)
                if free:
                    dve.wait_ge(*free)
                nc.vector.scalar_tensor_tensor(dst, h[u][:, :], stat[:, n, 2:3], gains[:, n, :],
                                               ALU.mult, ALU.mult).then_inc(done, 1)

            def close(t, u, count):
                dve.wait_ge(gate_done, t + 2)
                dve.wait_ge(ple_summed, t + 1)
                nc.vector.tensor_tensor(squares[:, :], gate[:, :], ple_ps[:, :], ALU.mult).then_inc(mixed, 1)
                dve.wait_ge(mixed, t + 2)
                nc.vector.tensor_tensor(h[u][:, :], h[u][:, :], squares[:, :], ALU.add).then_inc(added, 1)
                dve.wait_ge(added, t + 1)
                norm(1, u, y_sb[:, :], y_done, count, (y_free, t + 1))

            dve.wait_ge(tile_in[0], 32)
            norm(0, 0, b[:, :], b_done, 1)
            with dve.Fori(0, TP // 2) as r:
                for u in (1, 2):
                    t = 2 * r + u
                    wait_apart(dve, const, tile_in[u % 2], 32 * r + 32 * u)
                    dve.wait_ge(turned, 2 * t + 2)
                    norm(0, u % 2, b[:, :], b_done, 2 * t)
                    close(t - 1, 1 - u % 2, 2 * t + 1)
            close(TP, 0, 2 * T)


def shape_constants():
    import numpy as np

    pos = np.concatenate([np.arange(TP * P), np.tile(256 + np.arange(16), 8)]).astype(np.float32)
    inv = np.float32(10000.0) ** (-np.arange(0, 32, 2, dtype=np.float32) / np.float32(32))
    ang = pos[:, None] * inv[None, :].astype(np.float32)
    cos, sin = np.cos(ang), np.sin(ang)
    q, k = np.arange(P)[:, None], np.arange(P)[None, :]
    at, chunk, head = np.arange(P)[:, None, None], np.arange(4)[None, :, None], np.arange(8)[None, None, :]
    own_head = head == 2 * chunk + at // 64
    own_half = np.stack([own_head & (at % 64 < 32), own_head & (at % 64 >= 32), own_head], axis=1)
    return {
        "rope": np.concatenate([cos, cos, -sin, sin], axis=1).astype(np.float32),
        "steps16": np.tile(np.arange(16, dtype=np.float32), (P, 1)),
        "identity": np.eye(P, dtype=np.float32),
        "chunk_mask": np.where(k // 64 > q // 64, HIDDEN, 0).astype(np.float32),
        "strict_mask": np.where(k >= q, HIDDEN, 0).astype(np.float32),
        "half_mask": own_half.astype(np.float32).reshape(P, -1),
        "head_mask": (q // 16 == np.arange(W)[None, :] // 64).astype(np.float32),
        "fold": (q % 16 == np.arange(16)[None, :]).astype(np.float32),
        "late_mask": np.where(np.arange(16)[None, :] >= q % 16, HIDDEN, 0).astype(np.float32),
    }


HIDDEN = -1e30
LAMBDA_START = 0.8 - 0.6


class Const:
    pass


def load_constants(nc, ctx, ins):
    c = Const()
    c.ident = ctx.enter_context(nc.sbuf_tensor("ident", [P, P], F32))[:, :]
    c.chunk_mask = ctx.enter_context(nc.sbuf_tensor("chunk_mask", [P, P], F32))[:, :]
    c.strict_mask = ctx.enter_context(nc.sbuf_tensor("strict_mask", [P, P], F32))[:, :]
    c.one = ctx.enter_context(nc.sbuf_tensor("one", [P, 1], F32))[:, :]
    c.zero = ctx.enter_context(nc.sbuf_tensor("zero", [P, 1], F32))[:, :]
    c.lam = ctx.enter_context(nc.sbuf_tensor("lam", [P, 1], F32))[:, :]
    vectors = ctx.enter_context(nc.sbuf_tensor("lambda_vectors", [P, 2, 64], F32))
    sums = ctx.enter_context(nc.sbuf_tensor("lambda_sums", [P, 2], F32))
    raised = ctx.enter_context(nc.semaphore("lambda_raised"))
    c.minus_half = ctx.enter_context(nc.sbuf_tensor("minus_half", [P, 1], F32))[:, :]
    loaded = ctx.enter_context(nc.semaphore("shared_loaded"))
    filled = ctx.enter_context(nc.semaphore("shared_filled"))
    c.passed = {e.engine: ctx.enter_context(nc.semaphore(f"passed{n}"))
                for n, e in enumerate((nc.vector, nc.gpsimd, nc.sync))}
    with nc.Block() as block:
        @block.sync
        def _(sp):
            for dst, name in ((c.ident, "identity"), (c.chunk_mask, "chunk_mask"), (c.strict_mask, "strict_mask")):
                sp.dma_start(dst, ins[name]).then_inc(loaded, 16)
            sp.dma_start(vectors[:, :, :].rearrange("p a d -> p (a d)"),
                         bass.AP(ins["lambdas"].tensor, 0, [[0, P], [1, P]])).then_inc(loaded, 16)

        @block.vector
        def _(dve):
            nc.vector.memset(c.minus_half, -0.5)
            nc.vector.memset(c.one, 1.0)
            nc.vector.memset(c.zero, 0.0)
            dve.wait_ge(loaded, 64)
            nc.vector.tensor_tensor(vectors[:, 0, :], vectors[:, 0, :], vectors[:, 1, :], ALU.mult).then_inc(filled, 1)
            dve.wait_ge(filled, 1)
            nc.vector.tensor_reduce(sums[:, :], vectors[:, 0, :].rearrange("p (a d) -> p a d", a=2), AX.X,
                                    ALU.add).then_inc(filled, 1)
            dve.wait_ge(raised, 1)
            nc.vector.scalar_tensor_tensor(c.lam, sums[:, 0:1], LAMBDA_START, sums[:, 1:2], ALU.add,
                                           ALU.subtract).then_inc(filled, 1)
            dve.wait_ge(filled, 3)

        @block.scalar
        def _(act):
            act.wait_ge(filled, 2)
            nc.scalar.activation(sums[:, :], sums[:, :], ACT.Exp).then_inc(raised, 1)
    return c


def build(nc, ins, outs):
    with ExitStack() as ctx:
        const = load_constants(nc, ctx, ins)
        qk_turned = nc.dram_tensor("qk_turned", (4, 4, P, T, P), F32, kind="Internal").ap()
        new_rows = {KD: outs["new_dk"], VD: outs["new_dv"], KS: outs["new_sk"], VS: outs["new_sv"]}
        project_inputs(nc, const, ins["x_all"], ins["g_mix"], ins["w_in"], ins["rope"], new_rows, qk_turned)
        heads = nc.dram_tensor("sample_heads", (P, D), F32, kind="Internal").ap()
        attend_samples(nc, const, ins, qk_turned, new_rows, heads)
        summed = nc.dram_tensor("summed", (T, P, D), F32, kind="Internal").ap()
        attend_and_sum_experts(nc, const, ins, qk_turned, new_rows, heads, summed)
        finish(nc, const, ins, summed, outs["y"])


def kernel(**inputs):
    import numpy as _np
    import concourse.bacc as _bacc
    from concourse import mybir as _mybir
    from concourse.bass_utils import run_bass_kernel_spmd as _run

    def rows(*names):
        return _np.concatenate([_np.asarray(inputs[n]).reshape(-1, inputs[n].shape[-1]) for n in names])

    arrays = {
        "x_all": rows("x_prompt", "x_sample"),
        "p_all": rows("p_prompt", "p_sample"),
        "lambdas": _np.concatenate([_np.asarray(inputs[n]) for n in
                                    ("lambda_q1", "lambda_q2", "lambda_k1", "lambda_k2")]),
        **shape_constants(),
    }
    for n in ("cache_diff_k", "cache_diff_v", "cache_sb_k", "cache_sb_v"):
        arrays[n] = _np.asarray(inputs[n]).reshape(8, 256, W)
    for n in ("w_in", "w_out", "w_query", "w_pgate", "w_ple", "sub_keys", "expert_u", "expert_v"):
        arrays[n] = _np.asarray(inputs[n])[0]
    for n in ("g_mix", "g_subln", "g_ffn", "g_ple", "g_final"):
        arrays[n] = _np.asarray(inputs[n]).reshape(1, -1)
    arrays = {f"{n}_in": _np.ascontiguousarray(a) for n, a in arrays.items()}

    nc = _bacc.Bacc("TRN2", target_bir_lowering=False, num_devices=1)
    ins = {n[:-3]: nc.dram_tensor(n, a.shape, _mybir.dt.from_np(a.dtype), kind="ExternalInput").ap()
           for n, a in arrays.items()}
    outs = {n: nc.dram_tensor(n, (T * P, D if n == "y" else W), _mybir.dt.float32, kind="ExternalOutput").ap()
            for n in ("y", "new_dk", "new_dv", "new_sk", "new_sv")}
    build(nc, ins, outs)
    r = _run(nc, [arrays], core_ids=[0]).results[0]
    prompt = TP * P
    got = [r["y"][:prompt].reshape(1, prompt, D), r["y"][prompt:].reshape(8, 16, D)]
    for rows_of, shape in ((slice(0, prompt), (1, 1, prompt, 8, 64)), (slice(prompt, None), (1, 8, 16, 8, 64))):
        got += [r[n][rows_of].reshape(shape) for n in ("new_dk", "new_dv", "new_sk", "new_sv")]
    return tuple(got)
```
